# Optimizing a Trainium2 kernel written in Bass

```python
import jax, jax.numpy as jnp
from jax import lax
import numpy as np

D_MODEL = 1024
BATCH = 1
SEQ = 256
DEPTH = 2

MIX_WIDTH = D_MODEL
POOL_WIDTH = MIX_WIDTH // 2
POOL_WINDOWS = (2, 4, 8, 16)
N_POOL_GROUPS = len(POOL_WINDOWS)
POOL_GROUP = POOL_WIDTH // N_POOL_GROUPS
ATTN_WIDTH = MIX_WIDTH - POOL_WIDTH
HEAD_DIM = 64
N_HEADS = ATTN_WIDTH // HEAD_DIM
N_KV_HEADS = 2
GQA_GROUP = N_HEADS // N_KV_HEADS
WINDOW = 128
BLOCK = 128
Q_OFF = POOL_WIDTH
K_OFF = Q_OFF + N_HEADS * HEAD_DIM
V_OFF = K_OFF + N_KV_HEADS * HEAD_DIM
IN_WIDTH = V_OFF + N_KV_HEADS * HEAD_DIM

N_KEYS = 128
N_EXPERTS = N_KEYS * N_KEYS
PEER_HEADS = 8
PEER_TOPK = 16
D_KEY = 256
D_HALF = D_KEY // 2
PEER_CHUNK = 128

RMS_EPS = 1e-6
N_MOD = 6


def rms_norm(x, g):
    xf = x.astype(jnp.float32)
    y = xf * lax.rsqrt(jnp.mean(xf * xf, axis=-1, keepdims=True) + RMS_EPS)
    return (y * g.astype(jnp.float32)).astype(x.dtype)

def alibi_slopes(n_heads):
    return jnp.exp2(-8.0 * jnp.arange(1, n_heads + 1, dtype=jnp.float32) / n_heads)

def multiscale_pool(p, pool_w, pool_scale):
    B, S, _ = p.shape
    pg = p.reshape(B, S, N_POOL_GROUPS, POOL_GROUP)
    cs = jnp.cumsum(pg.astype(jnp.float32), axis=1)
    pos1 = jnp.arange(1, S + 1, dtype=jnp.float32)
    means = []
    for g, w in enumerate(POOL_WINDOWS):
        cg = cs[:, :, g]
        lag = jnp.pad(cg, ((0, 0), (w, 0), (0, 0)))[:, :S]
        means.append((cg - lag) / jnp.minimum(pos1, float(w))[None, :, None])
    pooled = jnp.stack(means, axis=2).astype(p.dtype) - pg
    mixed = jnp.einsum('bsgc,gcd->bsgd', pooled, pool_w)
    return mixed.reshape(B, S, POOL_WIDTH) * pool_scale

def band_blocks(t, nb):
    B = t.shape[0]
    tb = t.reshape(B, nb, BLOCK, N_KV_HEADS, HEAD_DIM)
    prev = jnp.pad(tb, ((0, 0), (1, 0), (0, 0), (0, 0), (0, 0)))[:, :nb]
    return jnp.concatenate([prev, tb], axis=2)

def sliding_window_attention(q, k, v, sinks):
    B, S = q.shape[:2]
    nb = S // BLOCK
    qb = q.reshape(B, nb, BLOCK, N_KV_HEADS, GQA_GROUP, HEAD_DIM)
    kb = band_blocks(k, nb)
    vb = band_blocks(v, nb)
    scores = jnp.einsum('bnqkgd,bnskd->bnkgqs', qb, kb,
                        preferred_element_type=jnp.float32) * (HEAD_DIM ** -0.5)
    qi = jnp.arange(BLOCK)[:, None]
    sj = jnp.arange(2 * BLOCK)[None, :]
    dist = qi + BLOCK - sj
    band_ok = (dist >= 0) & (dist < WINDOW)
    blk = jnp.arange(nb)[:, None, None]
    valid = band_ok[None] & ((blk > 0) | (sj[None] >= BLOCK))
    slopes = alibi_slopes(N_HEADS).reshape(N_KV_HEADS, GQA_GROUP)
    bias = -slopes[:, :, None, None] * dist.astype(jnp.float32)
    scores = jnp.where(valid[None, :, None, None], scores + bias[None, None], -jnp.inf)
    sink = sinks.astype(jnp.float32).reshape(N_KV_HEADS, GQA_GROUP)[None, None, :, :, None, None]
    sink = jnp.broadcast_to(sink, scores.shape[:-1] + (1,))
    probs = jax.nn.softmax(jnp.concatenate([scores, sink], axis=-1), axis=-1)[..., :-1]
    out = jnp.einsum('bnkgqs,bnskd->bnqkgd', probs.astype(v.dtype), vb)
    return out.reshape(B, S, N_HEADS * HEAD_DIM)

def peer_ffn(h, wq, subkeys, u, v):
    B, S, D = h.shape
    T = B * S
    hf = h.reshape(T, D)
    q = (hf @ wq).reshape(T, PEER_HEADS, 2, D_HALF)
    s = jnp.einsum('thpd,pnd->thpn', q, subkeys, preferred_element_type=jnp.float32)
    top_s, top_i = lax.top_k(s, PEER_TOPK)
    cand = top_s[:, :, 0, :, None] + top_s[:, :, 1, None, :]
    best_s, best_j = lax.top_k(cand.reshape(T, PEER_HEADS, PEER_TOPK * PEER_TOPK), PEER_TOPK)
    i1 = jnp.take_along_axis(top_i[:, :, 0], best_j // PEER_TOPK, axis=-1)
    i2 = jnp.take_along_axis(top_i[:, :, 1], best_j % PEER_TOPK, axis=-1)
    expert = (i1 * N_KEYS + i2).reshape(T, PEER_HEADS * PEER_TOPK)
    gate = jax.nn.softmax(best_s, axis=-1).reshape(T, PEER_HEADS * PEER_TOPK).astype(h.dtype)
    nc = T // PEER_CHUNK

    def expert_block(args):
        hc, ec, gc = args
        uc = jnp.take(u, ec, axis=0)
        a = jnp.einsum('cd,ced->ce', hc, uc)
        act = jax.nn.gelu(a, approximate=False) * gc
        vc = jnp.take(v, ec, axis=0)
        return jnp.einsum('ce,ced->cd', act, vc)

    out = lax.map(expert_block, (hf.reshape(nc, PEER_CHUNK, D),
                                 expert.reshape(nc, PEER_CHUNK, -1),
                                 gate.reshape(nc, PEER_CHUNK, -1)))
    return out.reshape(B, S, D)

def first_inputs(seed: int = 0) -> dict:
    key = jax.random.key(seed)
    ks = jax.random.split(key, 20)
    f32 = jnp.float32
    nrm = lambda k, shape, s: jax.random.normal(k, shape, f32) * s
    return {
        "x": nrm(ks[0], (BATCH, SEQ, D_MODEL), 1.0),
        "c": nrm(ks[1], (BATCH, D_MODEL), 1.0),
        "w_ada": nrm(ks[2], (DEPTH, D_MODEL, N_MOD * D_MODEL), 0.5 * D_MODEL ** -0.5),
        "b_ada": nrm(ks[3], (DEPTH, N_MOD * D_MODEL), 0.02),
        "norm1_g": 1.0 + nrm(ks[4], (DEPTH, D_MODEL), 0.05),
        "norm2_g": 1.0 + nrm(ks[5], (DEPTH, D_MODEL), 0.05),
        "w_in": nrm(ks[6], (DEPTH, D_MODEL, IN_WIDTH), D_MODEL ** -0.5),
        "pool_w": nrm(ks[7], (DEPTH, N_POOL_GROUPS, POOL_GROUP, POOL_GROUP), POOL_GROUP ** -0.5),
        "pool_scale": 1.0 + nrm(ks[8], (DEPTH, POOL_WIDTH), 0.1),
        "q_norm_g": 1.0 + nrm(ks[9], (DEPTH, HEAD_DIM), 0.05),
        "k_norm_g": 1.0 + nrm(ks[10], (DEPTH, HEAD_DIM), 0.05),
        "attn_sinks": nrm(ks[11], (DEPTH, N_HEADS), 0.5),
        "mix_norm_g": 1.0 + nrm(ks[12], (DEPTH, MIX_WIDTH), 0.05),
        "w_out": nrm(ks[13], (DEPTH, MIX_WIDTH, D_MODEL), MIX_WIDTH ** -0.5),
        "peer_wq": nrm(ks[14], (DEPTH, D_MODEL, PEER_HEADS * D_KEY), D_MODEL ** -0.5),
        "peer_subkeys": nrm(ks[15], (DEPTH, 2, N_KEYS, D_HALF), D_HALF ** -0.5),
        "peer_u": nrm(ks[16], (DEPTH, N_EXPERTS, D_MODEL), D_MODEL ** -0.5),
        "peer_v": nrm(ks[17], (DEPTH, N_EXPERTS, D_MODEL), PEER_HEADS ** -0.5),
    }

def first_block(x, c, w_ada, b_ada, norm1_g, norm2_g, w_in, pool_w, pool_scale, q_norm_g,
              k_norm_g, attn_sinks, mix_norm_g, w_out, peer_wq, peer_subkeys, peer_u, peer_v):
    B, S, D = x.shape
    cond = jax.nn.silu(c)
    for l in range(DEPTH):
        mod = (cond @ w_ada[l] + b_ada[l])[:, None, :]
        sh1, sc1, g1, sh2, sc2, g2 = jnp.split(mod, N_MOD, axis=-1)

        h = rms_norm(x, norm1_g[l]) * (1.0 + sc1) + sh1
        proj = h @ w_in[l]
        p = proj[..., :Q_OFF]
        q = proj[..., Q_OFF:K_OFF].reshape(B, S, N_HEADS, HEAD_DIM)
        k = proj[..., K_OFF:V_OFF].reshape(B, S, N_KV_HEADS, HEAD_DIM)
        v = proj[..., V_OFF:].reshape(B, S, N_KV_HEADS, HEAD_DIM)
        q = rms_norm(q, q_norm_g[l])
        k = rms_norm(k, k_norm_g[l])
        pool_out = multiscale_pool(p, pool_w[l], pool_scale[l])
        attn_out = sliding_window_attention(q, k, v, attn_sinks[l])
        y = jnp.concatenate([pool_out, attn_out], axis=-1).reshape(B, S, 2, MIX_WIDTH // 2)
        y = rms_norm(y, jnp.ones((MIX_WIDTH // 2,), jnp.float32)).reshape(B, S, MIX_WIDTH) * mix_norm_g[l]
        x = x + g1 * (y @ w_out[l])

        h2 = rms_norm(x, norm2_g[l]) * (1.0 + sc2) + sh2
        x = x + g2 * peer_ffn(h2, peer_wq[l], peer_subkeys[l], peer_u[l], peer_v[l])
    return x


FOX_HEADS = 8
FOX_HEAD_DIM = 64
FOX_WIDTH = FOX_HEADS * FOX_HEAD_DIM
MLA_HEADS = 8
MLA_NOPE_DIM = 64
MLA_ROPE_DIM = 32
MLA_V_DIM = 64
MLA_WIDTH = MLA_HEADS * MLA_V_DIM
D_MIX = FOX_WIDTH + MLA_WIDTH
Q_LORA_RANK = 256
KV_LORA_RANK = 128
ROPE_THETA = 10000.0
IN_WIDTH_2 = 3 * FOX_WIDTH + FOX_HEADS + Q_LORA_RANK + KV_LORA_RANK + MLA_ROPE_DIM
Q_BLOCK = 128
N_GROUPS = 8
EXPERTS_PER_GROUP = 4
N_EXPERTS_2 = N_GROUPS * EXPERTS_PER_GROUP
TOP_K_IN_GROUP = 2
D_EXPERT = 256
EXPERT_BLOCK = 128
NORM_EPS = 1e-6


def rms_norm_2(x, gain):
    xf = x.astype(jnp.float32)
    y = xf * lax.rsqrt(jnp.mean(xf * xf, axis=-1, keepdims=True) + NORM_EPS)
    return (y * gain.astype(jnp.float32)).astype(x.dtype)

def rotary(x, positions):
    half = MLA_ROPE_DIM // 2
    inv_freq = ROPE_THETA ** (-jnp.arange(half, dtype=jnp.float32) / half)
    ang = positions.astype(jnp.float32)[..., None] * inv_freq
    ang = ang.reshape(ang.shape[:2] + (1,) * (x.ndim - 3) + (half,))
    cos, sin = jnp.cos(ang), jnp.sin(ang)
    xf = x.astype(jnp.float32)
    x1, x2 = xf[..., :half], xf[..., half:]
    return jnp.concatenate([x1 * cos - x2 * sin, x2 * cos + x1 * sin], axis=-1).astype(x.dtype)

def causal_block_attention(q, k, v, log_forget_cum=None):
    B, S, H, dk = q.shape
    dv = v.shape[-1]
    nb = S // Q_BLOCK
    scale = dk ** -0.5
    kf = k.astype(jnp.float32)
    vf = v.astype(jnp.float32)
    key_pos = jnp.arange(S)
    q_blocks = q.reshape(B, nb, Q_BLOCK, H, dk).transpose(1, 0, 2, 3, 4)
    has_decay = log_forget_cum is not None
    if has_decay:
        d_keys = log_forget_cum.transpose(0, 2, 1)
        d_blocks = log_forget_cum.reshape(B, nb, Q_BLOCK, H).transpose(1, 0, 3, 2)
        xs = (jnp.arange(nb), q_blocks, d_blocks)
    else:
        xs = (jnp.arange(nb), q_blocks)

    def one_block(args):
        i, q_i = args[0], args[1]
        s = jnp.einsum('bqhd,bkhd->bhqk', q_i.astype(jnp.float32), kf) * scale
        if has_decay:
            s = s + args[2][..., :, None] - d_keys[:, :, None, :]
        q_pos = i * Q_BLOCK + jnp.arange(Q_BLOCK)
        s = jnp.where(key_pos[None, :] <= q_pos[:, None], s, -jnp.inf)
        p = jax.nn.softmax(s, axis=-1)
        return jnp.einsum('bhqk,bkhd->bqhd', p, vf)

    out = lax.map(one_block, xs)
    return out.transpose(1, 0, 2, 3, 4).reshape(B, S, H, dv).astype(v.dtype)

def hybrid_mixer(xn, positions, w_in, b_f, q_norm, w_uq, kv_norm, w_ukv, fox_out_norm, mla_out_norm, w_o):
    B, S, _ = xn.shape
    proj = xn @ w_in
    offs = [FOX_WIDTH, 2 * FOX_WIDTH, 3 * FOX_WIDTH, 3 * FOX_WIDTH + FOX_HEADS,
            3 * FOX_WIDTH + FOX_HEADS + Q_LORA_RANK,
            3 * FOX_WIDTH + FOX_HEADS + Q_LORA_RANK + KV_LORA_RANK]
    fq, fk, fv, f_logit, c_q, c_kv, k_rope = jnp.split(proj, offs, axis=-1)

    log_f = jax.nn.log_sigmoid(f_logit.astype(jnp.float32) + b_f.astype(jnp.float32))
    log_f_cum = jnp.cumsum(log_f, axis=1)
    fox = causal_block_attention(fq.reshape(B, S, FOX_HEADS, FOX_HEAD_DIM),
                                 fk.reshape(B, S, FOX_HEADS, FOX_HEAD_DIM),
                                 fv.reshape(B, S, FOX_HEADS, FOX_HEAD_DIM), log_f_cum)
    fox = rms_norm_2(fox, fox_out_norm.reshape(FOX_HEADS, FOX_HEAD_DIM)).reshape(B, S, FOX_WIDTH)

    q = (rms_norm_2(c_q, q_norm) @ w_uq).reshape(B, S, MLA_HEADS, MLA_NOPE_DIM + MLA_ROPE_DIM)
    q = jnp.concatenate([q[..., :MLA_NOPE_DIM], rotary(q[..., MLA_NOPE_DIM:], positions)], axis=-1)
    kv = (rms_norm_2(c_kv, kv_norm) @ w_ukv).reshape(B, S, MLA_HEADS, MLA_NOPE_DIM + MLA_V_DIM)
    k_nope, v = kv[..., :MLA_NOPE_DIM], kv[..., MLA_NOPE_DIM:]
    k_pe = rotary(k_rope, positions)
    k = jnp.concatenate([k_nope, jnp.broadcast_to(k_pe[:, :, None, :], (B, S, MLA_HEADS, MLA_ROPE_DIM))], axis=-1)
    mla = causal_block_attention(q, k, v)
    mla = rms_norm_2(mla, mla_out_norm.reshape(MLA_HEADS, MLA_V_DIM)).reshape(B, S, MLA_WIDTH)

    return jnp.concatenate([fox, mla], axis=-1) @ w_o

def hierarchical_moe(xn, w_group, w_router, w_gate, w_up, w_down):
    B, S, D = xn.shape
    T = B * S
    xt = xn.reshape(T, D)
    group_p = jax.nn.softmax((xt @ w_group).astype(jnp.float32), axis=-1)
    group_w, group_id = lax.top_k(group_p, 1)
    expert_logits = (xt @ w_router).astype(jnp.float32).reshape(T, N_GROUPS, EXPERTS_PER_GROUP)
    in_group = jnp.take_along_axis(expert_logits, group_id[:, :, None], axis=1)[:, 0]
    top_logits, local_id = lax.top_k(in_group, TOP_K_IN_GROUP)
    gates = group_w * jax.nn.softmax(top_logits, axis=-1)
    expert_id = group_id * EXPERTS_PER_GROUP + local_id

    A = T * TOP_K_IN_GROUP
    e_flat = expert_id.reshape(A)
    tok_flat = jnp.repeat(jnp.arange(T), TOP_K_IN_GROUP)
    g_flat = gates.reshape(A)
    order = jnp.argsort(e_flat)
    e_sorted, tok_sorted, g_sorted = e_flat[order], tok_flat[order], g_flat[order]
    counts = jnp.bincount(e_flat, length=N_EXPERTS_2)
    padded = (counts + EXPERT_BLOCK - 1) // EXPERT_BLOCK * EXPERT_BLOCK
    start = jnp.cumsum(counts) - counts
    pend = jnp.cumsum(padded)
    pstart = pend - padded
    dest = pstart[e_sorted] + (jnp.arange(A) - start[e_sorted])
    n_blocks = (A + N_EXPERTS_2 * (EXPERT_BLOCK - 1) + EXPERT_BLOCK - 1) // EXPERT_BLOCK
    buf = jnp.zeros((n_blocks * EXPERT_BLOCK, D), xn.dtype).at[dest].set(xt[tok_sorted])
    block_expert = jnp.clip(jnp.searchsorted(pend, jnp.arange(n_blocks) * EXPERT_BLOCK, side='right'), 0, N_EXPERTS_2 - 1)

    def expert_block(args):
        xb, e = args
        h = jax.nn.silu(xb @ w_gate[e]) * (xb @ w_up[e])
        return h @ w_down[e]

    ybuf = lax.map(expert_block, (buf.reshape(n_blocks, EXPERT_BLOCK, D), block_expert)).reshape(-1, D)
    contrib = ybuf[dest].astype(jnp.float32) * g_sorted[:, None]
    y = jax.ops.segment_sum(contrib, tok_sorted, num_segments=T)
    return y.reshape(B, S, D).astype(xn.dtype)

def second_inputs(seed: int = 0) -> dict:
    key = jax.random.key(seed)
    ks = jax.random.split(key, 20)
    f32 = jnp.float32

    def dense(k, shape, fan_in):
        return jax.random.normal(k, shape, f32) * (fan_in ** -0.5)

    def gain(k, shape):
        return 1.0 + 0.02 * jax.random.normal(k, shape, f32)

    return {
        'x': jax.random.normal(ks[0], (BATCH, SEQ, D_MODEL), f32),
        'positions': jnp.broadcast_to(jnp.arange(SEQ, dtype=jnp.int32), (BATCH, SEQ)),
        'attn_norm': gain(ks[1], (DEPTH, D_MODEL)),
        'w_in': dense(ks[2], (DEPTH, D_MODEL, IN_WIDTH_2), D_MODEL),
        'b_f': jax.random.uniform(ks[3], (DEPTH, FOX_HEADS), f32, 1.0, 4.0),
        'q_norm': gain(ks[4], (DEPTH, Q_LORA_RANK)),
        'w_uq': dense(ks[5], (DEPTH, Q_LORA_RANK, MLA_HEADS * (MLA_NOPE_DIM + MLA_ROPE_DIM)), Q_LORA_RANK),
        'kv_norm': gain(ks[6], (DEPTH, KV_LORA_RANK)),
        'w_ukv': dense(ks[7], (DEPTH, KV_LORA_RANK, MLA_HEADS * (MLA_NOPE_DIM + MLA_V_DIM)), KV_LORA_RANK),
        'fox_out_norm': gain(ks[8], (DEPTH, FOX_WIDTH)),
        'mla_out_norm': gain(ks[9], (DEPTH, MLA_WIDTH)),
        'w_o': dense(ks[10], (DEPTH, D_MIX, D_MODEL), D_MIX),
        'ffn_norm': gain(ks[11], (DEPTH, D_MODEL)),
        'w_group': dense(ks[12], (DEPTH, D_MODEL, N_GROUPS), D_MODEL),
        'w_router': dense(ks[13], (DEPTH, D_MODEL, N_EXPERTS_2), D_MODEL),
        'w_gate': dense(ks[14], (DEPTH, N_EXPERTS_2, D_MODEL, D_EXPERT), D_MODEL),
        'w_up': dense(ks[15], (DEPTH, N_EXPERTS_2, D_MODEL, D_EXPERT), D_MODEL),
        'w_down': dense(ks[16], (DEPTH, N_EXPERTS_2, D_EXPERT, D_MODEL), D_EXPERT),
        'final_norm': gain(ks[17], (D_MODEL,)),
    }

def second_block(x, positions, attn_norm, w_in, b_f, q_norm, w_uq, kv_norm, w_ukv, fox_out_norm, mla_out_norm, w_o,
              ffn_norm, w_group, w_router, w_gate, w_up, w_down, final_norm):
    h = x
    for l in range(DEPTH):
        h = h + hybrid_mixer(rms_norm_2(h, attn_norm[l]), positions, w_in[l], b_f[l], q_norm[l], w_uq[l],
                             kv_norm[l], w_ukv[l], fox_out_norm[l], mla_out_norm[l], w_o[l])
        h = h + hierarchical_moe(rms_norm_2(h, ffn_norm[l]), w_group[l], w_router[l], w_gate[l], w_up[l], w_down[l])
    return rms_norm_2(h, final_norm)


def setup_inputs(seed=0):
    out = dict(first_inputs(seed))
    for name, value in second_inputs(seed + 1).items():
        if name != "x":
            out[name + "_2"] = value
    return out


def reference(
    x, c, w_ada, b_ada, norm1_g, norm2_g, w_in, pool_w, pool_scale, q_norm_g, k_norm_g,
    attn_sinks, mix_norm_g, w_out, peer_wq, peer_subkeys, peer_u, peer_v, positions_2,
    attn_norm_2, w_in_2, b_f_2, q_norm_2, w_uq_2, kv_norm_2, w_ukv_2, fox_out_norm_2,
    mla_out_norm_2, w_o_2, ffn_norm_2, w_group_2, w_router_2, w_gate_2, w_up_2, w_down_2,
    final_norm_2,
):
    x = first_block(
        x, c, w_ada, b_ada, norm1_g, norm2_g, w_in, pool_w, pool_scale, q_norm_g, k_norm_g,
        attn_sinks, mix_norm_g, w_out, peer_wq, peer_subkeys, peer_u, peer_v,
    )
    return second_block(
        x, positions_2, attn_norm_2, w_in_2, b_f_2, q_norm_2, w_uq_2, kv_norm_2, w_ukv_2,
        fox_out_norm_2, mla_out_norm_2, w_o_2, ffn_norm_2, w_group_2, w_router_2, w_gate_2,
        w_up_2, w_down_2, final_norm_2,
    )


_drawn_inputs = setup_inputs


def setup_inputs(seed=0):
    import zlib

    import numpy as np

    out = dict(_drawn_inputs(seed))
    spreads = {}
    factors = {'q_norm_g': 3.276,
     'k_norm_g': 3.165,
     'q_norm_2': 5.29,
     'fox_out_norm_2': 2.86,
     'ffn_norm_2': 2.965,
     'final_norm_2': 2.823}
    for name, (base, spread) in spreads.items():
        noise = np.random.default_rng([zlib.crc32(name.encode()), seed]).standard_normal(out[name].shape)
        drawn = base * np.exp(spread * noise) if base else spread * noise
        out[name] = __import__('jax').numpy.asarray(drawn.astype(out[name].dtype))
    for name, factor in factors.items():
        out[name] = (out[name] * factor).astype(out[name].dtype)
    return out
```

```python
from contextlib import ExitStack
from math import pi

import concourse.bass as bass
from concourse import mybir

F32 = mybir.dt.float32
BF16 = mybir.dt.bfloat16
I32 = mybir.dt.int32
U32 = mybir.dt.uint32
ALU = mybir.AluOpType
ACT = mybir.ActivationFunctionType
AX = mybir.AxisListType.X

P = 128
D = 1024
KT = D // P
T = 256
TT = T // P
DEPTH = 2
EPS = 1e-6
MASKED = -1e30
LOWEST = -3.0e38

POOL = 512
WINDOWS = (2, 4, 8, 16)
HD = 64
NH = 8
NKV = 2
IN_A = 1280
NKEY = 128
NEXP = NKEY * NKEY
PH = 8
TOPK = 16
SLOTS = PH * TOPK
IN_B = 1960
REST = IN_B - 3 * 512
QL, KVL, ROPE = 256, 128, 32
DK = HD + ROPE
NG, EPG = 8, 4
NE = NG * EPG
DE = 256

CHUNK = 4096
NCHUNK = 4
RING = 4
EXP_F = 3 * KT * DE
EXP_RING = 4
NBANK = 6


def psum_jobs():
    jobs, order, count = {}, [], {"v": 0, "s": 0}

    def add(name, who):
        jobs[name] = (len(order), len(order) % NBANK, who, count[who])
        order.append(name)
        count[who] += 1

    for l in range(DEPTH):
        for n in range(12):
            add(("ada", l, n), "v" if n // 2 in (1, 4) else "s")
    for l in range(DEPTH):
        for tt in range(TT):
            for half in range(2):
                add(("hT", l, tt, half), "s")
        for c in range(3):
            for tt in range(TT):
                add(("in", l, c, tt), "s")
        for b in range(2):
            add(("pool", l, b), "s")
        for tt in range(TT):
            add(("mix", l, tt), "v")
        for tt in range(TT):
            add(("qT", l, tt), "s")
        add(("kT", l), "s")
        attention_jobs(add, "a", l)
        for tt in range(TT):
            for half in range(2):
                add(("yT", l, tt, half), "s")
        for c in range(2):
            for tt in range(TT):
                add(("out", l, c, tt), "v")
        add(("subT", l), "s")
        for tt in range(TT):
            for half in range(2):
                add(("h2T", l, tt, half), "s")
        for b in range(8):
            add(("wq", l, b), "s")
        for tt in range(TT):
            for b in range(4):
                add(("s", l, tt, b), "s")
    for l in range(DEPTH):
        for tt in range(TT):
            for half in range(2):
                add(("bhT", l, tt, half), "s")
        for b in range(4):
            add(("fqk", l, b), "s")
        for tt in range(TT):
            add(("fv", l, tt), "s")
        for tt in range(TT):
            add(("rest", l, tt), "v")
        for tt in range(TT):
            add(("cT", l, tt), "s")
        for tt in range(TT):
            for c in range(2):
                add(("uq", l, tt, c), "s")
            for c in range(2):
                add(("ukv", l, tt, c), "s")
        attention_jobs(add, "f", l)
        for name in ("qmT", "kmT"):
            for tt in range(TT):
                for b in range(2):
                    add((name, l, tt, b), "s")
        attention_jobs(add, "m", l)
        for tt in range(TT):
            for half in range(2):
                add(("byT", l, tt, half), "s")
        for c in range(2):
            for tt in range(TT):
                add(("bout", l, c, tt), "v")
        for tt in range(TT):
            for half in range(2):
                add(("fhT", l, tt, half), "s")
        for tt in range(TT):
            add(("route", l, tt), "v")
    return jobs, order


def attention_jobs(add, kind, l):
    for tt in range(TT):
        for b in range(2 * (tt + 1)):
            add((kind + "sc", l, tt, b), "v")
    for tt in range(TT):
        for b in range(2 * (tt + 1)):
            add((kind + "pT", l, tt, b), "s")
        add((kind + "pv", l, tt), "v")


def first_head(b, per):
    return b // 2 * 2 * per + b % 2


def weight_chunks():
    chunks, order, count = {}, [], {"v": 0, "p": 0}

    def add(name, who):
        chunks[name] = (len(order), len(order) % NCHUNK, who, count[who])
        order.append(name)
        count[who] += 1

    for l in range(DEPTH):
        for c in range(3):
            for kp in range(4):
                add(("ada", l, c, kp), "v")
    for l in range(DEPTH):
        for name, n in (("in", 3), ("out", 2), ("wq", 4)):
            for c in range(n):
                add((name, l, c), "p")
    for l in range(DEPTH):
        for name, n in (("bin", 4), ("bout", 2)):
            for c in range(n):
                add((name, l, c), "p")
    return chunks, order


def build(
    nc, x, c, w_ada, b_ada, norm1_g, norm2_g, w_in, pool_w, pool_scale, q_norm_g, k_norm_g,
    attn_sinks, mix_norm_g, w_out, peer_wq, peer_subkeys, peer_u, peer_v, positions_2,
    attn_norm_2, w_in_2, b_f_2, q_norm_2, w_uq_2, kv_norm_2, w_ukv_2, fox_out_norm_2,
    mla_out_norm_2, w_o_2, ffn_norm_2, w_group_2, w_router_2, w_gate_2, w_up_2, w_down_2,
    final_norm_2, out,
):
    J, JORDER = psum_jobs()
    CH, CORDER = weight_chunks()

    with ExitStack() as ctx:
        def sb(name, n, dt=F32):
            return ctx.enter_context(nc.sbuf_tensor(name, [P, n], dt))

        def sem(name):
            return ctx.enter_context(nc.semaphore(name))

        arena = sb("arena", NCHUNK * CHUNK + 12288)
        mod = sb("mod", 12288)
        small = sb("small", 4224)
        X = sb("X", TT * D)[:].rearrange("p (t d) -> p t d", t=TT)
        HR = sb("HR", TT * D)[:].rearrange("p (t d) -> p t d", t=TT)
        HT = sb("HT", KT * T)[:].rearrange("p (k t) -> p k t", k=KT)
        JKT = sb("JK", 512)
        JUNK = JKT[:].bitcast(BF16)
        TMP = JKT[:]
        IDENT = sb("IDENT", P)[:]
        ONES = sb("ONES", P)[:]
        IDX = sb("IDX", TT * SLOTS, I32)[:].rearrange("p (t s) -> p t s", t=TT)
        GATE = sb("GATE", TT * SLOTS)[:].rearrange("p (t s) -> p t s", t=TT)
        SSQ = sb("SSQ", 32)[:]
        RT = sb("RT", 32)[:]
        RS = sb("RS", 32)[:]
        SV = sb("SV", 6 * 16)[:].rearrange("p (a t h) -> p a t h", a=6, t=TT)
        MX, NM, DEN, RD, SE, EXS = (SV[:, i] for i in range(6))
        SINK = sb("SINK", NH)[:]
        COND = sb("COND", KT)[:]
        EPST = sb("EPST", 1)[:]
        IOTA = sb("IOTA", TOPK)[:]
        COS = sb("COS", TT * 16)[:].rearrange("p (t f) -> p t f", t=TT)
        SIN = sb("SIN", TT * 16)[:].rearrange("p (t f) -> p t f", t=TT)
        STAGE = sb("STAGE", RING, I32)[:]
        DOT = sb("DOT", RING)[:]
        ACTV = sb("ACTV", RING)[:]
        EG = sb("EG", TT * NE)[:].rearrange("p (t e) -> p t e", t=TT)
        RW = sb("RW", 64)[:]

        def view(buf, at, pattern, **kw):
            n = 1
            for v in kw.pop("shape"):
                n *= v
            return buf[:, at:at + n].rearrange(pattern, **kw)

        G0 = NCHUNK * CHUNK
        ring = [arena[:, s * CHUNK:(s + 1) * CHUNK] for s in range(NCHUNK)]

        def g3(at, a, b, buf=arena, base=G0):
            return buf[:, base + at:base + at + a * b].rearrange("p (a b) -> p a b", a=a)

        NGAIN = g3(0, 4, D)
        PROJ = g3(0, TT, IN_A)
        KD = arena[:, G0 + 2560:G0 + 3072].rearrange("p (t k u d) -> p t k u d", t=TT, k=NKV, u=2)
        QT = g3(3072, 4, T)
        KTA = g3(4096, NKV, T)
        S_A = [g3(4608, NH, P), g3(5632, NH, T)]
        PT_A = arena[:, G0 + 7680:G0 + 9728].rearrange("p (k h q) -> p k h q", k=2, h=NH)
        POOLT = g3(7680, 4, T)
        QSQ = arena[:, G0 + 5632:G0 + 6912]
        MIXG = arena[:, G0 + 10240:G0 + 11264]
        PSC = arena[:, G0 + 11264:G0 + 11776]
        SUBK = g3(11776, 2, NKEY)
        SUBT = g3(12032, 2, NKEY)
        QTP = g3(0, 16, T)
        SS = arena[:, G0 + 4096:G0 + 8192].rearrange("p (t a n) -> p t a n", t=TT, a=16)
        CAND = g3(8192, PH, 256)
        OH = arena[:, G0:G0 + 2048].rearrange("p (h k c) -> p h k c", h=PH, k=TOPK)
        V16 = g3(10240, 16, TOPK)
        I16 = g3(10496, 16, TOPK).bitcast(U32)
        F16 = g3(10752, 16, TOPK)
        BV = g3(11008, PH, TOPK)
        BI = g3(11136, PH, TOPK).bitcast(U32)
        BU = g3(11264, PH, TOPK).bitcast(U32)
        BF = g3(11392, PH, TOPK)
        E1 = g3(11520, PH, TOPK)
        E2 = g3(11648, PH, TOPK)
        GU = g3(0, RING, D)
        GV = g3(4096, RING, D)
        DIAG = g3(8192, RING, P)
        MODL = [mod[:, l * 6144:(l + 1) * 6144] for l in range(DEPTH)]

        def mrow(l, i):
            return MODL[l][:, i * D:(i + 1) * D]

        BIAS = small[:, 0:2048].rearrange("p (h s) -> p h s", h=NH)
        MT = small[:, 2048:3584].rearrange("p (g t) -> p g t", g=4)
        POOLW = small[:, 3584:4096].rearrange("p (g d) -> p g d", g=4)
        QKG = small[:, 4096:4224]
        UQ = small[:, 0:1536].rearrange("p (k n) -> p k n", k=2)
        UKV = small[:, 1536:2560]
        FN = small[:, 2560:3584]
        ON = mod[:, 0:1024]
        FINAL = mod[:, 1024:2048]
        QG = mod[:, 2048:2304]
        KG = mod[:, 2304:2432]
        BFB = mod[:, 2432:2440]
        GR = mod[:, 2440:2760].rearrange("p (k n) -> p k n", k=KT)
        FQT = g3(2760, 4, T, mod, 0)
        FKT = g3(3784, 4, T, mod, 0)
        FV = g3(4808, TT, 512, mod, 0)
        R = g3(5832, TT, REST, mod, 0)
        CT = g3(6680, 3, T, mod, 0)
        QM = mod[:, 7448:8984].rearrange("p (t h d) -> p t h d", t=TT, h=NH)
        KM = mod[:, 8984:10520].rearrange("p (t h d) -> p t h d", t=TT, h=NH)
        UTRI = g3(10520, TT, T, mod, 0)
        CMASK = mod[:, 11032:11288]
        RTMP = mod[:, 11288:12288]
        SG = g3(7448, 2, 512, mod, 0)
        HH = mod[:, 8472:9496].rearrange("p (b j t) -> p b j t", b=2, j=2)
        KV = arena[:, G0:G0 + 2048].rearrange("p (t h d) -> p t h d", t=TT, h=NH)
        QMT = g3(2048, NH, T)
        LFB = arena[:, G0 + 2048:G0 + 4096].rearrange("p (t h q) -> p t h q", t=TT, h=NH)
        KMT = g3(4096, NH, T)
        S_B = [g3(6144, NH, P), g3(7168, NH, T)]
        PT_B = arena[:, G0 + 9216:G0 + 11264].rearrange("p (k h q) -> p k h q", k=2, h=NH)
        SQB = arena[:, G0 + 7168:G0 + 9216]
        AN = arena[:, G0 + 11264:G0 + 12288]
        WG = [arena[:, s * EXP_F:s * EXP_F + 2048].rearrange("p (k f) -> p k f", k=KT) for s in range(EXP_RING)]
        WU = [arena[:, s * EXP_F + 2048:s * EXP_F + 4096].rearrange("p (k f) -> p k f", k=KT) for s in range(EXP_RING)]
        WD = [arena[:, s * EXP_F + 4096:s * EXP_F + 6144].rearrange("p (j d) -> p j d", j=2) for s in range(EXP_RING)]

        PS = ctx.enter_context(nc.psum_tensor("PS", [P, 8, 512], F32))
        PO = PS[:, NBANK:NBANK + 2, :]

        psum_ready = sem("psum_ready")
        evac = {"v": sem("evac_by_vector"), "s": sem("evac_by_scalar")}
        vector_step = sem("vector_step")
        scalar_step = sem("scalar_step")
        pool_step = sem("pool_step")
        x_loaded = sem("x_loaded")
        cond_loaded = sem("cond_loaded")
        cond_ready = sem("cond_ready")
        gains_loaded = sem("gains_loaded")
        bada_loaded = sem("bada_loaded")
        consts_ready = sem("consts_ready")
        acc_zeroed = sem("acc_zeroed")
        acc_ready = sem("acc_ready")
        params_loaded = sem("params_loaded")
        chunk_loaded = [sem(f"chunk_loaded{i}") for i in range(NCHUNK)]
        chunk_used = {"v": sem("chunk_used_by_vector"), "p": sem("chunk_used_by_tensor")}
        squares_ready = sem("squares_ready")
        root_ready = sem("root_ready")
        rows_ready = sem("rows_ready")
        qk_ready = sem("qk_ready")
        negmax_ready = sem("negmax_ready")
        probs_ready = sem("probs_ready")
        idx_ready = sem("idx_ready")
        gexp_in = sem("gexp_in")
        gexp_out = sem("gexp_out")
        staged = sem("staged")
        stage_seen = sem("stage_seen")
        u_loaded = [sem(f"u_loaded{i}") for i in range(RING)]
        v_loaded = [sem(f"v_loaded{i}") for i in range(RING)]
        dot_ready = sem("dot_ready")
        gelu_ready = sem("gelu_ready")
        diag_ready = sem("diag_ready")
        expert_added = sem("expert_added")
        sums_read = sem("sums_read")
        layer_done = sem("layer_done")
        logsig_in = sem("logsig_in")
        logsig_out = sem("logsig_out")
        decay_ready = sem("decay_ready")
        cn_ready = sem("cn_ready")
        mla_ready = sem("mla_ready")
        trig_in = sem("trig_in")
        trig_out = sem("trig_out")
        pos_loaded = sem("pos_loaded")
        expert_loaded = [sem(f"expert_loaded{i}") for i in range(EXP_RING)]
        gate_done = sem("gate_done")
        up_done = sem("up_done")
        silu_done = sem("silu_done")
        hidden_ready = sem("hidden_ready")
        down_done = sem("down_done")
        down_added = sem("down_added")
        router_in = sem("router_in")
        router_out = sem("router_out")
        out_ready = sem("out_ready")
        stored = sem("stored")

        def bank(name):
            return PS[:, J[name][1], :]

        def arrived(eng, name):
            eng.wait_ge(psum_ready, J[name][0] + 1)

        def taken(eng, name):
            eng.wait_ge(evac[J[name][2]], J[name][3] + 1)

        def loaded(eng, name):
            n, slot = CH[name][:2]
            eng.wait_ge(chunk_loaded[slot], 16 * (n // NCHUNK + 1))

        def row(ap, n):
            return ap.partition_broadcast(n)

        block = ctx.enter_context(nc.Block())

        @block.sync
        def _(sp):
            def source(name):
                kind, l, c = name[:3]
                if kind == "ada":
                    return w_ada[l, name[3] * 256:(name[3] + 1) * 256, c * 2048:(c + 1) * 2048]
                w = {"in": w_in, "out": w_out, "wq": peer_wq, "bin": w_in_2, "bout": w_o_2}[kind]
                return w[l, :, c * 512:min((c + 1) * 512, w.shape[2])]

            sp.dma_start(X, x[0].rearrange("(t p) d -> p t d", p=P)).then_inc(x_loaded, 16)
            for n, name in enumerate(CORDER):
                if n >= NCHUNK:
                    _, _, who, nth = CH[CORDER[n - NCHUNK]]
                    sp.wait_ge(chunk_used[who], nth + 1)
                if name[0] == "bin" and name[2] == 0 and name[1] > 0:
                    sp.wait_ge(down_done, 4 * NE * name[1])
                src = source(name).rearrange("(k p) n -> p k n", p=P)
                dst = ring[n % NCHUNK][:, 0:src.shape[1] * src.shape[2]].rearrange("p (k n) -> p k n", k=src.shape[1])
                sp.dma_start(dst, src).then_inc(chunk_loaded[n % NCHUNK], 16)
                if name[0] == "bout" and name[2] == 1:
                    l = name[1]
                    sp.wait_ge(chunk_used["p"], CH[name][3] + 1)
                    arrived(sp, ("fhT", l, 0, 0))
                    wg = w_gate_2.rearrange("l e (p k) f -> (l e) p (k f)", k=KT)
                    wu = w_up_2.rearrange("l e (p k) f -> (l e) p (k f)", k=KT)
                    wd = w_down_2.rearrange("l e (j p) d -> (l e) p j d", p=P)

                    def expert(e, s):
                        flat = arena[:, s * EXP_F:(s + 1) * EXP_F]
                        sp.dma_start(flat[:, 0:2048], wg[e]).then_inc(expert_loaded[s], 16)
                        sp.dma_start(flat[:, 2048:4096], wu[e]).then_inc(expert_loaded[s], 16)
                        sp.dma_start(WD[s], wd[e]).then_inc(expert_loaded[s], 16)

                    for s in range(EXP_RING):
                        expert(l * NE + s, s)
                    with sp.Fori(1, NE // EXP_RING) as i:
                        for s in range(EXP_RING):
                            sp.wait_ge(down_done, (i * EXP_RING + (l * NE + s - EXP_RING + 1)) * 4)
                            e = i * EXP_RING + (l * NE + s)
                            flat = arena[:, s * EXP_F:(s + 1) * EXP_F]
                            one = lambda w: w[bass.ds(e, 1)]
                            sp.dma_start(flat[:, 0:2048], one(wg)[0]).then_inc(expert_loaded[s], 16)
                            sp.dma_start(flat[:, 2048:4096], one(wu)[0]).then_inc(expert_loaded[s], 16)
                            sp.dma_start(WD[s], one(wd)[0]).then_inc(expert_loaded[s], 16)
            sp.wait_ge(out_ready, 2)
            sp.dma_start(out[0].rearrange("(t p) d -> p t d", p=P), HR).then_inc(stored, 16)
            sp.wait_ge(stored, 16)

        @block.gpsimd
        def _(pool):
            steps = [0]

            def go(ins):
                steps[0] += 1
                ins.then_inc(pool_step, 1)

            def sync():
                pool.wait_ge(pool_step, steps[0])

            def params(src_dst):
                for dst, src in src_dst:
                    pool.dma_start(dst, src).then_inc(params_loaded, 16)

            with nc.allow_non_contiguous_dma(reason="small parameter vectors"):
                pool.dma_start(COND, c[0].rearrange("(k p) -> p k", p=P)).then_inc(cond_loaded, 16)
                pool.dma_start(RW[:, 0:TT].bitcast(I32), positions_2[0].rearrange("(t p) -> p t", p=P)).then_inc(pos_loaded, 16)
            for l in range(DEPTH):
                pool.dma_start(NGAIN[:, 2 * l], row(norm1_g[l], P)).then_inc(gains_loaded, 16)
                pool.dma_start(NGAIN[:, 2 * l + 1], row(norm2_g[l], P)).then_inc(gains_loaded, 16)
            go(pool.memset(mod[:], 0.0))
            sync()
            for l in range(DEPTH):
                pool.dma_start(MODL[l][0:1, :], b_ada[l:l + 1, :]).then_inc(bada_loaded, 16)
            go(pool.memset(IDENT, 0.0))
            go(pool.memset(ONES, 1.0))
            go(pool.memset(EPST, EPS))
            go(pool.iota(IOTA, [[1, TOPK]], base=0, channel_multiplier=0, allow_small_or_imprecise_dtypes=True))
            go(pool.iota(BIAS, [[0, NH], [-1, 2 * P]], base=P, channel_multiplier=1, allow_small_or_imprecise_dtypes=True))
            sync()
            go(pool.affine_select(out=IDENT, in_=IDENT, compare_op=ALU.not_equal, fill=1.0, base=0,
                                  pattern=[[-1, P]], channel_multiplier=1))
            for h in range(NH):
                go(pool.tensor_scalar(BIAS[:, h], BIAS[:, h], -(2.0 ** (-8.0 * (h + 1) / NH)), None, ALU.mult))
            sync()
            go(pool.affine_select(out=BIAS, in_=BIAS, compare_op=ALU.is_ge, fill=MASKED, base=P,
                                  pattern=[[0, NH], [-1, 2 * P]], channel_multiplier=1))
            sync()
            go(pool.affine_select(out=BIAS, in_=BIAS, compare_op=ALU.is_ge, fill=MASKED, base=-1,
                                  pattern=[[0, NH], [1, 2 * P]], channel_multiplier=-1))
            for g, w in enumerate(WINDOWS):
                go(pool.memset(MT[:, g], 1.0 / w))
            sync()
            for g, w in enumerate(WINDOWS):
                for t in range(w - 1):
                    go(pool.memset(MT[:, g, t:t + 1], 1.0 / (t + 1)))
            sync()
            for part in (slice(0, T), slice(T, T + P)):
                n = part.stop - part.start
                go(pool.affine_select(out=MT[:, :, part], in_=MT[:, :, part], compare_op=ALU.is_ge, fill=0.0, base=0,
                                      pattern=[[0, 4], [1, n]], channel_multiplier=-1))
            sync()
            for part in (slice(0, T), slice(T, T + P)):
                n = part.stop - part.start
                for g, w in enumerate(WINDOWS):
                    go(pool.affine_select(out=MT[:, g, part], in_=MT[:, g, part], compare_op=ALU.is_ge, fill=0.0,
                                          base=w - 1, pattern=[[-1, n]], channel_multiplier=1))
            sync()
            for g in range(4):
                for at in (0, T):
                    go(pool.tensor_tensor(MT[:, g, at:at + P], MT[:, g, at:at + P], IDENT, ALU.subtract))
            sync()
            pool.sem_inc(consts_ready, 1)

            u_rows = peer_u.rearrange("l n d -> (l n) d")
            v_rows = peer_v.rearrange("l n d -> (l n) d")
            for l in range(DEPTH):
                if l:
                    pool.wait_ge(layer_done, l)
                with nc.allow_non_contiguous_dma(reason="small parameter vectors"):
                    params([
                        (QKG[:, 0:HD], row(q_norm_g[l], P)), (QKG[:, HD:2 * HD], row(k_norm_g[l], P)),
                        (SINK, row(attn_sinks[l], P)), (MIXG, row(mix_norm_g[l], P)), (PSC, row(pool_scale[l], P)),
                        (POOLW, pool_w[l].rearrange("g c d -> c g d")),
                        (SUBK, peer_subkeys[l].rearrange("q n d -> n q d")),
                    ])
                for tt in range(TT):
                    pool.wait_ge(idx_ready, l * TT + TT)
                    base = (l * TT + tt) * SLOTS

                    def gather(i, s):
                        pool.wait_ge(u_loaded[s], i * 16 + (base // RING) * 16) if (base or not isinstance(i, int)) else None
                        pool.wait_ge(v_loaded[s], i * 16 + (base // RING) * 16) if (base or not isinstance(i, int)) else None
                        pool.wait_ge(dot_ready, i * RING + (base + s + 1))
                        pool.wait_ge(expert_added, i * RING + (base + s + 1))
                        pool.tensor_copy(STAGE[:, s:s + 1], IDX[:, tt, bass.ds(i * RING + s, 1)]).then_inc(staged, 1)
                        pool.wait_ge(staged, i * RING + (base + s + 1))
                        pool.sem_inc(stage_seen, 1)
                        off = bass.IndirectOffsetOnAxis(ap=STAGE[:, s:s + 1], axis=0)
                        pool.indirect_dma_start(out=GU[:, s, :], out_offset=None, in_=u_rows, in_offset=off).then_inc(u_loaded[s], 16)
                        pool.indirect_dma_start(out=GV[:, s, :], out_offset=None, in_=v_rows, in_offset=off).then_inc(v_loaded[s], 16)

                    for s in range(RING):
                        gather(0, s)
                    with pool.Fori(1, SLOTS // RING) as i:
                        for s in range(RING):
                            gather(i, s)

            for l in range(DEPTH):
                pool.wait_ge(layer_done, DEPTH + l)
                with nc.allow_non_contiguous_dma(reason="small parameter vectors"):
                    if l == 0:
                        params([(FINAL, row(final_norm_2, P))])
                    params([
                        (AN, row(attn_norm_2[l], P)), (FN, row(ffn_norm_2[l], P)),
                        (BFB, row(b_f_2[l], P)), (QG, row(q_norm_2[l], P)), (KG, row(kv_norm_2[l], P)),
                        (ON[:, 0:512], row(fox_out_norm_2[l], P)), (ON[:, 512:1024], row(mla_out_norm_2[l], P)),
                        (UQ, w_uq_2[l].rearrange("(k p) n -> p k n", p=P)), (UKV, w_ukv_2[l]),
                        (GR[:, :, 0:NG], w_group_2[l].rearrange("(p k) n -> p k n", k=KT)),
                        (GR[:, :, NG:NG + NE], w_router_2[l].rearrange("(p k) n -> p k n", k=KT)),
                    ])
                if l == 0:
                    go(pool.memset(UTRI, 1.0))
                    go(pool.memset(CMASK, 0.0))
                    go(pool.iota(RW[:, 48:56], [[1, 8]], base=0, channel_multiplier=0, allow_small_or_imprecise_dtypes=True))
                    sync()
                    go(pool.affine_select(out=UTRI, in_=UTRI, compare_op=ALU.is_ge, fill=0.0, base=0,
                                          pattern=[[-P, TT], [1, T]], channel_multiplier=-1))
                    go(pool.affine_select(out=CMASK[:, P:2 * P], in_=CMASK[:, P:2 * P], compare_op=ALU.is_ge,
                                          fill=MASKED, base=0, pattern=[[-1, P]], channel_multiplier=1))
                    sync()
                    pool.sem_inc(consts_ready, 1)

        @block.scalar
        def _(act):
            steps = [0]
            roots = [0]
            maxes = [0]

            def go(ins):
                steps[0] += 1
                ins.then_inc(scalar_step, 1)

            def sync():
                act.wait_ge(scalar_step, steps[0])

            def copy_out(name, dst, src):
                arrived(act, name)
                act.activation(dst, src, ACT.Copy).then_inc(evac["s"], 1)

            def root(parts, of_x=False):
                roots[0] += 1
                act.wait_ge(squares_ready, roots[0])
                if of_x:
                    for tt in range(TT):
                        go(act.activation(JUNK, X[:, tt], ACT.Square, accum_out=SSQ[:, tt:tt + 1]))
                        sync()
                for a, b, n in parts:
                    last = act.activation(RT[:, a:b], SSQ[:, a:b], ACT.Sqrt, bias=EPST, scale=1.0 / n)
                    if b != parts[-1][1]:
                        go(last)
                        sync()
                last.then_inc(root_ready, 1)

            def exps(S, sink):
                for tt in range(TT):
                    maxes[0] += 1
                    act.wait_ge(negmax_ready, maxes[0])
                    for h in range(NH):
                        act.activation(S[tt][:, h, :], S[tt][:, h, :], ACT.Exp, bias=NM[:, tt, h:h + 1],
                                       accum_out=DEN[:, tt, h:h + 1]).then_inc(probs_ready, 1)
                    if sink:
                        act.activation(EXS[:, tt], SE[:, tt], ACT.Exp).then_inc(probs_ready, 1)

            def transposed_probs(kind, l, PTX):
                for tt in range(TT):
                    for b in range(2 * (tt + 1)):
                        kt, h = divmod(4 * b, NH)
                        copy_out((kind + "pT", l, tt, b), PTX[:, kt, h:h + 4, :],
                                 bank((kind + "pT", l, tt, b)).rearrange("p (h q) -> p h q", h=4))

            def rows_transposed(kind, l):
                for tt in range(TT):
                    for half in range(2):
                        copy_out((kind, l, tt, half), HT[:, 4 * half:4 * half + 4, tt * P:(tt + 1) * P],
                                 bank((kind, l, tt, half)).rearrange("p (k t) -> p k t", k=4))

            act.wait_ge(cond_loaded, 16)
            act.activation(COND, COND, ACT.Silu).then_inc(cond_ready, 1)
            for n, table in enumerate((SIN, COS)):
                act.wait_ge(trig_in, n + 1)
                act.activation(table, table, ACT.Sin).then_inc(trig_out, 1)
            for l in range(DEPTH):
                for n in range(12):
                    if J[("ada", l, n)][2] == "s":
                        copy_out(("ada", l, n), MODL[l][:, n * 512:(n + 1) * 512], bank(("ada", l, n)))

            for l in range(DEPTH):
                root([(0, TT, D)], of_x=True)
                rows_transposed("hT", l)
                for c in range(3):
                    n = min(512, IN_A - c * 512)
                    for tt in range(TT):
                        copy_out(("in", l, c, tt), PROJ[:, tt, c * 512:c * 512 + n], bank(("in", l, c, tt))[:, 0:n])
                for b in range(2):
                    copy_out(("pool", l, b), POOLT[:, 2 * b:2 * b + 2, :],
                             bank(("pool", l, b)).rearrange("p (g t) -> p g t", g=2))
                root([(0, 20, HD)])
                for tt in range(TT):
                    copy_out(("qT", l, tt), QT[:, :, tt * P:(tt + 1) * P],
                             bank(("qT", l, tt)).rearrange("p (k t) -> p k t", k=4))
                copy_out(("kT", l), KTA, bank(("kT", l)).rearrange("p (k t) -> p k t", k=NKV))
                exps(S_A, True)
                transposed_probs("a", l, PT_A)
                root([(0, 4, 512)])
                rows_transposed("yT", l)
                copy_out(("subT", l), SUBT, bank(("subT", l))[:, 0:256].rearrange("p (k t) -> p k t", k=2))
                root([(0, TT, D)], of_x=True)
                rows_transposed("h2T", l)
                for b in range(8):
                    copy_out(("wq", l, b), QTP[:, 2 * b:2 * b + 2, :],
                             bank(("wq", l, b)).rearrange("p (g t) -> p g t", g=2))
                for tt in range(TT):
                    for b in range(4):
                        copy_out(("s", l, tt, b), SS[:, tt, 4 * b:4 * b + 4, :],
                                 bank(("s", l, tt, b)).rearrange("p (g t) -> p g t", g=4))
                for tt in range(TT):
                    act.wait_ge(gexp_in, l * TT + tt + 1)
                    act.activation(GATE[:, tt], GATE[:, tt], ACT.Exp).then_inc(gexp_out, 1)
                for tt in range(TT):
                    base = (l * TT + tt) * SLOTS
                    with act.Fori(0, SLOTS // RING) as i:
                        for s in range(RING):
                            act.wait_ge(dot_ready, i * RING + (base + s + 1 + RING))
                            act.activation(ACTV[:, s:s + 1], DOT[:, s:s + 1], ACT.Gelu).then_inc(gelu_ready, 1)

            for l in range(DEPTH):
                root([(0, TT, D)], of_x=True)
                rows_transposed("bhT", l)
                for b in range(4):
                    dst = (FQT, FKT)[b // 2]
                    copy_out(("fqk", l, b), dst[:, 2 * (b % 2):2 * (b % 2) + 2, :],
                             bank(("fqk", l, b)).rearrange("p (g t) -> p g t", g=2))
                for tt in range(TT):
                    copy_out(("fv", l, tt), FV[:, tt], bank(("fv", l, tt)))
                act.wait_ge(logsig_in, l + 1)
                z = RTMP[:, 16:32]
                go(act.activation(z, z, ACT.Exp, scale=-1.0))
                sync()
                act.activation(z, z, ACT.Ln, bias=ONES[:, 0:1]).then_inc(logsig_out, 1)
                root([(0, 2, QL), (2, 4, KVL)])
                for tt in range(TT):
                    copy_out(("cT", l, tt), CT[:, :, tt * P:(tt + 1) * P],
                             bank(("cT", l, tt))[:, 0:384].rearrange("p (k t) -> p k t", k=3))
                for tt in range(TT):
                    q = QM[:, tt].rearrange("p h d -> p (h d)")
                    kv = KV[:, tt].rearrange("p h d -> p (h d)")
                    for c in range(2):
                        n = min(512, 768 - 512 * c)
                        copy_out(("uq", l, tt, c), q[:, 512 * c:512 * c + n], bank(("uq", l, tt, c))[:, 0:n])
                    for c in range(2):
                        copy_out(("ukv", l, tt, c), kv[:, 512 * c:512 * c + 512], bank(("ukv", l, tt, c)))
                exps(S_B, False)
                transposed_probs("f", l, PT_B)
                for name, dst in (("qmT", QMT), ("kmT", KMT)):
                    for tt in range(TT):
                        for b in range(2):
                            copy_out((name, l, tt, b), dst[0:DK, 4 * b:4 * b + 4, tt * P:(tt + 1) * P],
                                     bank((name, l, tt, b))[0:DK].rearrange("p (g t) -> p g t", g=4))
                exps(S_B, False)
                transposed_probs("m", l, PT_B)
                root([(0, 32, HD)])
                rows_transposed("byT", l)
                root([(0, TT, D)], of_x=True)
                rows_transposed("fhT", l)
                for n in range(2):
                    act.wait_ge(router_in, 2 * l + n + 1)
                    z = RTMP[:, 100:116] if n == 0 else RTMP[:, 200:202]
                    act.activation(z, z, ACT.Exp).then_inc(router_out, 1)

                def silu(i, s):
                    e = i * EXP_RING + (l * NE + s)
                    act.wait_ge(gate_done, e + 1)
                    act.wait_ge(hidden_ready, e + 1)
                    act.activation(SG[:, s % 2], PS[:, s % 2, :], ACT.Silu).then_inc(silu_done, 1)

                with act.Fori(0, NE // EXP_RING) as i:
                    for s in range(EXP_RING):
                        silu(i, s)
            root([(0, TT, D)], of_x=True)

        @block.tensor
        def _(pe):
            rows = [0]
            probs = [0]

            def begin(name):
                n = J[name][0]
                if n >= NBANK:
                    taken(pe, JORDER[n - NBANK])

            def transpose_rows(kind, l, interleave=False):
                rows[0] += 1
                for tt in range(TT):
                    pe.wait_ge(rows_ready, 4 * (rows[0] - 1) + 2 * (tt + 1))
                    for half in range(2):
                        begin((kind, l, tt, half))
                        for k in range(4):
                            kk = 4 * half + k
                            src = HR[:, tt].rearrange("p (a k) -> p k a", k=KT)[:, kk] if interleave \
                                else HR[:, tt, kk * P:(kk + 1) * P]
                            last = pe.transpose(bank((kind, l, tt, half))[:, k * P:(k + 1) * P], src, IDENT)
                        last.then_inc(psum_ready, 1)

            def project(job, l, wname, c, n, order=range(TT)):
                loaded(pe, (wname, l, c))
                w = ring[CH[(wname, l, c)][1]][:, 0:KT * n].rearrange("p (k n) -> p k n", k=KT)
                for tt in order:
                    name = job(tt)
                    begin(name)
                    for k in range(KT):
                        last = pe.matmul(bank(name)[:, 0:n], HT[:, k, tt * P:(tt + 1) * P], w[:, k, :],
                                         start=(k == 0), stop=(k == KT - 1))
                    last.then_inc(psum_ready, 1)

            def release():
                pe.sem_inc(chunk_used["p"], 1)

            def weights_first(name, l, wname, c, cols, first, final):
                if first:
                    loaded(pe, (wname, l, c))
                w = ring[CH[(wname, l, c)][1]][:, :].rearrange("p (k n) -> p k n", k=KT)
                begin(name)
                for j in range(2):
                    at = cols + j * P
                    for k in range(KT):
                        last = pe.matmul(bank(name)[:, j * T:(j + 1) * T], w[:, k, at:at + P], HT[:, k, :],
                                         start=(k == 0), stop=(k == KT - 1))
                last.then_inc(psum_ready, 1)

            def attend(kind, l, S, PTX, score, value, sink):
                for tt in range(TT):
                    nk = (tt + 1) * P
                    per = 512 // nk
                    for b in range(NH // per):
                        name = (kind + "sc", l, tt, b)
                        begin(name)
                        for j in range(per):
                            h = first_head(b, per) + 2 * j
                            last = score(bank(name)[:, j * nk:(j + 1) * nk], h, tt, nk)
                        last.then_inc(psum_ready, 1)
                for tt in range(TT):
                    probs[0] += NH + sink
                    pe.wait_ge(probs_ready, probs[0])
                    for b in range(2 * (tt + 1)):
                        name = (kind + "pT", l, tt, b)
                        begin(name)
                        kt, h = divmod(4 * b, NH)
                        for j in range(4):
                            last = pe.transpose(bank(name)[:, j * P:(j + 1) * P],
                                                S[tt][:, h + j, kt * P:(kt + 1) * P], IDENT)
                        last.then_inc(psum_ready, 1)
                    begin((kind + "pv", l, tt))
                    taken(pe, (kind + "pT", l, tt, 2 * (tt + 1) - 1))
                    for h in range(NH):
                        for kt in range(tt + 1):
                            last = pe.matmul(bank((kind + "pv", l, tt))[:, h * HD:(h + 1) * HD], PTX[:, kt, h, :],
                                             value(kt, h), start=(kt == 0), stop=(kt == tt))
                    last.then_inc(psum_ready, 1)

            pe.sem_inc(expert_added, RING)
            pe.wait_ge(consts_ready, 1)
            for l in range(DEPTH):
                pe.wait_ge(acc_ready, l + 1)
                for n in range(12):
                    begin(("ada", l, n))
                    pe.matmul(bank(("ada", l, n)), ONES, MODL[l][:, n * 512:(n + 1) * 512],
                              start=True, stop=True).then_inc(psum_ready, 1)

            for l in range(DEPTH):
                transpose_rows("hT", l)
                taken(pe, ("hT", l, 1, 1))
                for c in range(3):
                    project(lambda tt: ("in", l, c, tt), l, "in", c, min(512, IN_A - 512 * c))
                    arrived(pe, ("in", l, c, 1))
                    release()
                pe.wait_ge(params_loaded, 16 * 7 * (l + 1))
                taken(pe, ("in", l, 0, 1))
                for b in range(2):
                    begin(("pool", l, b))
                    for j in range(2):
                        g = 2 * b + j
                        to = bank(("pool", l, b))[:, j * T:(j + 1) * T]
                        pe.matmul(to, PROJ[:, 0, g * P:(g + 1) * P], MT[:, g, 0:T], start=True, stop=False)
                        last = pe.matmul(to[:, P:T], PROJ[:, 1, g * P:(g + 1) * P], MT[:, g, T:T + P],
                                         start=False, stop=True)
                    last.then_inc(psum_ready, 1)
                taken(pe, ("pool", l, 1))
                for tt in range(TT):
                    begin(("mix", l, tt))
                    for g in range(4):
                        last = pe.matmul(bank(("mix", l, tt))[:, g * P:(g + 1) * P], POOLT[:, g, tt * P:(tt + 1) * P],
                                         POOLW[:, g, :], start=True, stop=True)
                    last.then_inc(psum_ready, 1)
                pe.wait_ge(qk_ready, 3 * (l + 1))
                for tt in range(TT):
                    begin(("qT", l, tt))
                    for j in range(4):
                        last = pe.transpose(bank(("qT", l, tt))[:, j * P:(j + 1) * P],
                                            PROJ[:, tt, POOL + j * P:POOL + (j + 1) * P], IDENT)
                    last.then_inc(psum_ready, 1)
                begin(("kT", l))
                for kv in range(NKV):
                    for tt in range(TT):
                        at = kv * T + tt * P
                        last = pe.transpose(bank(("kT", l))[:, at:at + P],
                                            KD[:, tt, kv].rearrange("p u d -> p (u d)"), IDENT)
                last.then_inc(psum_ready, 1)
                taken(pe, ("kT", l))

                def score(to, h, tt, nk):
                    at = HD * (h % 2)
                    return pe.matmul(to, QT[at:at + HD, h // 2, tt * P:(tt + 1) * P],
                                     KTA[at:at + HD, h // (NH // NKV), 0:nk], start=True, stop=True)

                attend("a", l, S_A, PT_A, score,
                       lambda kt, h: PROJ[:, kt, 1152 + (h // 4) * HD:1152 + (h // 4 + 1) * HD], 1)
                transpose_rows("yT", l)
                taken(pe, ("yT", l, 1, 1))
                for c in range(2):
                    project(lambda tt: ("out", l, c, tt), l, "out", c, 512)
                    arrived(pe, ("out", l, c, 1))
                    release()
                begin(("subT", l))
                for q in range(2):
                    last = pe.transpose(bank(("subT", l))[:, q * P:(q + 1) * P], SUBK[:, q, :], IDENT)
                last.then_inc(psum_ready, 1)
                transpose_rows("h2T", l)
                taken(pe, ("h2T", l, 1, 1))
                for c in range(4):
                    for j in range(2):
                        weights_first(("wq", l, 2 * c + j), l, "wq", c, 2 * P * j, j == 0, j == 1)
                    arrived(pe, ("wq", l, 2 * c + 1))
                    release()
                taken(pe, ("wq", l, 7))
                for tt in range(TT):
                    for b in range(4):
                        begin(("s", l, tt, b))
                        for j in range(4):
                            hp = 4 * b + j
                            last = pe.matmul(bank(("s", l, tt, b))[:, j * P:(j + 1) * P],
                                             QTP[:, hp, tt * P:(tt + 1) * P], SUBT[:, hp % 2, :],
                                             start=True, stop=True)
                        last.then_inc(psum_ready, 1)
                for tt in range(TT):
                    base = (l * TT + tt) * SLOTS

                    def add(i, s, first=False):
                        pe.wait_ge(v_loaded[s], i * 16 + (base // RING + 1) * 16)
                        pe.wait_ge(diag_ready, i * RING + (base + s + 1))
                        for half in range(2):
                            last = pe.matmul(PO[:, half, :], DIAG[:, s, :], GV[:, s, half * 512:(half + 1) * 512],
                                             start=first, stop=False, skip_group_check=True)
                        last.then_inc(expert_added, 1)

                    if base:
                        pe.wait_ge(sums_read, 2 * (l * TT + tt))
                    for s in range(RING):
                        add(0, s, s == 0)
                    with pe.Fori(1, SLOTS // RING) as i:
                        for s in range(RING):
                            add(i, s)

            for l in range(DEPTH):
                transpose_rows("bhT", l)
                taken(pe, ("bhT", l, 1, 1))
                for c in range(2):
                    for j in range(2):
                        weights_first(("fqk", l, 2 * c + j), l, "bin", c, 2 * P * j, j == 0, j == 1)
                    arrived(pe, ("fqk", l, 2 * c + 1))
                    release()
                project(lambda tt: ("fv", l, tt), l, "bin", 2, 512)
                arrived(pe, ("fv", l, 1))
                release()
                project(lambda tt: ("rest", l, tt), l, "bin", 3, REST)
                arrived(pe, ("rest", l, 1))
                release()
                pe.wait_ge(cn_ready, 4 * (l + 1))
                for tt in range(TT):
                    begin(("cT", l, tt))
                    for j in range(3):
                        last = pe.transpose(bank(("cT", l, tt))[:, j * P:(j + 1) * P],
                                            R[:, tt, 8 + j * P:8 + (j + 1) * P], IDENT)
                    last.then_inc(psum_ready, 1)
                for tt in range(TT):
                    taken(pe, ("cT", l, tt))
                    for c in range(2):
                        n = min(512, 768 - 512 * c)
                        begin(("uq", l, tt, c))
                        for k in range(2):
                            last = pe.matmul(bank(("uq", l, tt, c))[:, 0:n], CT[:, k, tt * P:(tt + 1) * P],
                                             UQ[:, k, 512 * c:512 * c + n], start=(k == 0), stop=(k == 1))
                        last.then_inc(psum_ready, 1)
                    for c in range(2):
                        begin(("ukv", l, tt, c))
                        pe.matmul(bank(("ukv", l, tt, c)), CT[:, 2, tt * P:(tt + 1) * P],
                                  UKV[:, 512 * c:512 * c + 512], start=True, stop=True).then_inc(psum_ready, 1)
                pe.wait_ge(decay_ready, l + 1)
                if l == 0:
                    pe.wait_ge(consts_ready, 2)

                def fox_score(to, h, tt, nk):
                    at = HD * (h % 2)
                    pe.matmul(to, FQT[at:at + HD, h // 2, tt * P:(tt + 1) * P], FKT[at:at + HD, h // 2, 0:nk],
                              start=True, stop=False)
                    for k in range(tt + 1):
                        last = pe.matmul(to, LFB[:, k, h, :], UTRI[:, k, 0:nk], start=False, stop=(k == tt))
                    return last

                attend("f", l, S_B, PT_B, fox_score, lambda kt, h: FV[:, kt, h * HD:(h + 1) * HD], 0)
                pe.wait_ge(mla_ready, 2 * (l + 1))
                for name, src in (("qmT", QM), ("kmT", KM)):
                    for tt in range(TT):
                        for b in range(2):
                            begin((name, l, tt, b))
                            for j in range(4):
                                last = pe.transpose(bank((name, l, tt, b))[0:DK, j * P:(j + 1) * P],
                                                    src[:, tt, 4 * b + j, :], IDENT)
                            last.then_inc(psum_ready, 1)
                taken(pe, ("kmT", l, 1, 1))

                def mla_score(to, h, tt, nk):
                    return pe.matmul(to, QMT[0:DK, h, tt * P:(tt + 1) * P], KMT[0:DK, h, 0:nk], start=True, stop=True)

                attend("m", l, S_B, PT_B, mla_score, lambda kt, h: KV[:, kt, h, HD:2 * HD], 0)
                transpose_rows("byT", l)
                taken(pe, ("byT", l, 1, 1))
                for c in range(2):
                    project(lambda tt: ("bout", l, c, tt), l, "bout", c, 512)
                    arrived(pe, ("bout", l, c, 1))
                    release()
                transpose_rows("fhT", l, interleave=True)
                taken(pe, ("fhT", l, 1, 1))
                for tt in range(TT):
                    begin(("route", l, tt))
                    for k in range(KT):
                        last = pe.matmul(bank(("route", l, tt))[:, 0:NG + NE], HT[:, k, tt * P:(tt + 1) * P],
                                         GR[:, k, :], start=(k == 0), stop=(k == KT - 1))
                    last.then_inc(psum_ready, 1)
                taken(pe, ("route", l, 1))

                def gate_up(i, s):
                    e = i * EXP_RING + (l * NE + s)
                    pe.wait_ge(expert_loaded[s], i * 48 + (l * (NE // EXP_RING) + 1) * 48)
                    pe.wait_ge(hidden_ready, e + 1)
                    for w, at, done in ((WG[s], 0, gate_done), (WU[s], 2, up_done)):
                        for f in range(2):
                            for k in range(KT):
                                last = pe.matmul(PS[:, at + s % 2, f * T:(f + 1) * T], w[:, k, f * P:(f + 1) * P],
                                                 HT[:, k, :], start=(k == 0), stop=(k == KT - 1))
                        last.then_inc(done, 1)

                def down(i, s):
                    e = i * EXP_RING + (l * NE + s)
                    pe.wait_ge(hidden_ready, e + 3)
                    for tt in range(TT):
                        for c in range(2):
                            pe.wait_ge(down_added, e * 4 + (2 * tt + c + 1))
                            for j in range(2):
                                last = pe.matmul(PS[:, 4 + 2 * tt + c, :], HH[:, s % 2, j, tt * P:(tt + 1) * P],
                                                 WD[s][:, j, c * 512:(c + 1) * 512], start=(j == 0), stop=(j == 1))
                            last.then_inc(down_done, 1)

                gate_up(0, 0)
                for s in range(1, EXP_RING):
                    gate_up(0, s)
                    down(0, s - 1)
                with pe.Fori(1, NE // EXP_RING) as i:
                    gate_up(i, 0)
                    down(i - 1, EXP_RING - 1)
                    for s in range(1, EXP_RING):
                        gate_up(i, s)
                        down(i, s - 1)
                down(NE // EXP_RING - 1, EXP_RING - 1)

        @block.vector
        def _(dve):
            steps = [0]
            roots = [0]
            atts = [0]
            probs = [0]

            def go(ins):
                steps[0] += 1
                ins.then_inc(vector_step, 1)

            def sync():
                dve.wait_ge(vector_step, steps[0])

            def step(ins):
                go(ins)
                sync()

            def root(n):
                dve.sem_inc(squares_ready, 1)
                roots[0] += 1
                dve.wait_ge(root_ready, roots[0])
                step(dve.reciprocal(RS[:, 0:n], RT[:, 0:n]))

            def attention_rows(kind, l, S, scale, bias, sink):
                for tt in range(TT):
                    nk = (tt + 1) * P
                    per = 512 // nk
                    for b in range(NH // per):
                        name = (kind + "sc", l, tt, b)
                        arrived(dve, name)
                        heads = slice(first_head(b, per), first_head(b, per) + 2 * per - 1, 2)
                        dve.scalar_tensor_tensor(S[tt][:, heads, :],
                                                 bank(name).rearrange("p (h s) -> p h s", h=per), scale,
                                                 bias(tt, heads, per, nk), ALU.mult, ALU.add).then_inc(evac["v"], 1)
                    taken(dve, name)
                    step(dve.tensor_reduce(MX[:, tt], S[tt], AX, ALU.max))
                    if sink:
                        step(dve.tensor_tensor(MX[:, tt], MX[:, tt], SINK, ALU.max))
                        step(dve.tensor_tensor(SE[:, tt], SINK, MX[:, tt], ALU.subtract))
                    dve.tensor_scalar(NM[:, tt], MX[:, tt], -1.0, None, ALU.mult).then_inc(negmax_ready, 1)
                    atts[0] += 1
                    dve.wait_ge(negmax_ready, atts[0])

            def attention_values(kind, l, at, sink):
                for tt in range(TT):
                    probs[0] += NH + sink
                    dve.wait_ge(probs_ready, probs[0])
                    if sink:
                        step(dve.tensor_tensor(DEN[:, tt], DEN[:, tt], EXS[:, tt], ALU.add))
                    step(dve.reciprocal(RD[:, tt], DEN[:, tt]))
                    arrived(dve, (kind + "pv", l, tt))
                    dve.tensor_tensor(HR[:, tt, at:at + 512].rearrange("p (h d) -> p h d", h=NH),
                                      bank((kind + "pv", l, tt)).rearrange("p (h d) -> p h d", h=NH),
                                      RD[:, tt, :].unsqueeze(2).broadcast_to([P, NH, HD]), ALU.mult).then_inc(evac["v"], 1)

            dve.sem_inc(dot_ready, RING)
            dve.sem_inc(hidden_ready, 2)
            dve.sem_inc(down_added, 4)

            FREQ, ANG, TURN = TMP[:, 0:16], TMP[:, 32:64], TMP[:, 64:96]
            POS = RW[:, 2:4]
            for k in range(16):
                go(dve.memset(FREQ[:, k:k + 1], 10000.0 ** (-k / 16.0)))
            dve.wait_ge(pos_loaded, 16)
            step(dve.tensor_copy(POS, RW[:, 0:TT].bitcast(I32)))
            for tt in range(TT):
                step(dve.tensor_scalar(ANG[:, tt * 16:(tt + 1) * 16], FREQ, POS[:, tt:tt + 1], None, ALU.mult))
            C1 = 6.28125
            C2 = 0.0019350051879882812
            C3 = 2 * pi - C1 - C2
            for n, (table, turn, quarter) in enumerate(((SIN, 0.0, 0.0), (COS, 0.25, pi / 2))):
                tab = table.rearrange("p t f -> p (t f)")
                step(dve.tensor_scalar(TURN, ANG, 1.0 / (2 * pi), turn, ALU.mult, ALU.add))
                step(dve.tensor_scalar(TURN, TURN, 12582912.0, None, ALU.add))
                step(dve.tensor_scalar(TURN, TURN, 12582912.0, None, ALU.subtract))
                step(dve.scalar_tensor_tensor(tab, TURN, -C1, ANG, ALU.mult, ALU.add))
                step(dve.scalar_tensor_tensor(tab, TURN, -C2, tab, ALU.mult, ALU.add))
                step(dve.scalar_tensor_tensor(tab, TURN, -C3, tab, ALU.mult, ALU.add))
                step(dve.tensor_scalar(tab, tab, quarter, 3.1415925, ALU.add, ALU.min))
                step(dve.tensor_scalar(tab, tab, -3.1415925, None, ALU.max))
                dve.sem_inc(trig_in, 1)

            dve.wait_ge(cond_ready, 1)
            dve.wait_ge(bada_loaded, 16 * DEPTH)
            for l in range(DEPTH):
                for c3 in range(3):
                    for kp in range(4):
                        name = ("ada", l, c3, kp)
                        loaded(dve, name)
                        w = ring[CH[name][1]].rearrange("p (k n) -> p k n", k=2)
                        acc = MODL[l][:, c3 * 2048:(c3 + 1) * 2048]
                        for k in range(2):
                            step(dve.scalar_tensor_tensor(acc, w[:, k, :], COND[:, 2 * kp + k:2 * kp + k + 1], acc,
                                                          ALU.mult, ALU.add))
                        dve.sem_inc(chunk_used["v"], 1)
                dve.sem_inc(acc_ready, 1)
            dve.wait_ge(gains_loaded, 64)
            for l in range(DEPTH):
                for n in range(12):
                    name = ("ada", l, n)
                    if J[name][2] == "v":
                        arrived(dve, name)
                        gain = NGAIN[:, 2 * l + (n // 2 == 4), (n % 2) * 512:(n % 2 + 1) * 512]
                        dve.scalar_tensor_tensor(MODL[l][:, n * 512:(n + 1) * 512], bank(name), 1.0, gain,
                                                 ALU.add, ALU.mult).then_inc(evac["v"], 1)

            def modulated(l, i):
                for tt in range(TT):
                    step(dve.scalar_tensor_tensor(HR[:, tt], X[:, tt], RS[:, tt:tt + 1], mrow(l, i + 1), ALU.mult, ALU.mult))
                    dve.tensor_tensor(HR[:, tt], HR[:, tt], mrow(l, i), ALU.add).then_inc(rows_ready, 2)

            dve.wait_ge(x_loaded, 16)
            for l in range(DEPTH):
                root(TT)
                taken(dve, ("ada", l, 11))
                taken(dve, ("ada", l, 9))
                modulated(l, 0)
                dve.wait_ge(params_loaded, 16 * 7 * (l + 1))
                taken(dve, ("in", l, 2, 1))
                qk = PROJ[:, :, POOL:POOL + 640]
                sq = QSQ.rearrange("p (t n) -> p t n", t=TT)
                step(dve.tensor_tensor(sq, qk, qk, ALU.mult))
                step(dve.tensor_reduce(SSQ[:, 0:20], QSQ.rearrange("p (h d) -> p h d", d=HD), AX, ALU.add))
                root(20)
                heads = qk.rearrange("p t (h d) -> p t h d", d=HD)
                rs = RS[:, 0:20].rearrange("p (t h) -> p t h", t=TT)
                step(dve.tensor_tensor(heads, heads, rs.unsqueeze(3).broadcast_to([P, TT, 10, HD]), ALU.mult))
                for tt in range(TT):
                    q = heads[:, tt, 0:NH]
                    ins = dve.tensor_tensor(q, q, QKG[:, 0:HD].unsqueeze(1).broadcast_to([P, NH, HD]), ALU.mult)
                    if tt == 0:
                        step(ins)
                    else:
                        ins.then_inc(qk_ready, 1)
                for u in range(2):
                    for tt in range(TT):
                        ins = dve.tensor_tensor(KD[:, tt, :, u, :], heads[:, tt, NH:NH + NKV],
                                                QKG[:, HD:2 * HD].unsqueeze(1).broadcast_to([P, NKV, HD]), ALU.mult)
                        if tt == 0:
                            step(ins)
                        else:
                            ins.then_inc(qk_ready, 1)
                for tt in range(TT):
                    arrived(dve, ("mix", l, tt))
                    dve.tensor_tensor(HR[:, tt, 0:512], bank(("mix", l, tt)), PSC, ALU.mult).then_inc(evac["v"], 1)
                attention_rows("a", l, S_A, HD ** -0.5,
                               lambda tt, heads, per, nk: BIAS[:, heads, 2 * P - nk:2 * P], True)
                attention_values("a", l, 512, 1)
                taken(dve, ("apv", l, 1))
                for tt in range(TT):
                    for half in range(2):
                        y = HR[:, tt, half * 512:(half + 1) * 512]
                        n = 2 * tt + half
                        step(dve.tensor_tensor_reduce(JUNK[:, 0:512], y, y, 1.0, 0.0, ALU.mult, ALU.add, SSQ[:, n:n + 1]))
                root(4)
                for tt in range(TT):
                    for half in range(2):
                        y = HR[:, tt, half * 512:(half + 1) * 512]
                        n = 2 * tt + half
                        dve.scalar_tensor_tensor(y, y, RS[:, n:n + 1], MIXG[:, half * 512:(half + 1) * 512],
                                                 ALU.mult, ALU.mult).then_inc(rows_ready, 1)
                for c in range(2):
                    for tt in range(TT):
                        name = ("out", l, c, tt)
                        arrived(dve, name)
                        part = slice(c * 512, (c + 1) * 512)
                        dve.tensor_tensor(TMP, bank(name), mrow(l, 2)[:, part], ALU.mult).then_inc(evac["v"], 1)
                        taken(dve, name)
                        step(dve.tensor_tensor(X[:, tt, part], X[:, tt, part], TMP, ALU.add))
                root(TT)
                modulated(l, 3)

                def best16(n, values, vals, idxs):
                    for a in range(n):
                        go(dve.max(vals[:, a, 0:8], values[:, a, :]))
                    sync()
                    for a in range(n):
                        go(dve.max_index(idxs[:, a, 0:8], vals[:, a, 0:8], values[:, a, :]))
                    sync()
                    for a in range(n):
                        go(dve.match_replace(values[:, a, :], vals[:, a, 0:8], values[:, a, :], LOWEST))
                    sync()
                    for a in range(n):
                        go(dve.max(vals[:, a, 8:16], values[:, a, :]))
                    sync()
                    for a in range(n):
                        go(dve.max_index(idxs[:, a, 8:16], vals[:, a, 8:16], values[:, a, :]))
                    sync()

                for tt in range(TT):
                    taken(dve, ("s", l, TT - 1, 3))
                    best16(16, SS[:, tt], V16, I16)
                    step(dve.tensor_copy(F16, I16))
                    v2 = V16.rearrange("p (h q) k -> p h q k", q=2)
                    f2 = F16.rearrange("p (h q) k -> p h q k", q=2)
                    wide = [P, PH, TOPK, TOPK]
                    step(dve.tensor_tensor(CAND.rearrange("p h (i j) -> p h i j", i=TOPK),
                                           v2[:, :, 0, :].unsqueeze(3).broadcast_to(wide),
                                           v2[:, :, 1, :].unsqueeze(2).broadcast_to(wide), ALU.add))
                    best16(PH, CAND, BV, BI)
                    for half, (op, by, dst) in enumerate(((ALU.logical_shift_right, 4, E1), (ALU.bitwise_and, 15, E2))):
                        step(dve.tensor_scalar(BU, BI, by, None, op))
                        step(dve.tensor_copy(BF, BU))
                        flat = OH.rearrange("p h k c -> p (h k) c")
                        step(dve.tensor_tensor(flat, BF.rearrange("p h k -> p (h k)").unsqueeze(2).broadcast_to([P, SLOTS, TOPK]),
                                               IOTA.unsqueeze(1).broadcast_to([P, SLOTS, TOPK]), ALU.is_equal))
                        step(dve.tensor_tensor(OH, OH, f2[:, :, half, :].unsqueeze(2).broadcast_to(wide), ALU.mult))
                        step(dve.tensor_reduce(dst, OH, AX, ALU.add))
                    step(dve.scalar_tensor_tensor(E1, E1, float(NKEY), E2, ALU.mult, ALU.add))
                    gate = GATE[:, tt].rearrange("p (h k) -> p h k", h=PH)
                    step(dve.tensor_tensor(gate, BV, BV[:, :, 0:1].broadcast_to([P, PH, TOPK]), ALU.subtract))
                    dve.sem_inc(gexp_in, 1)
                    dve.tensor_scalar(IDX[:, tt].rearrange("p (h k) -> p h k", h=PH), E1, float(l * NEXP), None,
                                      ALU.add).then_inc(idx_ready, 1)
                    dve.wait_ge(gexp_out, l * TT + tt + 1)
                    step(dve.tensor_reduce(RS[:, 0:PH], gate, AX, ALU.add))
                    step(dve.reciprocal(RT[:, 0:PH], RS[:, 0:PH]))
                    step(dve.tensor_tensor(gate, gate, RT[:, 0:PH].unsqueeze(2).broadcast_to([P, PH, TOPK]), ALU.mult))

                for tt in range(TT):
                    base = (l * TT + tt) * SLOTS

                    def dot(i, s):
                        dve.wait_ge(u_loaded[s], i * 16 + (base // RING + 1) * 16)
                        dve.wait_ge(dot_ready, i * RING + (base + s + RING))
                        dve.tensor_tensor_reduce(JUNK, GU[:, s, :], HR[:, tt], 1.0, 0.0, ALU.mult, ALU.add,
                                                 DOT[:, s:s + 1]).then_inc(dot_ready, 1)

                    def diag(i, s):
                        dve.wait_ge(gelu_ready, i * RING + (base + s + 1))
                        dve.wait_ge(expert_added, i * RING + (base + s + 1))
                        dve.tensor_scalar(DIAG[:, s, :], IDENT, ACTV[:, s:s + 1], GATE[:, tt, bass.ds(i * RING + s, 1)],
                                          ALU.mult, ALU.mult).then_inc(diag_ready, 1)

                    dot(0, 0)
                    for s in range(1, RING):
                        dot(0, s)
                        diag(0, s - 1)
                    with dve.Fori(1, SLOTS // RING) as i:
                        dot(i, 0)
                        diag(i - 1, RING - 1)
                        for s in range(1, RING):
                            dot(i, s)
                            diag(i, s - 1)
                    diag(SLOTS // RING - 1, RING - 1)
                    dve.wait_ge(expert_added, base + SLOTS + RING)
                    for half in range(2):
                        part = slice(half * 512, (half + 1) * 512)
                        dve.tensor_tensor(TMP, PO[:, half, :], mrow(l, 5)[:, part], ALU.mult).then_inc(sums_read, 1)
                        dve.wait_ge(sums_read, 2 * (l * TT + tt) + half + 1)
                        step(dve.tensor_tensor(X[:, tt, part], X[:, tt, part], TMP, ALU.add))
                dve.sem_inc(layer_done, 1)

            def gained(gain, inc):
                for tt in range(TT):
                    dve.scalar_tensor_tensor(HR[:, tt], X[:, tt], RS[:, tt:tt + 1], gain, ALU.mult,
                                             ALU.mult).then_inc(inc, 2 if inc is rows_ready else 1)

            pb = 16 * 7 * DEPTH + 16
            for l in range(DEPTH):
                root(TT)
                dve.wait_ge(params_loaded, pb + 16 * 11 * (l + 1))
                gained(AN, rows_ready)
                for tt in range(TT):
                    arrived(dve, ("rest", l, tt))
                    dve.tensor_copy(R[:, tt, :], bank(("rest", l, tt))[:, 0:REST]).then_inc(evac["v"], 1)
                taken(dve, ("rest", l, 1))
                z, az = RTMP[:, 0:16].rearrange("p (t h) -> p t h", t=TT), RTMP[:, 16:32].rearrange("p (t h) -> p t h", t=TT)
                step(dve.tensor_tensor(z, R[:, :, 0:NH], BFB.unsqueeze(1).broadcast_to([P, TT, NH]), ALU.add))
                step(dve.tensor_scalar(az, z, -1.0, None, ALU.mult))
                step(dve.tensor_tensor(az, az, z, ALU.max))
                dve.sem_inc(logsig_in, 1)
                for tt in range(TT):
                    for n, (a, b) in enumerate(((8, 8 + QL), (8 + QL, 8 + QL + KVL))):
                        y = R[:, tt, a:b]
                        step(dve.tensor_tensor_reduce(JUNK[:, 0:b - a], y, y, 1.0, 0.0, ALU.mult, ALU.add,
                                                      SSQ[:, 2 * n + tt:2 * n + tt + 1]))
                dve.wait_ge(logsig_out, l + 1)
                step(dve.tensor_scalar(z, z, 0.0, None, ALU.min))
                step(dve.tensor_tensor(z, z, az, ALU.subtract))
                step(dve.tensor_scalar(z, z, -(HD ** 0.5), None, ALU.mult))
                dve.tensor_copy(LFB, z.unsqueeze(3).broadcast_to([P, TT, NH, P])).then_inc(decay_ready, 1)
                root(4)
                for tt in range(TT):
                    for n, (a, b, gain) in enumerate(((8, 8 + QL, QG), (8 + QL, 8 + QL + KVL, KG))):
                        y = R[:, tt, a:b]
                        dve.scalar_tensor_tensor(y, y, RS[:, 2 * n + tt:2 * n + tt + 1], gain, ALU.mult,
                                                 ALU.mult).then_inc(cn_ready, 1)
                if l == 0:
                    dve.wait_ge(trig_out, 2)
                    dve.wait_ge(consts_ready, 2)
                kr = R[:, :, 8 + QL + KVL:REST]
                kt = [RTMP[:, 300 + 32 * i:332 + 32 * i].rearrange("p (t f) -> p t f", t=TT) for i in range(4)]
                go(dve.tensor_tensor(kt[0], kr[:, :, 0:16], COS, ALU.mult))
                go(dve.tensor_tensor(kt[1], kr[:, :, 16:32], SIN, ALU.mult))
                go(dve.tensor_tensor(kt[2], kr[:, :, 16:32], COS, ALU.mult))
                step(dve.tensor_tensor(kt[3], kr[:, :, 0:16], SIN, ALU.mult))
                go(dve.tensor_tensor(kt[0], kt[0], kt[1], ALU.subtract))
                step(dve.tensor_tensor(kt[2], kt[2], kt[3], ALU.add))
                for tt in range(TT):
                    for n, src in ((0, kt[0]), (1, kt[2])):
                        go(dve.tensor_copy(KM[:, tt, :, HD + 16 * n:HD + 16 * n + 16],
                                           src[:, tt].unsqueeze(1).broadcast_to([P, NH, 16])))
                taken(dve, ("ukv", l, 1, 1))
                for tt in range(TT):
                    step(dve.tensor_copy(KM[:, tt, :, 0:HD], KV[:, tt, :, 0:HD]))
                dve.sem_inc(mla_ready, 1)
                for tt in range(TT):
                    x1, x2 = QM[:, tt, :, HD:HD + 16], QM[:, tt, :, HD + 16:DK]
                    cs, sn = (t[:, tt].unsqueeze(1).broadcast_to([P, NH, 16]) for t in (COS, SIN))
                    qt = [RTMP[:, 430 + 128 * i:558 + 128 * i].rearrange("p (h f) -> p h f", h=NH) for i in range(4)]
                    go(dve.tensor_tensor(qt[0], x1, cs, ALU.mult))
                    go(dve.tensor_tensor(qt[1], x2, sn, ALU.mult))
                    go(dve.tensor_tensor(qt[2], x2, cs, ALU.mult))
                    step(dve.tensor_tensor(qt[3], x1, sn, ALU.mult))
                    go(dve.tensor_tensor(x1, qt[0], qt[1], ALU.subtract))
                    step(dve.tensor_tensor(x2, qt[2], qt[3], ALU.add))
                dve.sem_inc(mla_ready, 1)

                def causal(tt, heads, per, nk):
                    return CMASK[:, 2 * P - nk:2 * P].unsqueeze(1).broadcast_to([P, per, nk])

                attention_rows("f", l, S_B, HD ** -0.5, causal, False)
                attention_values("f", l, 0, 0)
                attention_rows("m", l, S_B, DK ** -0.5, causal, False)
                attention_values("m", l, 512, 0)
                taken(dve, ("mpv", l, 1))
                sq = SQB.rearrange("p (t n) -> p t n", t=TT)
                step(dve.tensor_tensor(sq, HR, HR, ALU.mult))
                step(dve.tensor_reduce(SSQ[:, 0:32], SQB.rearrange("p (h d) -> p h d", d=HD), AX, ALU.add))
                root(32)
                for tt in range(TT):
                    y = HR[:, tt].rearrange("p (h d) -> p h d", d=HD)
                    step(dve.tensor_tensor(y, y, RS[:, 16 * tt:16 * tt + 16].unsqueeze(2).broadcast_to([P, 16, HD]), ALU.mult))
                    dve.tensor_tensor(HR[:, tt], HR[:, tt], ON, ALU.mult).then_inc(rows_ready, 2)
                for c in range(2):
                    for tt in range(TT):
                        name = ("bout", l, c, tt)
                        arrived(dve, name)
                        part = slice(c * 512, (c + 1) * 512)
                        dve.tensor_tensor(X[:, tt, part], X[:, tt, part], bank(name), ALU.add).then_inc(evac["v"], 1)
                taken(dve, ("bout", l, 1, 1))
                root(TT)
                gained(FN, rows_ready)

                GL = RTMP[:, 0:80].rearrange("p (t n) -> p t n", t=TT)
                for tt in range(TT):
                    arrived(dve, ("route", l, tt))
                    dve.tensor_copy(GL[:, tt], bank(("route", l, tt))[:, 0:NG + NE]).then_inc(evac["v"], 1)
                taken(dve, ("route", l, 1))
                gexp = RTMP[:, 100:116].rearrange("p (t g) -> p t g", t=TT)
                gtop = RTMP[:, 120:136].rearrange("p (t g) -> p t g", t=TT)
                gidx = RTMP[:, 140:156].rearrange("p (t g) -> p t g", t=TT).bitcast(U32)
                gone = RTMP[:, 160:176].rearrange("p (t g) -> p t g", t=TT)
                gfl = RTMP[:, 180:196].rearrange("p (t g) -> p t g", t=TT)
                d2 = RTMP[:, 200:202].rearrange("p (t g) -> p t g", t=TT)
                ig = RTMP[:, 210:226].rearrange("p (t g) -> p t g", t=TT)
                itop = RTMP[:, 230:246].rearrange("p (t g) -> p t g", t=TT)
                iidx = RTMP[:, 250:266].rearrange("p (t g) -> p t g", t=TT).bitcast(U32)
                ifl = RTMP[:, 270:286].rearrange("p (t g) -> p t g", t=TT)
                prod = RTMP[:, 300:364].rearrange("p (t g e) -> p t g e", t=TT, g=NG)
                sm = RTMP[:, 400:440].rearrange("p (n t g) -> p n t g", n=20, t=TT)
                w4 = RTMP[:, 450:466].rearrange("p (n t e) -> p n t e", n=2, t=TT)
                iota8 = RW[:, 48:56]
                for tt in range(TT):
                    go(dve.max(gtop[:, tt], GL[:, tt, 0:NG]))
                sync()
                for tt in range(TT):
                    go(dve.max_index(gidx[:, tt], gtop[:, tt], GL[:, tt, 0:NG]))
                step(dve.tensor_tensor(gexp, GL[:, :, 0:NG], gtop[:, :, 0:1].broadcast_to([P, TT, NG]), ALU.subtract))
                dve.sem_inc(router_in, 1)
                step(dve.tensor_copy(gfl, gidx))
                step(dve.tensor_tensor(gone, gfl[:, :, 0:1].broadcast_to([P, TT, NG]),
                                       iota8.unsqueeze(1).broadcast_to([P, TT, NG]), ALU.is_equal))
                logits = GL[:, :, NG:NG + NE].rearrange("p t (g e) -> p t g e", g=NG)
                step(dve.tensor_tensor(prod, logits, gone.unsqueeze(3).broadcast_to([P, TT, NG, EPG]), ALU.mult))
                step(dve.memset(ig, LOWEST))
                for tt in range(TT):
                    step(dve.tensor_reduce(ig[:, tt, 0:EPG], prod[:, tt].rearrange("p g e -> p e g"), AX, ALU.add))
                for tt in range(TT):
                    go(dve.max(itop[:, tt], ig[:, tt]))
                sync()
                for tt in range(TT):
                    go(dve.max_index(iidx[:, tt], itop[:, tt], ig[:, tt]))
                step(dve.tensor_tensor(d2, itop[:, :, 1:2], itop[:, :, 0:1], ALU.subtract))
                dve.sem_inc(router_in, 1)
                step(dve.tensor_copy(ifl, iidx))
                dve.wait_ge(router_out, 2 * l + 2)
                step(dve.tensor_reduce(sm[:, 0], gexp, AX, ALU.add))
                step(dve.reciprocal(sm[:, 1], sm[:, 0]))
                step(dve.tensor_scalar(sm[:, 2], d2, 1.0, None, ALU.add))
                step(dve.reciprocal(sm[:, 3], sm[:, 2]))
                step(dve.tensor_tensor(sm[:, 4], sm[:, 3], sm[:, 1], ALU.mult))
                step(dve.tensor_tensor(sm[:, 5], sm[:, 4], d2, ALU.mult))
                for k in range(2):
                    step(dve.tensor_tensor(w4[:, k], ifl[:, :, k:k + 1].broadcast_to([P, TT, EPG]),
                                           iota8[:, 0:EPG].unsqueeze(1).broadcast_to([P, TT, EPG]), ALU.is_equal))
                    step(dve.tensor_tensor(w4[:, k], w4[:, k], sm[:, 4 + k].broadcast_to([P, TT, EPG]), ALU.mult))
                step(dve.tensor_tensor(w4[:, 0], w4[:, 0], w4[:, 1], ALU.add))
                for tt in range(TT):
                    step(dve.tensor_tensor(EG[:, tt].rearrange("p (g e) -> p g e", g=NG),
                                           gone[:, tt].unsqueeze(2).broadcast_to([P, NG, EPG]),
                                           w4[:, 0, tt].unsqueeze(1).broadcast_to([P, NG, EPG]), ALU.mult))

                def hidden(i, s):
                    e = i * EXP_RING + (l * NE + s)
                    dve.wait_ge(silu_done, e + 1)
                    dve.wait_ge(up_done, e + 1)
                    dve.tensor_tensor(HH[:, s % 2].rearrange("p j t -> p (j t)"), SG[:, s % 2], PS[:, 2 + s % 2, :],
                                      ALU.mult).then_inc(hidden_ready, 1)

                def gather_out(i, s):
                    e = i * EXP_RING + (l * NE + s)
                    for tt in range(TT):
                        for c in range(2):
                            dve.wait_ge(down_done, e * 4 + (2 * tt + c + 1))
                            part = slice(c * 512, (c + 1) * 512)
                            dve.scalar_tensor_tensor(X[:, tt, part], PS[:, 4 + 2 * tt + c, :],
                                                     EG[:, tt, bass.ds(i * EXP_RING + s, 1)], X[:, tt, part],
                                                     ALU.mult, ALU.add).then_inc(down_added, 1)

                hidden(0, 0)
                for s in range(1, EXP_RING):
                    hidden(0, s)
                    gather_out(0, s - 1)
                with dve.Fori(1, NE // EXP_RING) as i:
                    hidden(i, 0)
                    gather_out(i - 1, EXP_RING - 1)
                    for s in range(1, EXP_RING):
                        hidden(i, s)
                        gather_out(i, s - 1)
                gather_out(NE // EXP_RING - 1, EXP_RING - 1)
                dve.wait_ge(down_added, 4 + 4 * NE * (l + 1))
                dve.sem_inc(layer_done, 1)
            root(TT)
            gained(FINAL, out_ready)


_INS = ["x", "c", "w_ada", "b_ada", "norm1_g", "norm2_g", "w_in", "pool_w", "pool_scale", "q_norm_g", "k_norm_g",
        "attn_sinks", "mix_norm_g", "w_out", "peer_wq", "peer_subkeys", "peer_u", "peer_v", "positions_2",
        "attn_norm_2", "w_in_2", "b_f_2", "q_norm_2", "w_uq_2", "kv_norm_2", "w_ukv_2", "fox_out_norm_2",
        "mla_out_norm_2", "w_o_2", "ffn_norm_2", "w_group_2", "w_router_2", "w_gate_2", "w_up_2", "w_down_2",
        "final_norm_2"]
_OUTS = [((1, 256, 1024), "float32")]


def kernel(**inputs):
    import numpy as _np
    import concourse.bacc as _bacc
    from concourse import mybir as _mybir
    from concourse.bass_utils import run_bass_kernel_spmd as _run

    nc = _bacc.Bacc("TRN2", target_bir_lowering=False, num_devices=1)
    arrays, args = {}, []
    for name in _INS:
        a = _np.ascontiguousarray(inputs[name])
        arrays[f"in_{name}_dram"] = a
        args.append(nc.dram_tensor(f"in_{name}_dram", a.shape, _mybir.dt.from_np(a.dtype), kind="ExternalInput").ap())
    for i, (shape, dtype) in enumerate(_OUTS):
        dt = _mybir.dt.from_np(_np.dtype(dtype))
        args.append(nc.dram_tensor(f"out_{i}_dram", shape, dt, kind="ExternalOutput").ap())
    build(nc, *args)
    r = _run(nc, [arrays], core_ids=[0])
    got = tuple(r.results[0][f"out_{i}_dram"] for i in range(len(_OUTS)))
    return got[0]
```

```python
from contextlib import ExitStack
from math import pi

import concourse.bass as bass
from concourse import mybir

F32 = mybir.dt.float32
BF16 = mybir.dt.bfloat16
I32 = mybir.dt.int32
U32 = mybir.dt.uint32
ALU = mybir.AluOpType
ACT = mybir.ActivationFunctionType
AX = mybir.AxisListType.X

P = 128
D = 1024
KT = D // P
T = 256
TT = T // P
DEPTH = 2
EPS = 1e-6
MASKED = -1e30
LOWEST = -3.0e38

POOL = 512
WINDOWS = (2, 4, 8, 16)
HD = 64
NH = 8
NKV = 2
IN_A = 1280
NKEY = 128
NEXP = NKEY * NKEY
PH = 8
TOPK = 16
SLOTS = PH * TOPK
IN_B = 1960
REST = IN_B - 3 * 512
QL, KVL, ROPE = 256, 128, 32
DK = HD + ROPE
NG, EPG = 8, 4
NE = NG * EPG
DE = 256

CHUNK = 4096
NCHUNK = 4
RING = 4
EXP_F = 3 * KT * DE
EXP_RING = 4
BT = 64
NB = NE
NX = 8
NBX = NB + NX
NBANK = 6


def psum_jobs():
    jobs, order, count = {}, [], {"v": 0, "s": 0}

    def add(name, who):
        jobs[name] = (len(order), len(order) % NBANK, who, count[who])
        order.append(name)
        count[who] += 1

    for l in range(DEPTH):
        for n in range(12):
            add(("ada", l, n), "v" if n // 2 in (1, 4) else "s")
    for l in range(DEPTH):
        for tt in range(TT):
            for half in range(2):
                add(("hT", l, tt, half), "s")
        for c in range(3):
            for tt in range(TT):
                add(("in", l, c, tt), "s")
        for b in range(2):
            add(("pool", l, b), "s")
        for tt in range(TT):
            add(("mix", l, tt), "v")
        for tt in range(TT):
            add(("qT", l, tt), "s")
        add(("kT", l), "s")
        attention_jobs(add, "a", l)
        for tt in range(TT):
            for half in range(2):
                add(("yT", l, tt, half), "s")
        for c in range(2):
            for tt in range(TT):
                add(("out", l, c, tt), "v")
        add(("subT", l), "s")
        for tt in range(TT):
            for half in range(2):
                add(("h2T", l, tt, half), "s")
        for b in range(8):
            add(("wq", l, b), "s")
        for tt in range(TT):
            for b in range(4):
                add(("s", l, tt, b), "s")
    for l in range(DEPTH):
        for tt in range(TT):
            for half in range(2):
                add(("bhT", l, tt, half), "s")
        for b in range(4):
            add(("fqk", l, b), "s")
        for tt in range(TT):
            add(("fv", l, tt), "s")
        for tt in range(TT):
            add(("rest", l, tt), "v")
        for tt in range(TT):
            add(("cT", l, tt), "s")
        for tt in range(TT):
            for c in range(2):
                add(("uq", l, tt, c), "s")
            for c in range(2):
                add(("ukv", l, tt, c), "s")
        attention_jobs(add, "f", l)
        for name in ("qmT", "kmT"):
            for tt in range(TT):
                for b in range(2):
                    add((name, l, tt, b), "s")
        attention_jobs(add, "m", l)
        for tt in range(TT):
            for half in range(2):
                add(("byT", l, tt, half), "s")
        for c in range(2):
            for tt in range(TT):
                add(("bout", l, c, tt), "v")
        for tt in range(TT):
            for half in range(2):
                add(("fhT", l, tt, half), "s")
        for tt in range(TT):
            add(("route", l, tt), "v")
        add(("rank", l), "v")
    return jobs, order


def attention_jobs(add, kind, l):
    for tt in range(TT):
        for b in range(2 * (tt + 1)):
            add((kind + "sc", l, tt, b), "v")
    for tt in range(TT):
        for b in range(2 * (tt + 1)):
            add((kind + "pT", l, tt, b), "s")
        add((kind + "pv", l, tt), "v")


def first_head(b, per):
    return b // 2 * 2 * per + b % 2


def weight_chunks():
    chunks, order, count = {}, [], {"v": 0, "p": 0}

    def add(name, who):
        chunks[name] = (len(order), len(order) % NCHUNK, who, count[who])
        order.append(name)
        count[who] += 1

    for l in range(DEPTH):
        for c in range(3):
            for kp in range(4):
                add(("ada", l, c, kp), "v")
    for l in range(DEPTH):
        for name, n in (("in", 3), ("out", 2), ("wq", 4)):
            for c in range(n):
                add((name, l, c), "p")
    for l in range(DEPTH):
        for name, n in (("bin", 4), ("bout", 2)):
            for c in range(n):
                add((name, l, c), "p")
    return chunks, order


def build(
    nc, x, c, w_ada, b_ada, norm1_g, norm2_g, w_in, pool_w, pool_scale, q_norm_g, k_norm_g,
    attn_sinks, mix_norm_g, w_out, peer_wq, peer_subkeys, peer_u, peer_v, positions_2,
    attn_norm_2, w_in_2, b_f_2, q_norm_2, w_uq_2, kv_norm_2, w_ukv_2, fox_out_norm_2,
    mla_out_norm_2, w_o_2, ffn_norm_2, w_group_2, w_router_2, w_gate_2, w_up_2, w_down_2,
    final_norm_2, out,
):
    J, JORDER = psum_jobs()
    CH, CORDER = weight_chunks()

    with ExitStack() as ctx:
        def sb(name, n, dt=F32):
            return ctx.enter_context(nc.sbuf_tensor(name, [P, n], dt))

        def sem(name):
            return ctx.enter_context(nc.semaphore(name))

        arena = sb("arena", NCHUNK * CHUNK + 12288)
        mod = sb("mod", 12288)
        small = sb("small", 4224)
        X = sb("X", TT * D)[:].rearrange("p (t d) -> p t d", t=TT)
        HR = sb("HR", TT * D)[:].rearrange("p (t d) -> p t d", t=TT)
        HTF = sb("HT", KT * T)[:]
        HT = HTF.rearrange("p (k t) -> p k t", k=KT)
        HTB = [HTF[:, i * KT * BT:(i + 1) * KT * BT].rearrange("p (k t) -> p k t", k=KT) for i in range(2)]
        JKT = sb("JK", 512)
        JUNK = JKT[:].bitcast(BF16)
        TMP = JKT[:]
        IDENT = sb("IDENT", P)[:]
        ONES = sb("ONES", P)[:]
        IDX = sb("IDX", TT * SLOTS, I32)[:].rearrange("p (t s) -> p t s", t=TT)
        GATE = sb("GATE", TT * SLOTS)[:].rearrange("p (t s) -> p t s", t=TT)
        SSQ = sb("SSQ", 32)[:]
        RT = sb("RT", 32)[:]
        RS = sb("RS", 32)[:]
        SV = sb("SV", 6 * 16)[:].rearrange("p (a t h) -> p a t h", a=6, t=TT)
        MX, NM, DEN, RD, SE, EXS = (SV[:, i] for i in range(6))
        SINK = sb("SINK", NH)[:]
        COND = sb("COND", KT)[:]
        EPST = sb("EPST", 1)[:]
        IOTA = sb("IOTA", TOPK)[:]
        COS = sb("COS", TT * 16)[:].rearrange("p (t f) -> p t f", t=TT)
        SIN = sb("SIN", TT * 16)[:].rearrange("p (t f) -> p t f", t=TT)
        STAGE = sb("STAGE", RING, I32)[:]
        DOT = sb("DOT", RING)[:]
        ACTV = sb("ACTV", RING)[:]
        SLOT = sb("SLOT", BT)[:]
        PLAN = sb("PLAN", 16, I32)[:]
        RW = sb("RW", 64)[:]

        def view(buf, at, pattern, **kw):
            n = 1
            for v in kw.pop("shape"):
                n *= v
            return buf[:, at:at + n].rearrange(pattern, **kw)

        G0 = NCHUNK * CHUNK
        ring = [arena[:, s * CHUNK:(s + 1) * CHUNK] for s in range(NCHUNK)]

        def g3(at, a, b, buf=arena, base=G0):
            return buf[:, base + at:base + at + a * b].rearrange("p (a b) -> p a b", a=a)

        NGAIN = g3(0, 4, D)
        PROJ = g3(0, TT, IN_A)
        KD = arena[:, G0 + 2560:G0 + 3072].rearrange("p (t k u d) -> p t k u d", t=TT, k=NKV, u=2)
        QT = g3(3072, 4, T)
        KTA = g3(4096, NKV, T)
        S_A = [g3(4608, NH, P), g3(5632, NH, T)]
        PT_A = arena[:, G0 + 7680:G0 + 9728].rearrange("p (k h q) -> p k h q", k=2, h=NH)
        POOLT = g3(7680, 4, T)
        QSQ = arena[:, G0 + 5632:G0 + 6912]
        MIXG = arena[:, G0 + 10240:G0 + 11264]
        PSC = arena[:, G0 + 11264:G0 + 11776]
        SUBK = g3(11776, 2, NKEY)
        SUBT = g3(12032, 2, NKEY)
        QTP = g3(0, 16, T)
        SS = arena[:, G0 + 4096:G0 + 8192].rearrange("p (t a n) -> p t a n", t=TT, a=16)
        CAND = g3(8192, PH, 256)
        OH = arena[:, G0:G0 + 2048].rearrange("p (h k c) -> p h k c", h=PH, k=TOPK)
        V16 = g3(10240, 16, TOPK)
        I16 = g3(10496, 16, TOPK).bitcast(U32)
        F16 = g3(10752, 16, TOPK)
        BV = g3(11008, PH, TOPK)
        BI = g3(11136, PH, TOPK).bitcast(U32)
        BU = g3(11264, PH, TOPK).bitcast(U32)
        BF = g3(11392, PH, TOPK)
        E1 = g3(11520, PH, TOPK)
        E2 = g3(11648, PH, TOPK)
        GU = g3(0, RING, D)
        GV = g3(4096, RING, D)
        DIAG = g3(8192, RING, P)
        MODL = [mod[:, l * 6144:(l + 1) * 6144] for l in range(DEPTH)]

        def mrow(l, i):
            return MODL[l][:, i * D:(i + 1) * D]

        BIAS = small[:, 0:2048].rearrange("p (h s) -> p h s", h=NH)
        MT = small[:, 2048:3584].rearrange("p (g t) -> p g t", g=4)
        POOLW = small[:, 3584:4096].rearrange("p (g d) -> p g d", g=4)
        QKG = small[:, 4096:4224]
        UQ = small[:, 0:1536].rearrange("p (k n) -> p k n", k=2)
        UKV = small[:, 1536:2560]
        FN = small[:, 2560:3584]
        ON = mod[:, 0:1024]
        FINAL = mod[:, 1024:2048]
        QG = mod[:, 2048:2304]
        KG = mod[:, 2304:2432]
        BFB = mod[:, 2432:2440]
        GR = mod[:, 2440:2760].rearrange("p (k n) -> p k n", k=KT)
        FQT = g3(2760, 4, T, mod, 0)
        FKT = g3(3784, 4, T, mod, 0)
        FV = g3(4808, TT, 512, mod, 0)
        R = g3(5832, TT, REST, mod, 0)
        CT = g3(6680, 3, T, mod, 0)
        QM = mod[:, 7448:8984].rearrange("p (t h d) -> p t h d", t=TT, h=NH)
        KM = mod[:, 8984:10520].rearrange("p (t h d) -> p t h d", t=TT, h=NH)
        UTRI = g3(10520, TT, T, mod, 0)
        CMASK = mod[:, 11032:11288]
        RTMP = mod[:, 11288:12288]
        YO = g3(7448, 2, D, mod, 0)
        SG = g3(9496, 2, P, mod, 0)
        HH = mod[:, 9752:10008].rearrange("p (b j t) -> p b j t", b=2, j=2)
        SEL = mod[:, 10008:10264].rearrange("p (b t s) -> p b t s", b=2, t=TT)
        EQ = mod[:, 10264:10520].rearrange("p (t k s) -> p t k s", t=TT, k=2)
        YG = g3(8192, 2 * TT, D)
        ENUM = RW[:, 16:48]
        GK = RW[:, 4:8].rearrange("p (t k) -> p t k", t=TT)
        DREL = RW[:, 8:12].rearrange("p (t k) -> p t k", t=TT)
        DESTI = RW[:, 12:16].bitcast(I32)
        KV = arena[:, G0:G0 + 2048].rearrange("p (t h d) -> p t h d", t=TT, h=NH)
        QMT = g3(2048, NH, T)
        LFB = arena[:, G0 + 2048:G0 + 4096].rearrange("p (t h q) -> p t h q", t=TT, h=NH)
        KMT = g3(4096, NH, T)
        S_B = [g3(6144, NH, P), g3(7168, NH, T)]
        PT_B = arena[:, G0 + 9216:G0 + 11264].rearrange("p (k h q) -> p k h q", k=2, h=NH)
        SQB = arena[:, G0 + 7168:G0 + 9216]
        AN = arena[:, G0 + 11264:G0 + 12288]
        ONEHOT = RTMP[:, 500:628].rearrange("p (k t e) -> p k t e", k=2, t=TT)
        PICKS = RTMP[:, 630:694].rearrange("p (t e) -> p t e", t=TT)
        WG = [arena[:, s * EXP_F:s * EXP_F + 2048].rearrange("p (k f) -> p k f", k=KT) for s in range(EXP_RING)]
        WU = [arena[:, s * EXP_F + 2048:s * EXP_F + 4096].rearrange("p (k f) -> p k f", k=KT) for s in range(EXP_RING)]
        WD = [arena[:, s * EXP_F + 4096:s * EXP_F + 6144].rearrange("p (j d) -> p j d", j=2) for s in range(EXP_RING)]

        PS = ctx.enter_context(nc.psum_tensor("PS", [P, 8, 512], F32))
        PO = PS[:, NBANK:NBANK + 2, :]

        psum_ready = sem("psum_ready")
        evac = {"v": sem("evac_by_vector"), "s": sem("evac_by_scalar")}
        vector_step = sem("vector_step")
        scalar_step = sem("scalar_step")
        pool_step = sem("pool_step")
        x_loaded = sem("x_loaded")
        cond_loaded = sem("cond_loaded")
        cond_ready = sem("cond_ready")
        gains_loaded = sem("gains_loaded")
        rows_cleared = sem("rows_cleared")
        bada_loaded = sem("bada_loaded")
        consts_ready = sem("consts_ready")
        acc_zeroed = sem("acc_zeroed")
        acc_ready = sem("acc_ready")
        params_loaded = sem("params_loaded")
        chunk_loaded = [sem(f"chunk_loaded{i}") for i in range(NCHUNK)]
        chunk_used = {"v": sem("chunk_used_by_vector"), "p": sem("chunk_used_by_tensor")}
        squares_ready = sem("squares_ready")
        root_ready = sem("root_ready")
        rows_ready = sem("rows_ready")
        qk_ready = sem("qk_ready")
        negmax_ready = sem("negmax_ready")
        probs_ready = sem("probs_ready")
        idx_ready = sem("idx_ready")
        gexp_in = sem("gexp_in")
        gexp_out = sem("gexp_out")
        staged = sem("staged")
        stage_seen = sem("stage_seen")
        u_loaded = [sem(f"u_loaded{i}") for i in range(RING)]
        v_loaded = [sem(f"v_loaded{i}") for i in range(RING)]
        dot_ready = sem("dot_ready")
        gelu_ready = sem("gelu_ready")
        diag_ready = sem("diag_ready")
        expert_added = sem("expert_added")
        sums_read = sem("sums_read")
        layer_done = sem("layer_done")
        logsig_in = sem("logsig_in")
        logsig_out = sem("logsig_out")
        decay_ready = sem("decay_ready")
        cn_ready = sem("cn_ready")
        mla_ready = sem("mla_ready")
        trig_in = sem("trig_in")
        trig_out = sem("trig_out")
        pos_loaded = sem("pos_loaded")
        expert_loaded = [sem(f"expert_loaded{i}") for i in range(EXP_RING)]
        sel_step = sem("sel_step")
        sel_ready = sem("sel_ready")
        picked = sem("picked")
        picked_out = sem("picked_out")
        gate_up_done = sem("gate_up_done")
        silu_done = sem("silu_done")
        hidden_ready = sem("hidden_ready")
        down_done = sem("down_done")
        y_out = sem("y_out")
        y_seen = sem("y_seen")
        y_stored = [sem(f"y_stored{i}") for i in range(2)]
        extra_stored = [[sem(f"extra_stored{l}{i}") for i in range(2)] for l in range(DEPTH)]
        plan_step = sem("plan_step")
        plan_ready = sem("plan_ready")
        y_gathered = sem("y_gathered")
        onehot_ready = sem("onehot_ready")
        router_in = sem("router_in")
        router_out = sem("router_out")
        out_ready = sem("out_ready")
        stored = sem("stored")

        def bank(name):
            return PS[:, J[name][1], :]

        def arrived(eng, name):
            eng.wait_ge(psum_ready, J[name][0] + 1)

        def taken(eng, name):
            eng.wait_ge(evac[J[name][2]], J[name][3] + 1)

        def loaded(eng, name):
            n, slot = CH[name][:2]
            eng.wait_ge(chunk_loaded[slot], 16 * (n // NCHUNK + 1))

        def row(ap, n):
            return ap.partition_broadcast(n)

        def if_extra(eng, l, extra, none):
            eng.wait_ge(plan_ready, 2 * l + 1)
            n = eng.value_load(PLAN[0:1, NX:NX + 1], min_val=0, max_val=NX)
            with eng.If(n > 0):
                extra()
            with eng.Else():
                none()

        def blocks(eng, l, body, flush, extra_counts):
            def run(first, count):
                body(first, 0, True)
                for s in range(1, EXP_RING):
                    body(first, s, False)
                if count > 2:
                    with eng.Fori(first + 1, first + count) as i:
                        for s in range(EXP_RING):
                            body(i, s, False)
                else:
                    for s in range(EXP_RING):
                        body(first + 1, s, False)
                flush(first + count - 1, EXP_RING - 1)

            def none():
                for which, each in extra_counts:
                    eng.wait_ge(which, each * (l * NBX + NB))
                    eng.sem_inc(which, each * NX)

            run(0, NB // EXP_RING)
            if_extra(eng, l, lambda: run(NB // EXP_RING, NX // EXP_RING), none)

        def before(i, s):
            return (i, s - 1) if s else (i - 1, EXP_RING - 1)

        Y = nc.dram_tensor("expert_rows", [NBX * BT, D], F32, kind="Internal").ap()

        block = ctx.enter_context(nc.Block())

        @block.sync
        def _(sp):
            def source(name):
                kind, l, c = name[:3]
                if kind == "ada":
                    return w_ada[l, name[3] * 256:(name[3] + 1) * 256, c * 2048:(c + 1) * 2048]
                w = {"in": w_in, "out": w_out, "wq": peer_wq, "bin": w_in_2, "bout": w_o_2}[kind]
                return w[l, :, c * 512:min((c + 1) * 512, w.shape[2])]

            sp.dma_start(X, x[0].rearrange("(t p) d -> p t d", p=P)).then_inc(x_loaded, 16)
            for n, name in enumerate(CORDER):
                if n >= NCHUNK:
                    _, _, who, nth = CH[CORDER[n - NCHUNK]]
                    sp.wait_ge(chunk_used[who], nth + 1)
                if name[0] == "bin" and name[2] == 0 and name[1] > 0:
                    sp.wait_ge(down_done, NBX * name[1])
                src = source(name).rearrange("(k p) n -> p k n", p=P)
                dst = ring[n % NCHUNK][:, 0:src.shape[1] * src.shape[2]].rearrange("p (k n) -> p k n", k=src.shape[1])
                sp.dma_start(dst, src).then_inc(chunk_loaded[n % NCHUNK], 16)
                if name[0] == "bout" and name[2] == 1:
                    l = name[1]
                    sp.wait_ge(chunk_used["p"], CH[name][3] + 1)
                    arrived(sp, ("fhT", l, 0, 0))
                    wg = w_gate_2.rearrange("l e (p k) f -> (l e) p (k f)", k=KT)
                    wu = w_up_2.rearrange("l e (p k) f -> (l e) p (k f)", k=KT)
                    wd = w_down_2.rearrange("l e (j p) d -> (l e) p j d", p=P)

                    def expert(e, s):
                        flat = arena[:, s * EXP_F:(s + 1) * EXP_F]
                        sp.dma_start(flat[:, 0:2048], wg[bass.ds(e, 1)][0]).then_inc(expert_loaded[s], 16)
                        sp.dma_start(flat[:, 2048:4096], wu[bass.ds(e, 1)][0]).then_inc(expert_loaded[s], 16)
                        sp.dma_start(WD[s], wd[bass.ds(e, 1)][0]).then_inc(expert_loaded[s], 16)

                    for s in range(EXP_RING):
                        expert(l * NE + s, s)
                    with sp.Fori(1, NB // EXP_RING) as i:
                        for s in range(EXP_RING):
                            sp.wait_ge(down_done, i * EXP_RING + (l * NBX + s - EXP_RING + 1))
                            expert(i * EXP_RING + (l * NE + s), s)

                    def extra():
                        for x in range(NX):
                            e = sp.value_load(PLAN[0:1, x:x + 1], min_val=0, max_val=NE - 1)
                            sp.wait_ge(down_done, l * NBX + NB + x - EXP_RING + 1)
                            expert(e + l * NE, x % EXP_RING)

                    def none():
                        for s in range(EXP_RING):
                            sp.wait_ge(expert_loaded[s], 48 * (l * NBX + NB) // EXP_RING)
                            sp.sem_inc(expert_loaded[s], 48 * NX // EXP_RING)

                    if_extra(sp, l, extra, none)
            sp.wait_ge(out_ready, 2)
            sp.dma_start(out[0].rearrange("(t p) d -> p t d", p=P), HR).then_inc(stored, 16)
            sp.wait_ge(stored, 16)

        @block.gpsimd
        def _(pool):
            steps = [0]

            def go(ins):
                steps[0] += 1
                ins.then_inc(pool_step, 1)

            def sync():
                pool.wait_ge(pool_step, steps[0])

            def params(src_dst):
                for dst, src in src_dst:
                    pool.dma_start(dst, src).then_inc(params_loaded, 16)

            with nc.allow_non_contiguous_dma(reason="small parameter vectors"):
                pool.dma_start(COND, c[0].rearrange("(k p) -> p k", p=P)).then_inc(cond_loaded, 16)
                pool.dma_start(RW[:, 0:TT].bitcast(I32), positions_2[0].rearrange("(t p) -> p t", p=P)).then_inc(pos_loaded, 16)
            for l in range(DEPTH):
                pool.dma_start(NGAIN[:, 2 * l], row(norm1_g[l], P)).then_inc(gains_loaded, 16)
                pool.dma_start(NGAIN[:, 2 * l + 1], row(norm2_g[l], P)).then_inc(gains_loaded, 16)
            go(pool.memset(mod[:], 0.0))
            sync()
            pool.dma_start(Y[NB * BT:NBX * BT].rearrange("(p r) d -> p (r d)", p=P), mod[:, 0:NX * BT // P * D]).then_inc(rows_cleared, 16)
            pool.wait_ge(rows_cleared, 16)
            for l in range(DEPTH):
                pool.dma_start(MODL[l][0:1, :], b_ada[l:l + 1, :]).then_inc(bada_loaded, 16)
            go(pool.memset(IDENT, 0.0))
            go(pool.memset(ONES, 1.0))
            go(pool.memset(EPST, EPS))
            go(pool.iota(IOTA, [[1, TOPK]], base=0, channel_multiplier=0, allow_small_or_imprecise_dtypes=True))
            go(pool.iota(BIAS, [[0, NH], [-1, 2 * P]], base=P, channel_multiplier=1, allow_small_or_imprecise_dtypes=True))
            sync()
            go(pool.affine_select(out=IDENT, in_=IDENT, compare_op=ALU.not_equal, fill=1.0, base=0,
                                  pattern=[[-1, P]], channel_multiplier=1))
            for h in range(NH):
                go(pool.tensor_scalar(BIAS[:, h], BIAS[:, h], -(2.0 ** (-8.0 * (h + 1) / NH)), None, ALU.mult))
            sync()
            go(pool.affine_select(out=BIAS, in_=BIAS, compare_op=ALU.is_ge, fill=MASKED, base=P,
                                  pattern=[[0, NH], [-1, 2 * P]], channel_multiplier=1))
            sync()
            go(pool.affine_select(out=BIAS, in_=BIAS, compare_op=ALU.is_ge, fill=MASKED, base=-1,
                                  pattern=[[0, NH], [1, 2 * P]], channel_multiplier=-1))
            for g, w in enumerate(WINDOWS):
                go(pool.memset(MT[:, g], 1.0 / w))
            sync()
            for g, w in enumerate(WINDOWS):
                for t in range(w - 1):
                    go(pool.memset(MT[:, g, t:t + 1], 1.0 / (t + 1)))
            sync()
            for part in (slice(0, T), slice(T, T + P)):
                n = part.stop - part.start
                go(pool.affine_select(out=MT[:, :, part], in_=MT[:, :, part], compare_op=ALU.is_ge, fill=0.0, base=0,
                                      pattern=[[0, 4], [1, n]], channel_multiplier=-1))
            sync()
            for part in (slice(0, T), slice(T, T + P)):
                n = part.stop - part.start
                for g, w in enumerate(WINDOWS):
                    go(pool.affine_select(out=MT[:, g, part], in_=MT[:, g, part], compare_op=ALU.is_ge, fill=0.0,
                                          base=w - 1, pattern=[[-1, n]], channel_multiplier=1))
            sync()
            for g in range(4):
                for at in (0, T):
                    go(pool.tensor_tensor(MT[:, g, at:at + P], MT[:, g, at:at + P], IDENT, ALU.subtract))
            sync()
            pool.sem_inc(consts_ready, 1)

            u_rows = peer_u.rearrange("l n d -> (l n) d")
            v_rows = peer_v.rearrange("l n d -> (l n) d")
            for l in range(DEPTH):
                if l:
                    pool.wait_ge(layer_done, l)
                with nc.allow_non_contiguous_dma(reason="small parameter vectors"):
                    params([
                        (QKG[:, 0:HD], row(q_norm_g[l], P)), (QKG[:, HD:2 * HD], row(k_norm_g[l], P)),
                        (SINK, row(attn_sinks[l], P)), (MIXG, row(mix_norm_g[l], P)), (PSC, row(pool_scale[l], P)),
                        (POOLW, pool_w[l].rearrange("g c d -> c g d")),
                        (SUBK, peer_subkeys[l].rearrange("q n d -> n q d")),
                    ])
                for tt in range(TT):
                    pool.wait_ge(idx_ready, l * TT + TT)
                    base = (l * TT + tt) * SLOTS

                    def gather(i, s):
                        pool.wait_ge(u_loaded[s], i * 16 + (base // RING) * 16) if (base or not isinstance(i, int)) else None
                        pool.wait_ge(v_loaded[s], i * 16 + (base // RING) * 16) if (base or not isinstance(i, int)) else None
                        pool.wait_ge(dot_ready, i * RING + (base + s + 1))
                        pool.wait_ge(expert_added, i * RING + (base + s + 1))
                        pool.tensor_copy(STAGE[:, s:s + 1], IDX[:, tt, bass.ds(i * RING + s, 1)]).then_inc(staged, 1)
                        pool.wait_ge(staged, i * RING + (base + s + 1))
                        pool.sem_inc(stage_seen, 1)
                        off = bass.IndirectOffsetOnAxis(ap=STAGE[:, s:s + 1], axis=0)
                        pool.indirect_dma_start(out=GU[:, s, :], out_offset=None, in_=u_rows, in_offset=off).then_inc(u_loaded[s], 16)
                        pool.indirect_dma_start(out=GV[:, s, :], out_offset=None, in_=v_rows, in_offset=off).then_inc(v_loaded[s], 16)

                    for s in range(RING):
                        gather(0, s)
                    with pool.Fori(1, SLOTS // RING) as i:
                        for s in range(RING):
                            gather(i, s)

            for l in range(DEPTH):
                pool.wait_ge(layer_done, DEPTH + l)
                with nc.allow_non_contiguous_dma(reason="small parameter vectors"):
                    if l == 0:
                        params([(FINAL, row(final_norm_2, P))])
                    params([
                        (AN, row(attn_norm_2[l], P)), (FN, row(ffn_norm_2[l], P)),
                        (BFB, row(b_f_2[l], P)), (QG, row(q_norm_2[l], P)), (KG, row(kv_norm_2[l], P)),
                        (ON[:, 0:512], row(fox_out_norm_2[l], P)), (ON[:, 512:1024], row(mla_out_norm_2[l], P)),
                        (UQ, w_uq_2[l].rearrange("(k p) n -> p k n", p=P)), (UKV, w_ukv_2[l]),
                        (GR[:, :, 0:NG], w_group_2[l].rearrange("(p k) n -> p k n", k=KT)),
                        (GR[:, :, NG:NG + NE], w_router_2[l].rearrange("(p k) n -> p k n", k=KT)),
                    ])
                if l == 0:
                    go(pool.memset(UTRI, 1.0))
                    go(pool.memset(CMASK, 0.0))
                    go(pool.iota(SLOT, [[1, BT]], base=0, channel_multiplier=0, allow_small_or_imprecise_dtypes=True))
                    go(pool.iota(ENUM, [[1, NE]], base=0, channel_multiplier=0, allow_small_or_imprecise_dtypes=True))
                    go(pool.iota(RW[:, 48:56], [[1, 8]], base=0, channel_multiplier=0, allow_small_or_imprecise_dtypes=True))
                    sync()
                    go(pool.affine_select(out=UTRI, in_=UTRI, compare_op=ALU.is_ge, fill=0.0, base=0,
                                          pattern=[[-P, TT], [1, T]], channel_multiplier=-1))
                    go(pool.affine_select(out=CMASK[:, P:2 * P], in_=CMASK[:, P:2 * P], compare_op=ALU.is_ge,
                                          fill=MASKED, base=0, pattern=[[-1, P]], channel_multiplier=1))
                    sync()
                    pool.sem_inc(consts_ready, 1)

                def store(i, s, done):
                    b = i * EXP_RING + s
                    pool.wait_ge(y_out, b + l * NBX + 1)
                    pool.sem_inc(y_seen, 1)
                    pool.dma_start(Y[bass.ds(b * BT, BT)], YO[0:BT, s % 2]).then_inc(done[s % 2], 16)

                def extra():
                    for b in range(NX):
                        store((NB + b) // EXP_RING, b % EXP_RING, extra_stored[l])
                    for k in range(2):
                        pool.wait_ge(extra_stored[l][k], 16 * NX // 2)

                with pool.Fori(0, NB // EXP_RING) as i:
                    for s in range(EXP_RING):
                        store(i, s, y_stored)
                if_extra(pool, l, extra, lambda: None)
                for k in range(2):
                    pool.wait_ge(y_stored[k], 16 * (l + 1) * NB // 2)
                pool.wait_ge(plan_ready, 2 * l + 2)
                for n in range(2 * TT):
                    pool.indirect_dma_start(out=YG[:, n, :], out_offset=None, in_=Y,
                                            in_offset=bass.IndirectOffsetOnAxis(ap=DESTI[:, n:n + 1], axis=0)).then_inc(y_gathered, 16)

        @block.scalar
        def _(act):
            steps = [0]
            roots = [0]
            maxes = [0]

            def go(ins):
                steps[0] += 1
                ins.then_inc(scalar_step, 1)

            def sync():
                act.wait_ge(scalar_step, steps[0])

            def copy_out(name, dst, src):
                arrived(act, name)
                act.activation(dst, src, ACT.Copy).then_inc(evac["s"], 1)

            def root(parts, of_x=False):
                roots[0] += 1
                act.wait_ge(squares_ready, roots[0])
                if of_x:
                    for tt in range(TT):
                        go(act.activation(JUNK, X[:, tt], ACT.Square, accum_out=SSQ[:, tt:tt + 1]))
                        sync()
                for a, b, n in parts:
                    last = act.activation(RT[:, a:b], SSQ[:, a:b], ACT.Sqrt, bias=EPST, scale=1.0 / n)
                    if b != parts[-1][1]:
                        go(last)
                        sync()
                last.then_inc(root_ready, 1)

            def exps(S, sink):
                for tt in range(TT):
                    maxes[0] += 1
                    act.wait_ge(negmax_ready, maxes[0])
                    for h in range(NH):
                        act.activation(S[tt][:, h, :], S[tt][:, h, :], ACT.Exp, bias=NM[:, tt, h:h + 1],
                                       accum_out=DEN[:, tt, h:h + 1]).then_inc(probs_ready, 1)
                    if sink:
                        act.activation(EXS[:, tt], SE[:, tt], ACT.Exp).then_inc(probs_ready, 1)

            def transposed_probs(kind, l, PTX):
                for tt in range(TT):
                    for b in range(2 * (tt + 1)):
                        kt, h = divmod(4 * b, NH)
                        copy_out((kind + "pT", l, tt, b), PTX[:, kt, h:h + 4, :],
                                 bank((kind + "pT", l, tt, b)).rearrange("p (h q) -> p h q", h=4))

            def rows_transposed(kind, l):
                for tt in range(TT):
                    for half in range(2):
                        copy_out((kind, l, tt, half), HT[:, 4 * half:4 * half + 4, tt * P:(tt + 1) * P],
                                 bank((kind, l, tt, half)).rearrange("p (k t) -> p k t", k=4))

            act.wait_ge(cond_loaded, 16)
            act.activation(COND, COND, ACT.Silu).then_inc(cond_ready, 1)
            for n, table in enumerate((SIN, COS)):
                act.wait_ge(trig_in, n + 1)
                act.activation(table, table, ACT.Sin).then_inc(trig_out, 1)
            for l in range(DEPTH):
                for n in range(12):
                    if J[("ada", l, n)][2] == "s":
                        copy_out(("ada", l, n), MODL[l][:, n * 512:(n + 1) * 512], bank(("ada", l, n)))

            for l in range(DEPTH):
                root([(0, TT, D)], of_x=True)
                rows_transposed("hT", l)
                for c in range(3):
                    n = min(512, IN_A - c * 512)
                    for tt in range(TT):
                        copy_out(("in", l, c, tt), PROJ[:, tt, c * 512:c * 512 + n], bank(("in", l, c, tt))[:, 0:n])
                for b in range(2):
                    copy_out(("pool", l, b), POOLT[:, 2 * b:2 * b + 2, :],
                             bank(("pool", l, b)).rearrange("p (g t) -> p g t", g=2))
                root([(0, 20, HD)])
                for tt in range(TT):
                    copy_out(("qT", l, tt), QT[:, :, tt * P:(tt + 1) * P],
                             bank(("qT", l, tt)).rearrange("p (k t) -> p k t", k=4))
                copy_out(("kT", l), KTA, bank(("kT", l)).rearrange("p (k t) -> p k t", k=NKV))
                exps(S_A, True)
                transposed_probs("a", l, PT_A)
                root([(0, 4, 512)])
                rows_transposed("yT", l)
                copy_out(("subT", l), SUBT, bank(("subT", l))[:, 0:256].rearrange("p (k t) -> p k t", k=2))
                root([(0, TT, D)], of_x=True)
                rows_transposed("h2T", l)
                for b in range(8):
                    copy_out(("wq", l, b), QTP[:, 2 * b:2 * b + 2, :],
                             bank(("wq", l, b)).rearrange("p (g t) -> p g t", g=2))
                for tt in range(TT):
                    for b in range(4):
                        copy_out(("s", l, tt, b), SS[:, tt, 4 * b:4 * b + 4, :],
                                 bank(("s", l, tt, b)).rearrange("p (g t) -> p g t", g=4))
                for tt in range(TT):
                    act.wait_ge(gexp_in, l * TT + tt + 1)
                    act.activation(GATE[:, tt], GATE[:, tt], ACT.Exp).then_inc(gexp_out, 1)
                for tt in range(TT):
                    base = (l * TT + tt) * SLOTS
                    with act.Fori(0, SLOTS // RING) as i:
                        for s in range(RING):
                            act.wait_ge(dot_ready, i * RING + (base + s + 1 + RING))
                            act.activation(ACTV[:, s:s + 1], DOT[:, s:s + 1], ACT.Gelu).then_inc(gelu_ready, 1)

            for l in range(DEPTH):
                root([(0, TT, D)], of_x=True)
                rows_transposed("bhT", l)
                for b in range(4):
                    dst = (FQT, FKT)[b // 2]
                    copy_out(("fqk", l, b), dst[:, 2 * (b % 2):2 * (b % 2) + 2, :],
                             bank(("fqk", l, b)).rearrange("p (g t) -> p g t", g=2))
                for tt in range(TT):
                    copy_out(("fv", l, tt), FV[:, tt], bank(("fv", l, tt)))
                act.wait_ge(logsig_in, l + 1)
                z = RTMP[:, 16:32]
                go(act.activation(z, z, ACT.Exp, scale=-1.0))
                sync()
                act.activation(z, z, ACT.Ln, bias=ONES[:, 0:1]).then_inc(logsig_out, 1)
                root([(0, 2, QL), (2, 4, KVL)])
                for tt in range(TT):
                    copy_out(("cT", l, tt), CT[:, :, tt * P:(tt + 1) * P],
                             bank(("cT", l, tt))[:, 0:384].rearrange("p (k t) -> p k t", k=3))
                for tt in range(TT):
                    q = QM[:, tt].rearrange("p h d -> p (h d)")
                    kv = KV[:, tt].rearrange("p h d -> p (h d)")
                    for c in range(2):
                        n = min(512, 768 - 512 * c)
                        copy_out(("uq", l, tt, c), q[:, 512 * c:512 * c + n], bank(("uq", l, tt, c))[:, 0:n])
                    for c in range(2):
                        copy_out(("ukv", l, tt, c), kv[:, 512 * c:512 * c + 512], bank(("ukv", l, tt, c)))
                exps(S_B, False)
                transposed_probs("f", l, PT_B)
                for name, dst in (("qmT", QMT), ("kmT", KMT)):
                    for tt in range(TT):
                        for b in range(2):
                            copy_out((name, l, tt, b), dst[0:DK, 4 * b:4 * b + 4, tt * P:(tt + 1) * P],
                                     bank((name, l, tt, b))[0:DK].rearrange("p (g t) -> p g t", g=4))
                exps(S_B, False)
                transposed_probs("m", l, PT_B)
                root([(0, 32, HD)])
                rows_transposed("byT", l)
                root([(0, TT, D)], of_x=True)
                rows_transposed("fhT", l)
                for n in range(2):
                    act.wait_ge(router_in, 2 * l + n + 1)
                    z = RTMP[:, 100:116] if n == 0 else RTMP[:, 200:202]
                    act.activation(z, z, ACT.Exp).then_inc(router_out, 1)

                def silu(i, s):
                    b = i * EXP_RING + (l * NBX + s)
                    act.wait_ge(gate_up_done, b + 1)
                    act.activation(SG[:, s % 2], PS[:, 2 + s % 2, 0:P], ACT.Silu).then_inc(silu_done, 1)

                def body(i, s, first):
                    b = i * EXP_RING + (l * NBX + s)
                    if not first:
                        silu(*before(i, s))
                    act.wait_ge(picked, b + 1)
                    act.activation(HTB[s % 2].rearrange("p k t -> p (k t)"), PS[:, s % 2, :], ACT.Copy).then_inc(picked_out, 1)

                blocks(act, l, body, silu, [(picked_out, 1), (silu_done, 1)])
            root([(0, TT, D)], of_x=True)

        @block.tensor
        def _(pe):
            rows = [0]
            probs = [0]

            def begin(name):
                n = J[name][0]
                if n >= NBANK:
                    taken(pe, JORDER[n - NBANK])

            def transpose_rows(kind, l):
                rows[0] += 1
                for tt in range(TT):
                    pe.wait_ge(rows_ready, 4 * (rows[0] - 1) + 2 * (tt + 1))
                    for half in range(2):
                        begin((kind, l, tt, half))
                        for k in range(4):
                            kk = 4 * half + k
                            last = pe.transpose(bank((kind, l, tt, half))[:, k * P:(k + 1) * P],
                                                HR[:, tt, kk * P:(kk + 1) * P], IDENT)
                        last.then_inc(psum_ready, 1)

            def project(job, l, wname, c, n, order=range(TT)):
                loaded(pe, (wname, l, c))
                w = ring[CH[(wname, l, c)][1]][:, 0:KT * n].rearrange("p (k n) -> p k n", k=KT)
                for tt in order:
                    name = job(tt)
                    begin(name)
                    for k in range(KT):
                        last = pe.matmul(bank(name)[:, 0:n], HT[:, k, tt * P:(tt + 1) * P], w[:, k, :],
                                         start=(k == 0), stop=(k == KT - 1))
                    last.then_inc(psum_ready, 1)

            def release():
                pe.sem_inc(chunk_used["p"], 1)

            def weights_first(name, l, wname, c, cols, first, final):
                if first:
                    loaded(pe, (wname, l, c))
                w = ring[CH[(wname, l, c)][1]][:, :].rearrange("p (k n) -> p k n", k=KT)
                begin(name)
                for j in range(2):
                    at = cols + j * P
                    for k in range(KT):
                        last = pe.matmul(bank(name)[:, j * T:(j + 1) * T], w[:, k, at:at + P], HT[:, k, :],
                                         start=(k == 0), stop=(k == KT - 1))
                last.then_inc(psum_ready, 1)

            def attend(kind, l, S, PTX, score, value, sink):
                for tt in range(TT):
                    nk = (tt + 1) * P
                    per = 512 // nk
                    for b in range(NH // per):
                        name = (kind + "sc", l, tt, b)
                        begin(name)
                        for j in range(per):
                            h = first_head(b, per) + 2 * j
                            last = score(bank(name)[:, j * nk:(j + 1) * nk], h, tt, nk)
                        last.then_inc(psum_ready, 1)
                for tt in range(TT):
                    probs[0] += NH + sink
                    pe.wait_ge(probs_ready, probs[0])
                    for b in range(2 * (tt + 1)):
                        name = (kind + "pT", l, tt, b)
                        begin(name)
                        kt, h = divmod(4 * b, NH)
                        for j in range(4):
                            last = pe.transpose(bank(name)[:, j * P:(j + 1) * P],
                                                S[tt][:, h + j, kt * P:(kt + 1) * P], IDENT)
                        last.then_inc(psum_ready, 1)
                    begin((kind + "pv", l, tt))
                    taken(pe, (kind + "pT", l, tt, 2 * (tt + 1) - 1))
                    for h in range(NH):
                        for kt in range(tt + 1):
                            last = pe.matmul(bank((kind + "pv", l, tt))[:, h * HD:(h + 1) * HD], PTX[:, kt, h, :],
                                             value(kt, h), start=(kt == 0), stop=(kt == tt))
                    last.then_inc(psum_ready, 1)

            pe.sem_inc(expert_added, RING)
            pe.wait_ge(consts_ready, 1)
            for l in range(DEPTH):
                pe.wait_ge(acc_ready, l + 1)
                for n in range(12):
                    begin(("ada", l, n))
                    pe.matmul(bank(("ada", l, n)), ONES, MODL[l][:, n * 512:(n + 1) * 512],
                              start=True, stop=True).then_inc(psum_ready, 1)

            for l in range(DEPTH):
                transpose_rows("hT", l)
                taken(pe, ("hT", l, 1, 1))
                for c in range(3):
                    project(lambda tt: ("in", l, c, tt), l, "in", c, min(512, IN_A - 512 * c))
                    arrived(pe, ("in", l, c, 1))
                    release()
                pe.wait_ge(params_loaded, 16 * 7 * (l + 1))
                taken(pe, ("in", l, 0, 1))
                for b in range(2):
                    begin(("pool", l, b))
                    for j in range(2):
                        g = 2 * b + j
                        to = bank(("pool", l, b))[:, j * T:(j + 1) * T]
                        pe.matmul(to, PROJ[:, 0, g * P:(g + 1) * P], MT[:, g, 0:T], start=True, stop=False)
                        last = pe.matmul(to[:, P:T], PROJ[:, 1, g * P:(g + 1) * P], MT[:, g, T:T + P],
                                         start=False, stop=True)
                    last.then_inc(psum_ready, 1)
                taken(pe, ("pool", l, 1))
                for tt in range(TT):
                    begin(("mix", l, tt))
                    for g in range(4):
                        last = pe.matmul(bank(("mix", l, tt))[:, g * P:(g + 1) * P], POOLT[:, g, tt * P:(tt + 1) * P],
                                         POOLW[:, g, :], start=True, stop=True)
                    last.then_inc(psum_ready, 1)
                pe.wait_ge(qk_ready, 3 * (l + 1))
                for tt in range(TT):
                    begin(("qT", l, tt))
                    for j in range(4):
                        last = pe.transpose(bank(("qT", l, tt))[:, j * P:(j + 1) * P],
                                            PROJ[:, tt, POOL + j * P:POOL + (j + 1) * P], IDENT)
                    last.then_inc(psum_ready, 1)
                begin(("kT", l))
                for kv in range(NKV):
                    for tt in range(TT):
                        at = kv * T + tt * P
                        last = pe.transpose(bank(("kT", l))[:, at:at + P],
                                            KD[:, tt, kv].rearrange("p u d -> p (u d)"), IDENT)
                last.then_inc(psum_ready, 1)
                taken(pe, ("kT", l))

                def score(to, h, tt, nk):
                    at = HD * (h % 2)
                    return pe.matmul(to, QT[at:at + HD, h // 2, tt * P:(tt + 1) * P],
                                     KTA[at:at + HD, h // (NH // NKV), 0:nk], start=True, stop=True)

                attend("a", l, S_A, PT_A, score,
                       lambda kt, h: PROJ[:, kt, 1152 + (h // 4) * HD:1152 + (h // 4 + 1) * HD], 1)
                transpose_rows("yT", l)
                taken(pe, ("yT", l, 1, 1))
                for c in range(2):
                    project(lambda tt: ("out", l, c, tt), l, "out", c, 512)
                    arrived(pe, ("out", l, c, 1))
                    release()
                begin(("subT", l))
                for q in range(2):
                    last = pe.transpose(bank(("subT", l))[:, q * P:(q + 1) * P], SUBK[:, q, :], IDENT)
                last.then_inc(psum_ready, 1)
                transpose_rows("h2T", l)
                taken(pe, ("h2T", l, 1, 1))
                for c in range(4):
                    for j in range(2):
                        weights_first(("wq", l, 2 * c + j), l, "wq", c, 2 * P * j, j == 0, j == 1)
                    arrived(pe, ("wq", l, 2 * c + 1))
                    release()
                taken(pe, ("wq", l, 7))
                for tt in range(TT):
                    for b in range(4):
                        begin(("s", l, tt, b))
                        for j in range(4):
                            hp = 4 * b + j
                            last = pe.matmul(bank(("s", l, tt, b))[:, j * P:(j + 1) * P],
                                             QTP[:, hp, tt * P:(tt + 1) * P], SUBT[:, hp % 2, :],
                                             start=True, stop=True)
                        last.then_inc(psum_ready, 1)
                for tt in range(TT):
                    base = (l * TT + tt) * SLOTS

                    def add(i, s, first=False):
                        pe.wait_ge(v_loaded[s], i * 16 + (base // RING + 1) * 16)
                        pe.wait_ge(diag_ready, i * RING + (base + s + 1))
                        for half in range(2):
                            last = pe.matmul(PO[:, half, :], DIAG[:, s, :], GV[:, s, half * 512:(half + 1) * 512],
                                             start=first, stop=False, skip_group_check=True)
                        last.then_inc(expert_added, 1)

                    if base:
                        pe.wait_ge(sums_read, 2 * (l * TT + tt))
                    for s in range(RING):
                        add(0, s, s == 0)
                    with pe.Fori(1, SLOTS // RING) as i:
                        for s in range(RING):
                            add(i, s)

            for l in range(DEPTH):
                transpose_rows("bhT", l)
                taken(pe, ("bhT", l, 1, 1))
                for c in range(2):
                    for j in range(2):
                        weights_first(("fqk", l, 2 * c + j), l, "bin", c, 2 * P * j, j == 0, j == 1)
                    arrived(pe, ("fqk", l, 2 * c + 1))
                    release()
                project(lambda tt: ("fv", l, tt), l, "bin", 2, 512)
                arrived(pe, ("fv", l, 1))
                release()
                project(lambda tt: ("rest", l, tt), l, "bin", 3, REST)
                arrived(pe, ("rest", l, 1))
                release()
                pe.wait_ge(cn_ready, 4 * (l + 1))
                for tt in range(TT):
                    begin(("cT", l, tt))
                    for j in range(3):
                        last = pe.transpose(bank(("cT", l, tt))[:, j * P:(j + 1) * P],
                                            R[:, tt, 8 + j * P:8 + (j + 1) * P], IDENT)
                    last.then_inc(psum_ready, 1)
                for tt in range(TT):
                    taken(pe, ("cT", l, tt))
                    for c in range(2):
                        n = min(512, 768 - 512 * c)
                        begin(("uq", l, tt, c))
                        for k in range(2):
                            last = pe.matmul(bank(("uq", l, tt, c))[:, 0:n], CT[:, k, tt * P:(tt + 1) * P],
                                             UQ[:, k, 512 * c:512 * c + n], start=(k == 0), stop=(k == 1))
                        last.then_inc(psum_ready, 1)
                    for c in range(2):
                        begin(("ukv", l, tt, c))
                        pe.matmul(bank(("ukv", l, tt, c)), CT[:, 2, tt * P:(tt + 1) * P],
                                  UKV[:, 512 * c:512 * c + 512], start=True, stop=True).then_inc(psum_ready, 1)
                pe.wait_ge(decay_ready, l + 1)
                if l == 0:
                    pe.wait_ge(consts_ready, 2)

                def fox_score(to, h, tt, nk):
                    at = HD * (h % 2)
                    pe.matmul(to, FQT[at:at + HD, h // 2, tt * P:(tt + 1) * P], FKT[at:at + HD, h // 2, 0:nk],
                              start=True, stop=False)
                    for k in range(tt + 1):
                        last = pe.matmul(to, LFB[:, k, h, :], UTRI[:, k, 0:nk], start=False, stop=(k == tt))
                    return last

                attend("f", l, S_B, PT_B, fox_score, lambda kt, h: FV[:, kt, h * HD:(h + 1) * HD], 0)
                pe.wait_ge(mla_ready, 2 * (l + 1))
                for name, src in (("qmT", QM), ("kmT", KM)):
                    for tt in range(TT):
                        for b in range(2):
                            begin((name, l, tt, b))
                            for j in range(4):
                                last = pe.transpose(bank((name, l, tt, b))[0:DK, j * P:(j + 1) * P],
                                                    src[:, tt, 4 * b + j, :], IDENT)
                            last.then_inc(psum_ready, 1)
                taken(pe, ("kmT", l, 1, 1))

                def mla_score(to, h, tt, nk):
                    return pe.matmul(to, QMT[0:DK, h, tt * P:(tt + 1) * P], KMT[0:DK, h, 0:nk], start=True, stop=True)

                attend("m", l, S_B, PT_B, mla_score, lambda kt, h: KV[:, kt, h, HD:2 * HD], 0)
                transpose_rows("byT", l)
                taken(pe, ("byT", l, 1, 1))
                for c in range(2):
                    project(lambda tt: ("bout", l, c, tt), l, "bout", c, 512)
                    arrived(pe, ("bout", l, c, 1))
                    release()
                transpose_rows("fhT", l)
                taken(pe, ("fhT", l, 1, 1))
                for tt in range(TT):
                    begin(("route", l, tt))
                    for k in range(KT):
                        last = pe.matmul(bank(("route", l, tt))[:, 0:NG + NE], HT[:, k, tt * P:(tt + 1) * P],
                                         GR[:, k, :], start=(k == 0), stop=(k == KT - 1))
                    last.then_inc(psum_ready, 1)
                pe.wait_ge(onehot_ready, l + 1)
                begin(("rank", l))
                rank = bank(("rank", l))[:, 0:3 * NE].rearrange("p (n e) -> p n e", e=NE)
                for n, terms in enumerate((
                    [(UTRI[:, 0, 0:P], 0)], [(UTRI[:, 0, P:T], 0), (UTRI[:, 1, P:T], 1)], [(ONES, 0), (ONES, 1)],
                )):
                    for m, (ones, tt) in enumerate(terms):
                        last = pe.matmul(rank[:, n], ones, PICKS[:, tt], start=(m == 0), stop=(m == len(terms) - 1))
                last.then_inc(psum_ready, 1)
                taken(pe, ("rank", l))

                def down(i, s):
                    b = i * EXP_RING + (l * NBX + s)
                    pe.wait_ge(hidden_ready, b + 1)
                    for c in range(2):
                        for j in range(2):
                            last = pe.matmul(PS[0:BT, 4 + c, :], HH[:, s % 2, j, :], WD[s][:, j, c * 512:(c + 1) * 512],
                                             start=(j == 0), stop=(j == 1))
                    last.then_inc(down_done, 1)

                def body(i, s, first):
                    b = i * EXP_RING + (l * NBX + s)
                    pe.wait_ge(sel_ready, b + 1)
                    for k in range(KT):
                        for tt in range(TT):
                            last = pe.matmul(PS[:, s % 2, k * BT:(k + 1) * BT], HR[:, tt, k * P:(k + 1) * P],
                                             SEL[:, s % 2, tt, :], start=(tt == 0), stop=(tt == 1))
                    last.then_inc(picked, 1)
                    if not first:
                        down(*before(i, s))
                    if isinstance(i, int):
                        pe.wait_ge(expert_loaded[s], (l * NBX // EXP_RING + i + 1) * 48)
                    else:
                        pe.wait_ge(expert_loaded[s], i * 48 + (l * NBX // EXP_RING + 1) * 48)
                    pe.wait_ge(picked_out, b + 1)
                    for n, w in enumerate((WG[s], WU[s])):
                        for f in range(2):
                            at = (2 * n + f) * BT
                            for k in range(KT):
                                last = pe.matmul(PS[:, 2 + s % 2, at:at + BT], w[:, k, f * P:(f + 1) * P],
                                                 HTB[s % 2][:, k, :], start=(k == 0), stop=(k == KT - 1))
                    last.then_inc(gate_up_done, 1)

                blocks(pe, l, body, down, [(picked, 1), (gate_up_done, 1), (down_done, 1)])

        @block.vector
        def _(dve):
            steps = [0]
            roots = [0]
            atts = [0]
            probs = [0]

            def go(ins):
                steps[0] += 1
                ins.then_inc(vector_step, 1)

            def sync():
                dve.wait_ge(vector_step, steps[0])

            def step(ins):
                go(ins)
                sync()

            def root(n):
                dve.sem_inc(squares_ready, 1)
                roots[0] += 1
                dve.wait_ge(root_ready, roots[0])
                step(dve.reciprocal(RS[:, 0:n], RT[:, 0:n]))

            def attention_rows(kind, l, S, scale, bias, sink):
                for tt in range(TT):
                    nk = (tt + 1) * P
                    per = 512 // nk
                    for b in range(NH // per):
                        name = (kind + "sc", l, tt, b)
                        arrived(dve, name)
                        heads = slice(first_head(b, per), first_head(b, per) + 2 * per - 1, 2)
                        dve.scalar_tensor_tensor(S[tt][:, heads, :],
                                                 bank(name).rearrange("p (h s) -> p h s", h=per), scale,
                                                 bias(tt, heads, per, nk), ALU.mult, ALU.add).then_inc(evac["v"], 1)
                    taken(dve, name)
                    step(dve.tensor_reduce(MX[:, tt], S[tt], AX, ALU.max))
                    if sink:
                        step(dve.tensor_tensor(MX[:, tt], MX[:, tt], SINK, ALU.max))
                        step(dve.tensor_tensor(SE[:, tt], SINK, MX[:, tt], ALU.subtract))
                    dve.tensor_scalar(NM[:, tt], MX[:, tt], -1.0, None, ALU.mult).then_inc(negmax_ready, 1)
                    atts[0] += 1
                    dve.wait_ge(negmax_ready, atts[0])

            def attention_values(kind, l, at, sink):
                for tt in range(TT):
                    probs[0] += NH + sink
                    dve.wait_ge(probs_ready, probs[0])
                    if sink:
                        step(dve.tensor_tensor(DEN[:, tt], DEN[:, tt], EXS[:, tt], ALU.add))
                    step(dve.reciprocal(RD[:, tt], DEN[:, tt]))
                    arrived(dve, (kind + "pv", l, tt))
                    dve.tensor_tensor(HR[:, tt, at:at + 512].rearrange("p (h d) -> p h d", h=NH),
                                      bank((kind + "pv", l, tt)).rearrange("p (h d) -> p h d", h=NH),
                                      RD[:, tt, :].unsqueeze(2).broadcast_to([P, NH, HD]), ALU.mult).then_inc(evac["v"], 1)

            dve.sem_inc(dot_ready, RING)

            FREQ, ANG, TURN = TMP[:, 0:16], TMP[:, 32:64], TMP[:, 64:96]
            POS = RW[:, 2:4]
            for k in range(16):
                go(dve.memset(FREQ[:, k:k + 1], 10000.0 ** (-k / 16.0)))
            dve.wait_ge(pos_loaded, 16)
            step(dve.tensor_copy(POS, RW[:, 0:TT].bitcast(I32)))
            for tt in range(TT):
                step(dve.tensor_scalar(ANG[:, tt * 16:(tt + 1) * 16], FREQ, POS[:, tt:tt + 1], None, ALU.mult))
            C1 = 6.28125
            C2 = 0.0019350051879882812
            C3 = 2 * pi - C1 - C2
            for n, (table, turn, quarter) in enumerate(((SIN, 0.0, 0.0), (COS, 0.25, pi / 2))):
                tab = table.rearrange("p t f -> p (t f)")
                step(dve.tensor_scalar(TURN, ANG, 1.0 / (2 * pi), turn, ALU.mult, ALU.add))
                step(dve.tensor_scalar(TURN, TURN, 12582912.0, None, ALU.add))
                step(dve.tensor_scalar(TURN, TURN, 12582912.0, None, ALU.subtract))
                step(dve.scalar_tensor_tensor(tab, TURN, -C1, ANG, ALU.mult, ALU.add))
                step(dve.scalar_tensor_tensor(tab, TURN, -C2, tab, ALU.mult, ALU.add))
                step(dve.scalar_tensor_tensor(tab, TURN, -C3, tab, ALU.mult, ALU.add))
                step(dve.tensor_scalar(tab, tab, quarter, 3.1415925, ALU.add, ALU.min))
                step(dve.tensor_scalar(tab, tab, -3.1415925, None, ALU.max))
                dve.sem_inc(trig_in, 1)

            dve.wait_ge(cond_ready, 1)
            dve.wait_ge(bada_loaded, 16 * DEPTH)
            for l in range(DEPTH):
                for c3 in range(3):
                    for kp in range(4):
                        name = ("ada", l, c3, kp)
                        loaded(dve, name)
                        w = ring[CH[name][1]].rearrange("p (k n) -> p k n", k=2)
                        acc = MODL[l][:, c3 * 2048:(c3 + 1) * 2048]
                        for k in range(2):
                            step(dve.scalar_tensor_tensor(acc, w[:, k, :], COND[:, 2 * kp + k:2 * kp + k + 1], acc,
                                                          ALU.mult, ALU.add))
                        dve.sem_inc(chunk_used["v"], 1)
                dve.sem_inc(acc_ready, 1)
            dve.wait_ge(gains_loaded, 64)
            for l in range(DEPTH):
                for n in range(12):
                    name = ("ada", l, n)
                    if J[name][2] == "v":
                        arrived(dve, name)
                        gain = NGAIN[:, 2 * l + (n // 2 == 4), (n % 2) * 512:(n % 2 + 1) * 512]
                        dve.scalar_tensor_tensor(MODL[l][:, n * 512:(n + 1) * 512], bank(name), 1.0, gain,
                                                 ALU.add, ALU.mult).then_inc(evac["v"], 1)

            def modulated(l, i):
                for tt in range(TT):
                    step(dve.scalar_tensor_tensor(HR[:, tt], X[:, tt], RS[:, tt:tt + 1], mrow(l, i + 1), ALU.mult, ALU.mult))
                    dve.tensor_tensor(HR[:, tt], HR[:, tt], mrow(l, i), ALU.add).then_inc(rows_ready, 2)

            dve.wait_ge(x_loaded, 16)
            for l in range(DEPTH):
                root(TT)
                taken(dve, ("ada", l, 11))
                taken(dve, ("ada", l, 9))
                modulated(l, 0)
                dve.wait_ge(params_loaded, 16 * 7 * (l + 1))
                taken(dve, ("in", l, 2, 1))
                qk = PROJ[:, :, POOL:POOL + 640]
                sq = QSQ.rearrange("p (t n) -> p t n", t=TT)
                step(dve.tensor_tensor(sq, qk, qk, ALU.mult))
                step(dve.tensor_reduce(SSQ[:, 0:20], QSQ.rearrange("p (h d) -> p h d", d=HD), AX, ALU.add))
                root(20)
                heads = qk.rearrange("p t (h d) -> p t h d", d=HD)
                rs = RS[:, 0:20].rearrange("p (t h) -> p t h", t=TT)
                step(dve.tensor_tensor(heads, heads, rs.unsqueeze(3).broadcast_to([P, TT, 10, HD]), ALU.mult))
                for tt in range(TT):
                    q = heads[:, tt, 0:NH]
                    ins = dve.tensor_tensor(q, q, QKG[:, 0:HD].unsqueeze(1).broadcast_to([P, NH, HD]), ALU.mult)
                    if tt == 0:
                        step(ins)
                    else:
                        ins.then_inc(qk_ready, 1)
                for u in range(2):
                    for tt in range(TT):
                        ins = dve.tensor_tensor(KD[:, tt, :, u, :], heads[:, tt, NH:NH + NKV],
                                                QKG[:, HD:2 * HD].unsqueeze(1).broadcast_to([P, NKV, HD]), ALU.mult)
                        if tt == 0:
                            step(ins)
                        else:
                            ins.then_inc(qk_ready, 1)
                for tt in range(TT):
                    arrived(dve, ("mix", l, tt))
                    dve.tensor_tensor(HR[:, tt, 0:512], bank(("mix", l, tt)), PSC, ALU.mult).then_inc(evac["v"], 1)
                attention_rows("a", l, S_A, HD ** -0.5,
                               lambda tt, heads, per, nk: BIAS[:, heads, 2 * P - nk:2 * P], True)
                attention_values("a", l, 512, 1)
                taken(dve, ("apv", l, 1))
                for tt in range(TT):
                    for half in range(2):
                        y = HR[:, tt, half * 512:(half + 1) * 512]
                        n = 2 * tt + half
                        step(dve.tensor_tensor_reduce(JUNK[:, 0:512], y, y, 1.0, 0.0, ALU.mult, ALU.add, SSQ[:, n:n + 1]))
                root(4)
                for tt in range(TT):
                    for half in range(2):
                        y = HR[:, tt, half * 512:(half + 1) * 512]
                        n = 2 * tt + half
                        dve.scalar_tensor_tensor(y, y, RS[:, n:n + 1], MIXG[:, half * 512:(half + 1) * 512],
                                                 ALU.mult, ALU.mult).then_inc(rows_ready, 1)
                for c in range(2):
                    for tt in range(TT):
                        name = ("out", l, c, tt)
                        arrived(dve, name)
                        part = slice(c * 512, (c + 1) * 512)
                        dve.tensor_tensor(TMP, bank(name), mrow(l, 2)[:, part], ALU.mult).then_inc(evac["v"], 1)
                        taken(dve, name)
                        step(dve.tensor_tensor(X[:, tt, part], X[:, tt, part], TMP, ALU.add))
                root(TT)
                modulated(l, 3)

                def best16(n, values, vals, idxs):
                    for a in range(n):
                        go(dve.max(vals[:, a, 0:8], values[:, a, :]))
                    sync()
                    for a in range(n):
                        go(dve.max_index(idxs[:, a, 0:8], vals[:, a, 0:8], values[:, a, :]))
                    sync()
                    for a in range(n):
                        go(dve.match_replace(values[:, a, :], vals[:, a, 0:8], values[:, a, :], LOWEST))
                    sync()
                    for a in range(n):
                        go(dve.max(vals[:, a, 8:16], values[:, a, :]))
                    sync()
                    for a in range(n):
                        go(dve.max_index(idxs[:, a, 8:16], vals[:, a, 8:16], values[:, a, :]))
                    sync()

                for tt in range(TT):
                    taken(dve, ("s", l, TT - 1, 3))
                    best16(16, SS[:, tt], V16, I16)
                    step(dve.tensor_copy(F16, I16))
                    v2 = V16.rearrange("p (h q) k -> p h q k", q=2)
                    f2 = F16.rearrange("p (h q) k -> p h q k", q=2)
                    wide = [P, PH, TOPK, TOPK]
                    step(dve.tensor_tensor(CAND.rearrange("p h (i j) -> p h i j", i=TOPK),
                                           v2[:, :, 0, :].unsqueeze(3).broadcast_to(wide),
                                           v2[:, :, 1, :].unsqueeze(2).broadcast_to(wide), ALU.add))
                    best16(PH, CAND, BV, BI)
                    for half, (op, by, dst) in enumerate(((ALU.logical_shift_right, 4, E1), (ALU.bitwise_and, 15, E2))):
                        step(dve.tensor_scalar(BU, BI, by, None, op))
                        step(dve.tensor_copy(BF, BU))
                        flat = OH.rearrange("p h k c -> p (h k) c")
                        step(dve.tensor_tensor(flat, BF.rearrange("p h k -> p (h k)").unsqueeze(2).broadcast_to([P, SLOTS, TOPK]),
                                               IOTA.unsqueeze(1).broadcast_to([P, SLOTS, TOPK]), ALU.is_equal))
                        step(dve.tensor_tensor(OH, OH, f2[:, :, half, :].unsqueeze(2).broadcast_to(wide), ALU.mult))
                        step(dve.tensor_reduce(dst, OH, AX, ALU.add))
                    step(dve.scalar_tensor_tensor(E1, E1, float(NKEY), E2, ALU.mult, ALU.add))
                    gate = GATE[:, tt].rearrange("p (h k) -> p h k", h=PH)
                    step(dve.tensor_tensor(gate, BV, BV[:, :, 0:1].broadcast_to([P, PH, TOPK]), ALU.subtract))
                    dve.sem_inc(gexp_in, 1)
                    dve.tensor_scalar(IDX[:, tt].rearrange("p (h k) -> p h k", h=PH), E1, float(l * NEXP), None,
                                      ALU.add).then_inc(idx_ready, 1)
                    dve.wait_ge(gexp_out, l * TT + tt + 1)
                    step(dve.tensor_reduce(RS[:, 0:PH], gate, AX, ALU.add))
                    step(dve.reciprocal(RT[:, 0:PH], RS[:, 0:PH]))
                    step(dve.tensor_tensor(gate, gate, RT[:, 0:PH].unsqueeze(2).broadcast_to([P, PH, TOPK]), ALU.mult))

                for tt in range(TT):
                    base = (l * TT + tt) * SLOTS

                    def dot(i, s):
                        dve.wait_ge(u_loaded[s], i * 16 + (base // RING + 1) * 16)
                        dve.wait_ge(dot_ready, i * RING + (base + s + RING))
                        dve.tensor_tensor_reduce(JUNK, GU[:, s, :], HR[:, tt], 1.0, 0.0, ALU.mult, ALU.add,
                                                 DOT[:, s:s + 1]).then_inc(dot_ready, 1)

                    def diag(i, s):
                        dve.wait_ge(gelu_ready, i * RING + (base + s + 1))
                        dve.wait_ge(expert_added, i * RING + (base + s + 1))
                        dve.tensor_scalar(DIAG[:, s, :], IDENT, ACTV[:, s:s + 1], GATE[:, tt, bass.ds(i * RING + s, 1)],
                                          ALU.mult, ALU.mult).then_inc(diag_ready, 1)

                    dot(0, 0)
                    for s in range(1, RING):
                        dot(0, s)
                        diag(0, s - 1)
                    with dve.Fori(1, SLOTS // RING) as i:
                        dot(i, 0)
                        diag(i - 1, RING - 1)
                        for s in range(1, RING):
                            dot(i, s)
                            diag(i, s - 1)
                    diag(SLOTS // RING - 1, RING - 1)
                    dve.wait_ge(expert_added, base + SLOTS + RING)
                    for half in range(2):
                        part = slice(half * 512, (half + 1) * 512)
                        dve.tensor_tensor(TMP, PO[:, half, :], mrow(l, 5)[:, part], ALU.mult).then_inc(sums_read, 1)
                        dve.wait_ge(sums_read, 2 * (l * TT + tt) + half + 1)
                        step(dve.tensor_tensor(X[:, tt, part], X[:, tt, part], TMP, ALU.add))
                dve.sem_inc(layer_done, 1)

            def gained(gain, inc):
                for tt in range(TT):
                    dve.scalar_tensor_tensor(HR[:, tt], X[:, tt], RS[:, tt:tt + 1], gain, ALU.mult,
                                             ALU.mult).then_inc(inc, 2 if inc is rows_ready else 1)

            pb = 16 * 7 * DEPTH + 16
            for l in range(DEPTH):
                root(TT)
                dve.wait_ge(params_loaded, pb + 16 * 11 * (l + 1))
                gained(AN, rows_ready)
                for tt in range(TT):
                    arrived(dve, ("rest", l, tt))
                    dve.tensor_copy(R[:, tt, :], bank(("rest", l, tt))[:, 0:REST]).then_inc(evac["v"], 1)
                taken(dve, ("rest", l, 1))
                z, az = RTMP[:, 0:16].rearrange("p (t h) -> p t h", t=TT), RTMP[:, 16:32].rearrange("p (t h) -> p t h", t=TT)
                step(dve.tensor_tensor(z, R[:, :, 0:NH], BFB.unsqueeze(1).broadcast_to([P, TT, NH]), ALU.add))
                step(dve.tensor_scalar(az, z, -1.0, None, ALU.mult))
                step(dve.tensor_tensor(az, az, z, ALU.max))
                dve.sem_inc(logsig_in, 1)
                for tt in range(TT):
                    for n, (a, b) in enumerate(((8, 8 + QL), (8 + QL, 8 + QL + KVL))):
                        y = R[:, tt, a:b]
                        step(dve.tensor_tensor_reduce(JUNK[:, 0:b - a], y, y, 1.0, 0.0, ALU.mult, ALU.add,
                                                      SSQ[:, 2 * n + tt:2 * n + tt + 1]))
                dve.wait_ge(logsig_out, l + 1)
                step(dve.tensor_scalar(z, z, 0.0, None, ALU.min))
                step(dve.tensor_tensor(z, z, az, ALU.subtract))
                step(dve.tensor_scalar(z, z, -(HD ** 0.5), None, ALU.mult))
                dve.tensor_copy(LFB, z.unsqueeze(3).broadcast_to([P, TT, NH, P])).then_inc(decay_ready, 1)
                root(4)
                for tt in range(TT):
                    for n, (a, b, gain) in enumerate(((8, 8 + QL, QG), (8 + QL, 8 + QL + KVL, KG))):
                        y = R[:, tt, a:b]
                        dve.scalar_tensor_tensor(y, y, RS[:, 2 * n + tt:2 * n + tt + 1], gain, ALU.mult,
                                                 ALU.mult).then_inc(cn_ready, 1)
                if l == 0:
                    dve.wait_ge(trig_out, 2)
                    dve.wait_ge(consts_ready, 2)
                kr = R[:, :, 8 + QL + KVL:REST]
                kt = [RTMP[:, 300 + 32 * i:332 + 32 * i].rearrange("p (t f) -> p t f", t=TT) for i in range(4)]
                go(dve.tensor_tensor(kt[0], kr[:, :, 0:16], COS, ALU.mult))
                go(dve.tensor_tensor(kt[1], kr[:, :, 16:32], SIN, ALU.mult))
                go(dve.tensor_tensor(kt[2], kr[:, :, 16:32], COS, ALU.mult))
                step(dve.tensor_tensor(kt[3], kr[:, :, 0:16], SIN, ALU.mult))
                go(dve.tensor_tensor(kt[0], kt[0], kt[1], ALU.subtract))
                step(dve.tensor_tensor(kt[2], kt[2], kt[3], ALU.add))
                for tt in range(TT):
                    for n, src in ((0, kt[0]), (1, kt[2])):
                        go(dve.tensor_copy(KM[:, tt, :, HD + 16 * n:HD + 16 * n + 16],
                                           src[:, tt].unsqueeze(1).broadcast_to([P, NH, 16])))
                taken(dve, ("ukv", l, 1, 1))
                for tt in range(TT):
                    step(dve.tensor_copy(KM[:, tt, :, 0:HD], KV[:, tt, :, 0:HD]))
                dve.sem_inc(mla_ready, 1)
                for tt in range(TT):
                    x1, x2 = QM[:, tt, :, HD:HD + 16], QM[:, tt, :, HD + 16:DK]
                    cs, sn = (t[:, tt].unsqueeze(1).broadcast_to([P, NH, 16]) for t in (COS, SIN))
                    qt = [RTMP[:, 430 + 128 * i:558 + 128 * i].rearrange("p (h f) -> p h f", h=NH) for i in range(4)]
                    go(dve.tensor_tensor(qt[0], x1, cs, ALU.mult))
                    go(dve.tensor_tensor(qt[1], x2, sn, ALU.mult))
                    go(dve.tensor_tensor(qt[2], x2, cs, ALU.mult))
                    step(dve.tensor_tensor(qt[3], x1, sn, ALU.mult))
                    go(dve.tensor_tensor(x1, qt[0], qt[1], ALU.subtract))
                    step(dve.tensor_tensor(x2, qt[2], qt[3], ALU.add))
                dve.sem_inc(mla_ready, 1)

                def causal(tt, heads, per, nk):
                    return CMASK[:, 2 * P - nk:2 * P].unsqueeze(1).broadcast_to([P, per, nk])

                attention_rows("f", l, S_B, HD ** -0.5, causal, False)
                attention_values("f", l, 0, 0)
                attention_rows("m", l, S_B, DK ** -0.5, causal, False)
                attention_values("m", l, 512, 0)
                taken(dve, ("mpv", l, 1))
                sq = SQB.rearrange("p (t n) -> p t n", t=TT)
                step(dve.tensor_tensor(sq, HR, HR, ALU.mult))
                step(dve.tensor_reduce(SSQ[:, 0:32], SQB.rearrange("p (h d) -> p h d", d=HD), AX, ALU.add))
                root(32)
                for tt in range(TT):
                    y = HR[:, tt].rearrange("p (h d) -> p h d", d=HD)
                    step(dve.tensor_tensor(y, y, RS[:, 16 * tt:16 * tt + 16].unsqueeze(2).broadcast_to([P, 16, HD]), ALU.mult))
                    dve.tensor_tensor(HR[:, tt], HR[:, tt], ON, ALU.mult).then_inc(rows_ready, 2)
                for c in range(2):
                    for tt in range(TT):
                        name = ("bout", l, c, tt)
                        arrived(dve, name)
                        part = slice(c * 512, (c + 1) * 512)
                        dve.tensor_tensor(X[:, tt, part], X[:, tt, part], bank(name), ALU.add).then_inc(evac["v"], 1)
                taken(dve, ("bout", l, 1, 1))
                root(TT)
                for tt in range(TT):
                    dve.scalar_tensor_tensor(HR[:, tt].rearrange("p (k a) -> p k a", k=KT),
                                             X[:, tt].rearrange("p (a k) -> p k a", k=KT), RS[:, tt:tt + 1],
                                             FN.rearrange("p (a k) -> p k a", k=KT), ALU.mult,
                                             ALU.mult).then_inc(rows_ready, 2)

                GL = RTMP[:, 0:80].rearrange("p (t n) -> p t n", t=TT)
                for tt in range(TT):
                    arrived(dve, ("route", l, tt))
                    dve.tensor_copy(GL[:, tt], bank(("route", l, tt))[:, 0:NG + NE]).then_inc(evac["v"], 1)
                taken(dve, ("route", l, 1))
                gexp = RTMP[:, 100:116].rearrange("p (t g) -> p t g", t=TT)
                gtop = RTMP[:, 120:136].rearrange("p (t g) -> p t g", t=TT)
                gidx = RTMP[:, 140:156].rearrange("p (t g) -> p t g", t=TT).bitcast(U32)
                gone = RTMP[:, 160:176].rearrange("p (t g) -> p t g", t=TT)
                gfl = RTMP[:, 180:196].rearrange("p (t g) -> p t g", t=TT)
                d2 = RTMP[:, 200:202].rearrange("p (t g) -> p t g", t=TT)
                ig = RTMP[:, 210:226].rearrange("p (t g) -> p t g", t=TT)
                itop = RTMP[:, 230:246].rearrange("p (t g) -> p t g", t=TT)
                iidx = RTMP[:, 250:266].rearrange("p (t g) -> p t g", t=TT).bitcast(U32)
                ifl = RTMP[:, 270:286].rearrange("p (t g) -> p t g", t=TT)
                prod = RTMP[:, 300:364].rearrange("p (t g e) -> p t g e", t=TT, g=NG)
                sm = RTMP[:, 400:440].rearrange("p (n t g) -> p n t g", n=20, t=TT)
                w4 = RTMP[:, 450:466].rearrange("p (n t e) -> p n t e", n=2, t=TT)
                iota8 = RW[:, 48:56]
                for tt in range(TT):
                    go(dve.max(gtop[:, tt], GL[:, tt, 0:NG]))
                sync()
                for tt in range(TT):
                    go(dve.max_index(gidx[:, tt], gtop[:, tt], GL[:, tt, 0:NG]))
                step(dve.tensor_tensor(gexp, GL[:, :, 0:NG], gtop[:, :, 0:1].broadcast_to([P, TT, NG]), ALU.subtract))
                dve.sem_inc(router_in, 1)
                step(dve.tensor_copy(gfl, gidx))
                step(dve.tensor_tensor(gone, gfl[:, :, 0:1].broadcast_to([P, TT, NG]),
                                       iota8.unsqueeze(1).broadcast_to([P, TT, NG]), ALU.is_equal))
                logits = GL[:, :, NG:NG + NE].rearrange("p t (g e) -> p t g e", g=NG)
                step(dve.tensor_tensor(prod, logits, gone.unsqueeze(3).broadcast_to([P, TT, NG, EPG]), ALU.mult))
                step(dve.memset(ig, LOWEST))
                for tt in range(TT):
                    step(dve.tensor_reduce(ig[:, tt, 0:EPG], prod[:, tt].rearrange("p g e -> p e g"), AX, ALU.add))
                for tt in range(TT):
                    go(dve.max(itop[:, tt], ig[:, tt]))
                sync()
                for tt in range(TT):
                    go(dve.max_index(iidx[:, tt], itop[:, tt], ig[:, tt]))
                step(dve.tensor_tensor(d2, itop[:, :, 1:2], itop[:, :, 0:1], ALU.subtract))
                dve.sem_inc(router_in, 1)
                step(dve.tensor_copy(ifl, iidx))
                dve.wait_ge(router_out, 2 * l + 2)
                step(dve.tensor_reduce(sm[:, 0], gexp, AX, ALU.add))
                step(dve.reciprocal(sm[:, 1], sm[:, 0]))
                step(dve.tensor_scalar(sm[:, 2], d2, 1.0, None, ALU.add))
                step(dve.reciprocal(sm[:, 3], sm[:, 2]))
                step(dve.tensor_tensor(GK[:, :, 0:1], sm[:, 3], sm[:, 1], ALU.mult))
                step(dve.tensor_tensor(GK[:, :, 1:2], GK[:, :, 0:1], d2, ALU.mult))
                for k in range(2):
                    step(dve.tensor_tensor(w4[:, k], ifl[:, :, k:k + 1].broadcast_to([P, TT, EPG]),
                                           iota8[:, 0:EPG].unsqueeze(1).broadcast_to([P, TT, EPG]), ALU.is_equal))
                    for tt in range(TT):
                        step(dve.tensor_tensor(ONEHOT[:, k, tt].rearrange("p (g e) -> p g e", g=NG),
                                               gone[:, tt].unsqueeze(2).broadcast_to([P, NG, EPG]),
                                               w4[:, k, tt].unsqueeze(1).broadcast_to([P, NG, EPG]), ALU.mult))
                dve.tensor_tensor(PICKS, ONEHOT[:, 0], ONEHOT[:, 1], ALU.add).then_inc(onehot_ready, 1)

                rk = RTMP[:, 700:796].rearrange("p (n e) -> p n e", e=NE)
                arrived(dve, ("rank", l))
                dve.tensor_copy(rk, bank(("rank", l))[:, 0:3 * NE].rearrange("p (n e) -> p n e", e=NE)).then_inc(evac["v"], 1)
                taken(dve, ("rank", l))
                nx, xend, xb = (RTMP[:, 800 + 32 * n:832 + 32 * n] for n in range(3))
                rank, count = rk[:, 0:TT], rk[:, TT]
                q = RTMP[:, 300:364].rearrange("p (t e) -> p t e", t=TT)
                blk = RTMP[:, 900:964].rearrange("p (t e) -> p t e", t=TT)
                more = RTMP[:, 100:164].rearrange("p (t e) -> p t e", t=TT)
                step(dve.tensor_scalar(rank, rank, -1.0, None, ALU.add))
                step(dve.tensor_scalar(nx, count, BT + 0.5, None, ALU.is_gt))
                step(dve.tensor_scalar(q, rank, BT - 0.5, None, ALU.is_gt))
                for n in range(2, T // BT):
                    step(dve.scalar_tensor_tensor(nx, count, n * BT + 0.5, nx, ALU.is_gt, ALU.add))
                    step(dve.scalar_tensor_tensor(q, rank, n * BT - 0.5, q, ALU.is_gt, ALU.add))
                step(dve.tensor_tensor_scan(xend, nx, CMASK[:, 0:NE], 0.0, ALU.add, ALU.add))
                dve.tensor_copy(PLAN[:, NX:NX + 1], xend[:, NE - 1:NE]).then_inc(plan_step, 1)
                cmpx = EQ.rearrange("p t k s -> p (t k s)").rearrange("p (x e) -> p x e", e=NE)
                step(dve.tensor_tensor(cmpx, xend.unsqueeze(1).broadcast_to([P, NX, NE]),
                                       iota8.unsqueeze(2).broadcast_to([P, NX, NE]), ALU.is_le))
                step(dve.tensor_reduce(RT[:, 0:NX], cmpx, AX, ALU.add))
                dve.wait_ge(plan_step, l + 1)
                dve.tensor_scalar(PLAN[:, 0:NX], RT[:, 0:NX], float(NE - 1), None, ALU.min).then_inc(plan_ready, 1)
                step(dve.tensor_tensor(xb, xend, nx, ALU.subtract))
                step(dve.tensor_tensor(xb, xb, ENUM, ALU.subtract))
                step(dve.tensor_scalar(xb, xb, float(NB - 1), None, ALU.add))
                step(dve.tensor_scalar(more, q, 1.0, None, ALU.min))
                step(dve.tensor_tensor(blk, q, xb.unsqueeze(1).broadcast_to([P, TT, NE]), ALU.add))
                step(dve.tensor_tensor(blk, blk, more, ALU.mult))
                step(dve.tensor_tensor(blk, blk, ENUM.unsqueeze(1).broadcast_to([P, TT, NE]), ALU.add))
                step(dve.tensor_tensor(blk, blk, q, ALU.subtract))
                step(dve.scalar_tensor_tensor(blk, blk, float(BT), rank, ALU.mult, ALU.add))
                for k in range(2):
                    step(dve.tensor_tensor(q, ONEHOT[:, k], blk, ALU.mult))
                    step(dve.tensor_reduce(DREL[:, :, k], q, AX, ALU.add))
                step(dve.tensor_copy(DESTI, DREL.rearrange("p t k -> p (t k)")))
                dve.sem_inc(plan_ready, 1)

                def y_rows(i, s):
                    b = i * EXP_RING + (l * NBX + s)
                    dve.wait_ge(down_done, b + 1)
                    if not isinstance(i, int):
                        dve.wait_ge(y_stored[s % 2], i * 32 + 16 * (l * NB // 2 + s // 2))
                    elif EXP_RING * i + s - 2 < NB:
                        if l or i or s > 1:
                            dve.wait_ge(y_stored[s % 2], 16 * (l * NB // 2 + i * 2 + s // 2))
                    else:
                        dve.wait_ge(extra_stored[l][s % 2], 16 * ((EXP_RING * i + s - NB) // 2))
                    dve.tensor_copy(YO[0:BT, s % 2], PS[0:BT, 4:6, :].rearrange("p c d -> p (c d)")).then_inc(y_out, 1)

                def hidden_then_rows(i, s):
                    b = i * EXP_RING + (l * NBX + s)
                    dve.wait_ge(silu_done, b + 1)
                    dve.tensor_tensor(HH[:, s % 2].rearrange("p j t -> p (j t)"), SG[:, s % 2], PS[:, 2 + s % 2, P:2 * P],
                                      ALU.mult).then_inc(hidden_ready, 1)
                    y_rows(i, s)

                def body(i, s, first):
                    b = i * EXP_RING + (l * NBX + s)
                    if l or s or not isinstance(i, int) or i:
                        dve.wait_ge(sel_step, 2 * b)
                    dve.tensor_tensor(EQ, SLOT.unsqueeze(1).unsqueeze(1).broadcast_to([P, TT, 2, BT]),
                                      DREL.unsqueeze(3).broadcast_to([P, TT, 2, BT]), ALU.is_equal).then_inc(sel_step, 1)
                    dve.wait_ge(sel_step, 2 * b + 1)
                    dve.tensor_tensor(SEL[:, s % 2], EQ[:, :, 0], EQ[:, :, 1], ALU.add).then_inc(sel_ready, 1)
                    dve.tensor_scalar(DREL, DREL, float(-BT), None, ALU.add).then_inc(sel_step, 1)
                    if not first:
                        hidden_then_rows(*before(i, s))

                blocks(dve, l, body, hidden_then_rows, [(sel_step, 2), (sel_ready, 1), (hidden_ready, 1), (y_out, 1)])
                dve.wait_ge(y_gathered, 16 * 2 * TT * (l + 1))
                for tt in range(TT):
                    for k in range(2):
                        step(dve.scalar_tensor_tensor(X[:, tt], YG[:, 2 * tt + k], GK[:, tt, k:k + 1], X[:, tt], ALU.mult, ALU.add))
                dve.sem_inc(layer_done, 1)
            root(TT)
            gained(FINAL, out_ready)


_INS = ["x", "c", "w_ada", "b_ada", "norm1_g", "norm2_g", "w_in", "pool_w", "pool_scale", "q_norm_g", "k_norm_g",
        "attn_sinks", "mix_norm_g", "w_out", "peer_wq", "peer_subkeys", "peer_u", "peer_v", "positions_2",
        "attn_norm_2", "w_in_2", "b_f_2", "q_norm_2", "w_uq_2", "kv_norm_2", "w_ukv_2", "fox_out_norm_2",
        "mla_out_norm_2", "w_o_2", "ffn_norm_2", "w_group_2", "w_router_2", "w_gate_2", "w_up_2", "w_down_2",
        "final_norm_2"]
_OUTS = [((1, 256, 1024), "float32")]


def kernel(**inputs):
    import numpy as _np
    import concourse.bacc as _bacc
    from concourse import mybir as _mybir
    from concourse.bass_utils import run_bass_kernel_spmd as _run

    nc = _bacc.Bacc("TRN2", target_bir_lowering=False, num_devices=1)
    arrays, args = {}, []
    for name in _INS:
        a = _np.ascontiguousarray(inputs[name])
        arrays[f"in_{name}_dram"] = a
        args.append(nc.dram_tensor(f"in_{name}_dram", a.shape, _mybir.dt.from_np(a.dtype), kind="ExternalInput").ap())
    for i, (shape, dtype) in enumerate(_OUTS):
        dt = _mybir.dt.from_np(_np.dtype(dtype))
        args.append(nc.dram_tensor(f"out_{i}_dram", shape, dt, kind="ExternalOutput").ap())
    build(nc, *args)
    r = _run(nc, [arrays], core_ids=[0])
    got = tuple(r.results[0][f"out_{i}_dram"] for i in range(len(_OUTS)))
    return got[0]
```

```python
from contextlib import ExitStack
from math import pi

import concourse.bass as bass
from concourse import mybir

F32 = mybir.dt.float32
BF16 = mybir.dt.bfloat16
I32 = mybir.dt.int32
U32 = mybir.dt.uint32
ALU = mybir.AluOpType
ACT = mybir.ActivationFunctionType
AX = mybir.AxisListType.X

P = 128
D = 1024
KT = D // P
T = 256
TT = T // P
DEPTH = 2
EPS = 1e-6
MASKED = -1e30
LOWEST = -3.0e38

POOL = 512
WINDOWS = (2, 4, 8, 16)
HD = 64
NH = 8
NKV = 2
IN_A = 1280
NKEY = 128
NEXP = NKEY * NKEY
PH = 8
TOPK = 16
SLOTS = PH * TOPK
IN_B = 1960
REST = IN_B - 3 * 512
QL, KVL, ROPE = 256, 128, 32
DK = HD + ROPE
NG, EPG = 8, 4
NE = NG * EPG
DE = 256

CHUNK = 4096
NCHUNK = 4
RING = 4
EXP_F = 3 * KT * DE
EXP_RING = 4
BT = 64
NB = NE
NX = 8
NBX = NB + NX
NQ = 4
HQ = PH // NQ
NBANK = 6


def psum_jobs():
    jobs, order, count = {}, [], {"v": 0, "s": 0}

    def add(name, who):
        jobs[name] = (len(order), len(order) % NBANK, who, count[who])
        order.append(name)
        count[who] += 1

    for n in range(12):
        add(("ada", 0, n), "v" if n // 2 in (1, 4) else "s")
    for l in range(DEPTH):
        for tt in range(TT):
            for half in range(2):
                add(("hT", l, tt, half), "s")
        for c in range(3):
            for tt in range(TT):
                add(("in", l, c, tt), "s")
        for b in range(2):
            add(("pool", l, b), "s")
        for tt in range(TT):
            add(("mix", l, tt), "v")
        for tt in range(TT):
            add(("qT", l, tt), "s")
        add(("kT", l), "s")
        attention_jobs(add, "a", l)
        for tt in range(TT):
            for half in range(2):
                add(("yT", l, tt, half), "s")
        for c in range(2):
            for tt in range(TT):
                add(("out", l, c, tt), "v")
        add(("subT", l), "s")
        for tt in range(TT):
            for half in range(2):
                add(("h2T", l, tt, half), "s")
        for c in range(NQ):
            add(("wq", l, 2 * c), "s")
            if c:
                for tt in range(TT):
                    add(("s", l, tt, c - 1), "s")
            add(("wq", l, 2 * c + 1), "s")
        for tt in range(TT):
            add(("s", l, tt, NQ - 1), "s")
        if l + 1 < DEPTH:
            for n in range(12):
                add(("ada", l + 1, n), "s")
    for l in range(DEPTH):
        for tt in range(TT):
            for half in range(2):
                add(("bhT", l, tt, half), "s")
        for b in range(4):
            add(("fqk", l, b), "s")
        for tt in range(TT):
            add(("fv", l, tt), "s")
        for tt in range(TT):
            add(("rest", l, tt), "v")
        for tt in range(TT):
            add(("cT", l, tt), "s")
        for tt in range(TT):
            for c in range(2):
                add(("uq", l, tt, c), "s")
            for c in range(2):
                add(("ukv", l, tt, c), "s")
        attention_jobs(add, "f", l)
        for name in ("qmT", "kmT"):
            for tt in range(TT):
                for b in range(2):
                    add((name, l, tt, b), "s")
        attention_jobs(add, "m", l)
        for tt in range(TT):
            for half in range(2):
                add(("byT", l, tt, half), "s")
        for c in range(2):
            for tt in range(TT):
                add(("bout", l, c, tt), "v")
        for tt in range(TT):
            for half in range(2):
                add(("fhT", l, tt, half), "s")
        for tt in range(TT):
            add(("route", l, tt), "v")
        add(("rank", l), "v")
    return jobs, order


def attention_jobs(add, kind, l):
    for tt in range(TT):
        for b in range(2 * (tt + 1)):
            add((kind + "sc", l, tt, b), "v")
    for tt in range(TT):
        for b in range(2 * (tt + 1)):
            add((kind + "pT", l, tt, b), "s")
        add((kind + "pv", l, tt), "v")


def first_head(b, per):
    return b // 2 * 2 * per + b % 2


MIXER_CHUNKS = ("in0 ada ada in1 ada in2 ada ada ada out0 out1 ada ada ada wq0 ada wq1 ada ada wq2 wq3").split()


def weight_chunks():
    chunks, order, count = {}, [], {"v": 0, "p": 0}

    def add(name, who):
        chunks[name] = (len(order), len(order) % NCHUNK, who, count[who])
        order.append(name)
        count[who] += 1

    for n in range(12):
        add(("ada", 0, n // 4, n % 4), "v")
    for l in range(DEPTH):
        n = 0
        for name in MIXER_CHUNKS:
            if name != "ada":
                add((name[:-1], l, int(name[-1])), "p")
            elif l + 1 < DEPTH:
                add(("ada", l + 1, n // 4, n % 4), "v")
                n += 1
    for l in range(DEPTH):
        for name, n in (("bin", 4), ("bout", 2)):
            for c in range(n):
                add((name, l, c), "p")
    return chunks, order


def build(
    nc, x, c, w_ada, b_ada, norm1_g, norm2_g, w_in, pool_w, pool_scale, q_norm_g, k_norm_g,
    attn_sinks, mix_norm_g, w_out, peer_wq, peer_subkeys, peer_u, peer_v, positions_2,
    attn_norm_2, w_in_2, b_f_2, q_norm_2, w_uq_2, kv_norm_2, w_ukv_2, fox_out_norm_2,
    mla_out_norm_2, w_o_2, ffn_norm_2, w_group_2, w_router_2, w_gate_2, w_up_2, w_down_2,
    final_norm_2, out,
):
    J, JORDER = psum_jobs()
    CH, CORDER = weight_chunks()

    with ExitStack() as ctx:
        def sb(name, n, dt=F32):
            return ctx.enter_context(nc.sbuf_tensor(name, [P, n], dt))

        def sem(name):
            return ctx.enter_context(nc.semaphore(name))

        arena = sb("arena", NCHUNK * CHUNK + 12288)
        mod = sb("mod", 12288)
        small = sb("small", 4224)
        X = sb("X", TT * D)[:].rearrange("p (t d) -> p t d", t=TT)
        HR = sb("HR", TT * D)[:].rearrange("p (t d) -> p t d", t=TT)
        HTF = sb("HT", KT * T)[:]
        HT = HTF.rearrange("p (k t) -> p k t", k=KT)
        HTB = HTF[:, 0:KT * 2 * BT].rearrange("p (k t) -> p k t", k=KT)
        JKT = sb("JK", 512)
        JUNK = JKT[:].bitcast(BF16)
        TMP = JKT[:]
        IDENT = sb("IDENT", P)[:]
        ONES = sb("ONES", P)[:]
        IDX = sb("IDX", TT * SLOTS, I32)[:].rearrange("p (t s) -> p t s", t=TT)
        GATE = sb("GATE", TT * SLOTS)[:].rearrange("p (t s) -> p t s", t=TT)
        SSQ = sb("SSQ", 32)[:]
        RT = sb("RT", 32)[:]
        RS = sb("RS", 32)[:]
        SV = sb("SV", 6 * 16)[:].rearrange("p (a t h) -> p a t h", a=6, t=TT)
        MX, NM, DEN, RD, SE, EXS = (SV[:, i] for i in range(6))
        SINK = sb("SINK", NH)[:]
        COND = sb("COND", KT)[:]
        EPST = sb("EPST", 1)[:]
        IOTA = sb("IOTA", TOPK)[:]
        COS = sb("COS", TT * 16)[:].rearrange("p (t f) -> p t f", t=TT)
        SIN = sb("SIN", TT * 16)[:].rearrange("p (t f) -> p t f", t=TT)
        STAGE = sb("STAGE", RING, I32)[:]
        DOT = sb("DOT", RING)[:]
        ACTV = sb("ACTV", RING)[:]
        UNUSED = sb("UNUSED", 1)[:]
        SLOT = sb("SLOT", 2 * BT)[:]
        PLAN = sb("PLAN", 16, I32)[:]
        RW = sb("RW", 64)[:]

        def view(buf, at, pattern, **kw):
            n = 1
            for v in kw.pop("shape"):
                n *= v
            return buf[:, at:at + n].rearrange(pattern, **kw)

        G0 = NCHUNK * CHUNK
        ring = [arena[:, s * CHUNK:(s + 1) * CHUNK] for s in range(NCHUNK)]

        def g3(at, a, b, buf=arena, base=G0):
            return buf[:, base + at:base + at + a * b].rearrange("p (a b) -> p a b", a=a)

        NGAIN = g3(0, 2, D)
        ZEROS = arena[:, G0 + 4096:G0 + 4096 + NX * BT // P * D]
        PROJ = g3(0, TT, IN_A)
        KD = arena[:, G0 + 2560:G0 + 3072].rearrange("p (t k u d) -> p t k u d", t=TT, k=NKV, u=2)
        QT = g3(3072, 4, T)
        KTA = g3(4096, NKV, T)
        S_A = [g3(4608, NH, P), g3(5632, NH, T)]
        PT_A = arena[:, G0 + 7680:G0 + 9728].rearrange("p (k h q) -> p k h q", k=2, h=NH)
        POOLT = g3(7680, 4, T)
        QSQ = arena[:, G0 + 5632:G0 + 6912]
        MIXG = arena[:, G0 + 10240:G0 + 11264]
        PSC = arena[:, G0 + 11264:G0 + 11776]
        SUBK = g3(11776, 2, NKEY)
        SUBT = g3(6144, 2, NKEY)
        QTP = g3(0, 16, T)
        SS = [g3(4096, 16, NKEY), g3(8704, 16, NKEY)]
        OH = arena[:, G0 + 10752:G0 + 11264].rearrange("p (h k c) -> p h k c", h=HQ, k=TOPK)
        CAND = g3(11264, HQ, 256)
        V16, I16, F16 = (g3(11776 + 64 * n, 2 * HQ, TOPK) for n in range(3))
        BV, BI, BU, BF, E1, E2 = (g3(11968 + 32 * n, HQ, TOPK) for n in range(6))
        I16, BI, BU = I16.bitcast(U32), BI.bitcast(U32), BU.bitcast(U32)
        GU = g3(0, RING, D)
        GV = g3(4096, RING, D)
        DIAG = g3(8192, RING, P)
        MODL = [mod[:, l * 6144:(l + 1) * 6144] for l in range(DEPTH)]

        def mrow(l, i):
            return MODL[l][:, i * D:(i + 1) * D]

        BIAS = small[:, 0:2048].rearrange("p (h s) -> p h s", h=NH)
        MT = small[:, 2048:3584].rearrange("p (g t) -> p g t", g=4)
        POOLW = small[:, 3584:4096].rearrange("p (g d) -> p g d", g=4)
        QKG = small[:, 4096:4224]
        UQ = small[:, 0:1536].rearrange("p (k n) -> p k n", k=2)
        UKV = small[:, 1536:2560]
        FN = small[:, 2560:3584]
        ON = mod[:, 0:1024]
        FINAL = mod[:, 1024:2048]
        QG = mod[:, 2048:2304]
        KG = mod[:, 2304:2432]
        BFB = mod[:, 2432:2440]
        GR = mod[:, 2440:2760].rearrange("p (k n) -> p k n", k=KT)
        FQT = g3(2760, 4, T, mod, 0)
        FKT = g3(3784, 4, T, mod, 0)
        FV = g3(4808, TT, 512, mod, 0)
        R = g3(5832, TT, REST, mod, 0)
        CT = g3(6680, 3, T, mod, 0)
        QM = mod[:, 7448:8984].rearrange("p (t h d) -> p t h d", t=TT, h=NH)
        KM = mod[:, 8984:10520].rearrange("p (t h d) -> p t h d", t=TT, h=NH)
        UTRI = g3(10520, TT, T, mod, 0)
        CMASK = mod[:, 11032:11288]
        RTMP = mod[:, 11288:12288]
        YO = g3(7448, 2, D // 2, mod, 0)
        GUO = g3(8472, 2, DE, mod, 0)
        SG = mod[:, 10264:10520].rearrange("p (b j t) -> p b j t", b=2, j=2)
        HH = mod[:, 8984:9240].rearrange("p (b j t) -> p b j t", b=2, j=2)
        SEL = mod[:, 9240:9752].rearrange("p (b t s) -> p b t s", b=2, t=TT)
        EQ = mod[:, 9752:10264].rearrange("p (t k s) -> p t k s", t=TT, k=2)
        YG = g3(8192, 2 * TT, D)
        ENUM = RW[:, 16:48]
        GK = RW[:, 4:8].rearrange("p (t k) -> p t k", t=TT)
        DREL = RW[:, 8:12].rearrange("p (t k) -> p t k", t=TT)
        DESTI = RW[:, 12:16].bitcast(I32)
        KV = arena[:, G0:G0 + 2048].rearrange("p (t h d) -> p t h d", t=TT, h=NH)
        QMT = g3(2048, NH, T)
        LFB = arena[:, G0 + 2048:G0 + 4096].rearrange("p (t h q) -> p t h q", t=TT, h=NH)
        KMT = g3(4096, NH, T)
        S_B = [g3(6144, NH, P), g3(7168, NH, T)]
        PT_B = arena[:, G0 + 9216:G0 + 11264].rearrange("p (k h q) -> p k h q", k=2, h=NH)
        SQB = arena[:, G0 + 7168:G0 + 9216]
        AN = mod[:, 2760:3784]
        ONEHOT = RTMP[:, 500:628].rearrange("p (k t e) -> p k t e", k=2, t=TT)
        PICKS = RTMP[:, 630:694].rearrange("p (t e) -> p t e", t=TT)
        EXP = [arena[:, at:at + EXP_F] for at in (0, 2 * CHUNK, 2 * CHUNK + EXP_F, 2 * CHUNK + 2 * EXP_F)]
        WG = [slot[:, 0:2048].rearrange("p (k f) -> p k f", k=KT) for slot in EXP]
        WU = [slot[:, 2048:4096].rearrange("p (k f) -> p k f", k=KT) for slot in EXP]
        WD = [slot[:, 4096:6144].rearrange("p (j d) -> p j d", j=2) for slot in EXP]

        PS = ctx.enter_context(nc.psum_tensor("PS", [P, 8, 512], F32))
        PO = PS[:, NBANK:NBANK + 2, :]

        psum_ready = sem("psum_ready")
        evac = {"v": sem("evac_by_vector"), "s": sem("evac_by_scalar")}
        vector_step = sem("vector_step")
        scalar_step = sem("scalar_step")
        pool_step = sem("pool_step")
        x_loaded = sem("x_loaded")
        cond_loaded = sem("cond_loaded")
        cond_ready = sem("cond_ready")
        gains_loaded = sem("gains_loaded")
        rows_cleared = sem("rows_cleared")
        bada_loaded = sem("bada_loaded")
        consts_ready = sem("consts_ready")
        second_squared = sem("second_squared")
        table_loaded = sem("table_loaded")
        acc_zeroed = sem("acc_zeroed")
        acc_ready = sem("acc_ready")
        params_loaded = sem("params_loaded")
        chunk_loaded = [sem(f"chunk_loaded{i}") for i in range(NCHUNK)]
        chunk_used = {"v": sem("chunk_used_by_vector"), "p": sem("chunk_used_by_tensor")}
        squares_ready = sem("squares_ready")
        root_ready = sem("root_ready")
        rows_ready = sem("rows_ready")
        qk_ready = sem("qk_ready")
        negmax_ready = sem("negmax_ready")
        probs_ready = sem("probs_ready")
        idx_ready = sem("idx_ready")
        gexp_in = sem("gexp_in")
        gexp_out = sem("gexp_out")
        staged = sem("staged")
        stage_seen = sem("stage_seen")
        u_loaded = [sem(f"u_loaded{i}") for i in range(RING)]
        v_loaded = [sem(f"v_loaded{i}") for i in range(RING)]
        dot_ready = sem("dot_ready")
        gelu_ready = sem("gelu_ready")
        diag_ready = sem("diag_ready")
        expert_added = sem("expert_added")
        sums_read = sem("sums_read")
        layer_done = sem("layer_done")
        logsig_in = sem("logsig_in")
        logsig_out = sem("logsig_out")
        decay_ready = sem("decay_ready")
        cn_ready = sem("cn_ready")
        mla_ready = sem("mla_ready")
        trig_in = sem("trig_in")
        trig_out = sem("trig_out")
        pos_loaded = sem("pos_loaded")
        expert_loaded = [sem(f"expert_loaded{i}") for i in range(EXP_RING)]
        sel_step = sem("sel_step")
        sel_ready = sem("sel_ready")
        picked = sem("picked")
        picked_out = sem("picked_out")
        gate_up_done = sem("gate_up_done")
        gate_up_out = sem("gate_up_out")
        turned = sem("turned")
        silu_done = sem("silu_done")
        hidden_ready = sem("hidden_ready")
        down_done = sem("down_done")
        y_out = sem("y_out")
        y_seen = sem("y_seen")
        y_stored = [sem(f"y_stored{i}") for i in range(2)]
        extra_stored = [[sem(f"extra_stored{l}{i}") for i in range(2)] for l in range(DEPTH)]
        plan_step = sem("plan_step")
        plan_ready = sem("plan_ready")
        y_gathered = sem("y_gathered")
        onehot_ready = sem("onehot_ready")
        router_in = sem("router_in")
        router_out = sem("router_out")
        out_ready = sem("out_ready")
        stored = sem("stored")

        def bank(name):
            return PS[:, J[name][1], :]

        def arrived(eng, name):
            eng.wait_ge(psum_ready, J[name][0] + 1)

        def taken(eng, name):
            eng.wait_ge(evac[J[name][2]], J[name][3] + 1)

        def loaded(eng, name):
            n, slot = CH[name][:2]
            eng.wait_ge(chunk_loaded[slot], 16 * (n // NCHUNK + 1))

        def row(ap, n):
            return ap.partition_broadcast(n)

        def if_extra(eng, l, extra, none):
            eng.wait_ge(plan_ready, 2 * l + 1)
            n = eng.value_load(PLAN[0:1, NX:NX + 1], min_val=0, max_val=NX)
            with eng.If(n > 0):
                extra()
            with eng.Else():
                none()

        def blocks(eng, l, body, flush, extra_counts):
            def run(first, count):
                for s in range(EXP_RING):
                    body(first, s, s)
                if count > 2:
                    with eng.Fori(first + 1, first + count) as i:
                        for s in range(EXP_RING):
                            body(i, s, EXP_RING)
                else:
                    for s in range(EXP_RING):
                        body(first + 1, s, EXP_RING)
                flush(first + count - 1, EXP_RING - 1)

            def none():
                for which, each in extra_counts:
                    eng.wait_ge(which, each * (l * NBX + NB))
                    eng.sem_inc(which, each * NX)

            run(0, NB // EXP_RING)
            if_extra(eng, l, lambda: run(NB // EXP_RING, NX // EXP_RING), none)

        def before(i, s, n):
            return (i, s - n) if s >= n else (i - 1, s - n + EXP_RING)

        Y = nc.dram_tensor("expert_rows", [NBX * BT, D], F32, kind="Internal").ap()

        block = ctx.enter_context(nc.Block())

        @block.sync
        def _(sp):
            def source(name):
                kind, l, c = name[:3]
                if kind == "ada":
                    return w_ada[l, name[3] * 256:(name[3] + 1) * 256, c * 2048:(c + 1) * 2048]
                w = {"in": w_in, "out": w_out, "wq": peer_wq, "bin": w_in_2, "bout": w_o_2}[kind]
                return w[l, :, c * 512:min((c + 1) * 512, w.shape[2])]

            with nc.allow_non_contiguous_dma(reason="small parameter vectors"):
                sp.dma_start(COND, c[0].rearrange("(k p) -> p k", p=P)).then_inc(cond_loaded, 16)
                sp.dma_start(RW[:, 0:TT].bitcast(I32), positions_2[0].rearrange("(t p) -> p t", p=P)).then_inc(pos_loaded, 16)
            for n, name in enumerate(CORDER):
                if n == 1:
                    sp.wait_ge(bada_loaded, 16)
                if n == NCHUNK:
                    sp.dma_start(X, x[0].rearrange("(t p) d -> p t d", p=P)).then_inc(x_loaded, 16)
                if n >= NCHUNK:
                    _, _, who, nth = CH[CORDER[n - NCHUNK]]
                    sp.wait_ge(chunk_used[who], nth + 1)
                if name[0] == "bin" and name[2] == 0 and name[1] > 0:
                    sp.wait_ge(y_gathered, 16 * 2 * TT * name[1])
                src = source(name).rearrange("(k p) n -> p k n", p=P)
                dst = ring[n % NCHUNK][:, 0:src.shape[1] * src.shape[2]].rearrange("p (k n) -> p k n", k=src.shape[1])
                sp.dma_start(dst, src).then_inc(chunk_loaded[n % NCHUNK], 16)
                if name[0] == "bout" and name[2] == 1:
                    l = name[1]
                    wg = w_gate_2.rearrange("l e (p k) f -> (l e) p (k f)", k=KT)
                    wu = w_up_2.rearrange("l e (p k) f -> (l e) p (k f)", k=KT)
                    wd = w_down_2.rearrange("l e (j p) d -> (l e) p j d", p=P)

                    def expert(e, s):
                        sp.dma_start(EXP[s][:, 0:2048], wg[bass.ds(e, 1)][0]).then_inc(expert_loaded[s], 16)
                        sp.dma_start(EXP[s][:, 2048:4096], wu[bass.ds(e, 1)][0]).then_inc(expert_loaded[s], 16)
                        sp.dma_start(WD[s], wd[bass.ds(e, 1)][0]).then_inc(expert_loaded[s], 16)

                    ahead = 1 - n % NCHUNK // 2
                    sp.wait_ge(chunk_used["p"], CH[("bin", l, 3)][3] + 1)
                    expert(l * NE + ahead, ahead)
                    sp.wait_ge(chunk_used["p"], CH[name][3] + 1)
                    for s in range(EXP_RING):
                        if s != ahead:
                            expert(l * NE + s, s)
                    with sp.Fori(1, NB // EXP_RING) as i:
                        for s in range(EXP_RING):
                            sp.wait_ge(down_done, i * EXP_RING + (l * NBX + s - EXP_RING + 1))
                            expert(i * EXP_RING + (l * NE + s), s)

                    def extra():
                        for x in range(NX):
                            e = sp.value_load(PLAN[0:1, x:x + 1], min_val=0, max_val=NE - 1)
                            sp.wait_ge(down_done, l * NBX + NB + x - EXP_RING + 1)
                            expert(e + l * NE, x % EXP_RING)

                    def none():
                        for s in range(EXP_RING):
                            sp.wait_ge(expert_loaded[s], 48 * (l * NBX + NB) // EXP_RING)
                            sp.sem_inc(expert_loaded[s], 48 * NX // EXP_RING)

                    if_extra(sp, l, extra, none)
            sp.wait_ge(out_ready, 2)
            sp.dma_start(out[0].rearrange("(t p) d -> p t d", p=P), HR).then_inc(stored, 16)
            sp.wait_ge(stored, 16)

        @block.gpsimd
        def _(pool):
            steps = [0]

            def go(ins):
                steps[0] += 1
                ins.then_inc(pool_step, 1)

            def sync():
                pool.wait_ge(pool_step, steps[0])

            def params(src_dst):
                for dst, src in src_dst:
                    pool.dma_start(dst, src).then_inc(params_loaded, 16)

            go(pool.memset(MODL[0][:, 0:3072], 0.0))
            sync()
            pool.wait_ge(acc_zeroed, 1)
            pool.dma_start(MODL[0][0:1, :], b_ada[0:1, :]).then_inc(bada_loaded, 16)
            go(pool.memset(mod[:, 6144:DEPTH * 6144], 0.0))
            go(pool.memset(ZEROS, 0.0))
            sync()
            pool.wait_ge(bada_loaded, 16)
            for l in range(1, DEPTH):
                pool.dma_start(MODL[l][0:1, :], b_ada[l:l + 1, :]).then_inc(bada_loaded, 16)
            pool.dma_start(NGAIN[:, 0], row(norm1_g[0], P)).then_inc(gains_loaded, 16)
            pool.dma_start(NGAIN[:, 1], row(norm2_g[0], P)).then_inc(gains_loaded, 16)
            pool.dma_start(Y[NB * BT:NBX * BT].rearrange("(p r) d -> p (r d)", p=P), ZEROS).then_inc(rows_cleared, 16)
            go(pool.memset(IDENT, 0.0))
            go(pool.memset(ONES, 1.0))
            go(pool.memset(EPST, EPS))
            go(pool.iota(IOTA, [[1, TOPK]], base=0, channel_multiplier=0, allow_small_or_imprecise_dtypes=True))
            go(pool.iota(BIAS, [[0, NH], [-1, 2 * P]], base=P, channel_multiplier=1, allow_small_or_imprecise_dtypes=True))
            sync()
            go(pool.affine_select(out=IDENT, in_=IDENT, compare_op=ALU.not_equal, fill=1.0, base=0,
                                  pattern=[[-1, P]], channel_multiplier=1))
            for h in range(NH):
                go(pool.tensor_scalar(BIAS[:, h], BIAS[:, h], -(2.0 ** (-8.0 * (h + 1) / NH)), None, ALU.mult))
            sync()
            go(pool.affine_select(out=BIAS, in_=BIAS, compare_op=ALU.is_ge, fill=MASKED, base=P,
                                  pattern=[[0, NH], [-1, 2 * P]], channel_multiplier=1))
            sync()
            go(pool.affine_select(out=BIAS, in_=BIAS, compare_op=ALU.is_ge, fill=MASKED, base=-1,
                                  pattern=[[0, NH], [1, 2 * P]], channel_multiplier=-1))
            for g, w in enumerate(WINDOWS):
                go(pool.memset(MT[:, g], 1.0 / w))
            sync()
            for g, w in enumerate(WINDOWS):
                for t in range(w - 1):
                    go(pool.memset(MT[:, g, t:t + 1], 1.0 / (t + 1)))
            sync()
            for part in (slice(0, T), slice(T, T + P)):
                n = part.stop - part.start
                go(pool.affine_select(out=MT[:, :, part], in_=MT[:, :, part], compare_op=ALU.is_ge, fill=0.0, base=0,
                                      pattern=[[0, 4], [1, n]], channel_multiplier=-1))
            sync()
            for part in (slice(0, T), slice(T, T + P)):
                n = part.stop - part.start
                for g, w in enumerate(WINDOWS):
                    go(pool.affine_select(out=MT[:, g, part], in_=MT[:, g, part], compare_op=ALU.is_ge, fill=0.0,
                                          base=w - 1, pattern=[[-1, n]], channel_multiplier=1))
            sync()
            for g in range(4):
                for at in (0, T):
                    go(pool.tensor_tensor(MT[:, g, at:at + P], MT[:, g, at:at + P], IDENT, ALU.subtract))
            sync()
            pool.wait_ge(rows_cleared, 16)
            pool.sem_inc(consts_ready, 1)

            u_rows = peer_u.rearrange("l n d -> (l n) d")
            v_rows = peer_v.rearrange("l n d -> (l n) d")

            def params_of_b(l):
                with nc.allow_non_contiguous_dma(reason="small parameter vectors"):
                    params([
                        (AN, row(attn_norm_2[l], P)), (FN, row(ffn_norm_2[l], P)),
                        (BFB, row(b_f_2[l], P)), (QG, row(q_norm_2[l], P)), (KG, row(kv_norm_2[l], P)),
                        (ON[:, 0:512], row(fox_out_norm_2[l], P)), (ON[:, 512:1024], row(mla_out_norm_2[l], P)),
                        (UQ, w_uq_2[l].rearrange("(k p) n -> p k n", p=P)), (UKV, w_ukv_2[l]),
                        (GR[:, :, 0:NG], w_group_2[l].rearrange("(p k) n -> p k n", k=KT)),
                        (GR[:, :, NG:NG + NE], w_router_2[l].rearrange("(p k) n -> p k n", k=KT)),
                    ])

            for l in range(DEPTH):
                if l:
                    pool.wait_ge(layer_done, l)
                with nc.allow_non_contiguous_dma(reason="small parameter vectors"):
                    params([
                        (QKG[:, 0:HD], row(q_norm_g[l], P)), (QKG[:, HD:2 * HD], row(k_norm_g[l], P)),
                        (SINK, row(attn_sinks[l], P)), (MIXG, row(mix_norm_g[l], P)), (PSC, row(pool_scale[l], P)),
                        (POOLW, pool_w[l].rearrange("g c d -> c g d")),
                        (SUBK, peer_subkeys[l].rearrange("q n d -> n q d")),
                    ])
                for tt in range(TT):
                    pool.wait_ge(idx_ready, NQ * (l * TT + tt + 1))
                    arrived(pool, ("s", l, TT - 1, NQ - 1))
                    if tt == 0 and l + 1 < DEPTH:
                        pool.dma_start(HTF[:, 0:D], row(norm1_g[l + 1], P)).then_inc(gains_loaded, 16)
                        pool.dma_start(HTF[:, D:2 * D], row(norm2_g[l + 1], P)).then_inc(gains_loaded, 16)
                    base = (l * TT + tt) * SLOTS

                    def gather(i, s):
                        pool.wait_ge(u_loaded[s], i * 16 + (base // RING) * 16) if (base or not isinstance(i, int)) else None
                        pool.wait_ge(v_loaded[s], i * 16 + (base // RING) * 16) if (base or not isinstance(i, int)) else None
                        pool.wait_ge(dot_ready, i * RING + (base + s + 1))
                        pool.wait_ge(expert_added, i * RING + (base + s + 1))
                        pool.tensor_copy(STAGE[:, s:s + 1], IDX[:, tt, bass.ds(i * RING + s, 1)]).then_inc(staged, 1)
                        pool.wait_ge(staged, i * RING + (base + s + 1))
                        pool.sem_inc(stage_seen, 1)
                        off = bass.IndirectOffsetOnAxis(ap=STAGE[:, s:s + 1], axis=0)
                        pool.indirect_dma_start(out=GU[:, s, :], out_offset=None, in_=u_rows, in_offset=off).then_inc(u_loaded[s], 16)
                        pool.indirect_dma_start(out=GV[:, s, :], out_offset=None, in_=v_rows, in_offset=off).then_inc(v_loaded[s], 16)

                    for s in range(RING):
                        gather(0, s)
                    if l == DEPTH - 1 and tt == 0:
                        params([(FINAL, row(final_norm_2, P))])
                        params_of_b(0)
                    with pool.Fori(1, SLOTS // RING) as i:
                        for s in range(RING):
                            gather(i, s)

            for l in range(DEPTH):
                if l == 0:
                    pool.wait_ge(layer_done, DEPTH)
                    go(pool.memset(UTRI, 1.0))
                    go(pool.memset(CMASK, 0.0))
                    go(pool.iota(SLOT, [[1, 2 * BT]], base=0, channel_multiplier=0, allow_small_or_imprecise_dtypes=True))
                    go(pool.iota(ENUM, [[1, NE]], base=0, channel_multiplier=0, allow_small_or_imprecise_dtypes=True))
                    go(pool.iota(RW[:, 48:56], [[1, 8]], base=0, channel_multiplier=0, allow_small_or_imprecise_dtypes=True))
                    sync()
                    go(pool.affine_select(out=UTRI, in_=UTRI, compare_op=ALU.is_ge, fill=0.0, base=0,
                                          pattern=[[-P, TT], [1, T]], channel_multiplier=-1))
                    go(pool.affine_select(out=CMASK[:, P:2 * P], in_=CMASK[:, P:2 * P], compare_op=ALU.is_ge,
                                          fill=MASKED, base=0, pattern=[[-1, P]], channel_multiplier=1))
                    sync()
                    pool.sem_inc(consts_ready, 1)

                def store(i, s, done):
                    b = i * EXP_RING + s
                    pool.wait_ge(y_out, b + l * NBX + 1)
                    pool.sem_inc(y_seen, 1)
                    for c in range(2):
                        pool.dma_start(Y[bass.ds(b * BT, BT), c * 512:(c + 1) * 512],
                                       YO[c * BT:(c + 1) * BT, s % 2]).then_inc(done[s % 2], 16)

                def extra():
                    for b in range(NX):
                        store((NB + b) // EXP_RING, b % EXP_RING, extra_stored[l])
                    for k in range(2):
                        pool.wait_ge(extra_stored[l][k], 32 * NX // 2)

                if l < DEPTH - 1:
                    pool.wait_ge(plan_ready, 2 * l + 2)
                    params_of_b(l + 1)
                with pool.Fori(0, NB // EXP_RING) as i:
                    for s in range(EXP_RING):
                        store(i, s, y_stored)
                if_extra(pool, l, extra, lambda: None)
                for k in range(2):
                    pool.wait_ge(y_stored[k], 32 * (l + 1) * NB // 2)
                pool.wait_ge(plan_ready, 2 * l + 2)
                for n in range(2 * TT):
                    pool.indirect_dma_start(out=YG[:, n, :], out_offset=None, in_=Y,
                                            in_offset=bass.IndirectOffsetOnAxis(ap=DESTI[:, n:n + 1], axis=0)).then_inc(y_gathered, 16)

        @block.scalar
        def _(act):
            steps = [0]
            roots, tables, x_roots = [0], [0], [0]
            maxes = [0]

            def go(ins):
                steps[0] += 1
                ins.then_inc(scalar_step, 1)

            def sync():
                act.wait_ge(scalar_step, steps[0])

            def copy_out(name, dst, src):
                arrived(act, name)
                act.activation(dst, src, ACT.Copy).then_inc(evac["s"], 1)

            def prepare(function):
                act.activation(UNUSED, EPST, function).then_inc(table_loaded, 1)
                tables[0] += 1
                act.wait_ge(table_loaded, tables[0])

            def root(parts, of_x=False):
                roots[0] += 1
                if of_x:
                    prepare(ACT.Sqrt)
                act.wait_ge(squares_ready, roots[0])
                if of_x:
                    go(act.activation(JUNK, X[:, 0], ACT.Square, accum_out=SSQ[:, 0:1]))
                    sync()
                    x_roots[0] += 1
                    act.wait_ge(second_squared, x_roots[0])
                for a, b, n in parts:
                    last = act.activation(RT[:, a:b], SSQ[:, a:b], ACT.Sqrt, bias=EPST, scale=1.0 / n)
                    if b != parts[-1][1]:
                        go(last)
                        sync()
                last.then_inc(root_ready, 1)

            def exps(S, sink):
                for tt in range(TT):
                    maxes[0] += 1
                    act.wait_ge(negmax_ready, maxes[0])
                    for h in range(NH):
                        act.activation(S[tt][:, h, :], S[tt][:, h, :], ACT.Exp, bias=NM[:, tt, h:h + 1],
                                       accum_out=DEN[:, tt, h:h + 1]).then_inc(probs_ready, 1)
                    if sink:
                        act.activation(EXS[:, tt], SE[:, tt], ACT.Exp).then_inc(probs_ready, 1)

            def transposed_probs(kind, l, PTX):
                for tt in range(TT):
                    for b in range(2 * (tt + 1)):
                        kt, h = divmod(4 * b, NH)
                        copy_out((kind + "pT", l, tt, b), PTX[:, kt, h:h + 4, :],
                                 bank((kind + "pT", l, tt, b)).rearrange("p (h q) -> p h q", h=4))

            def rows_transposed(kind, l):
                for tt in range(TT):
                    for half in range(2):
                        copy_out((kind, l, tt, half), HT[:, 4 * half:4 * half + 4, tt * P:(tt + 1) * P],
                                 bank((kind, l, tt, half)).rearrange("p (k t) -> p k t", k=4))

            act.wait_ge(cond_loaded, 16)
            act.activation(COND, COND, ACT.Silu).then_inc(cond_ready, 1)
            for n, table in enumerate((SIN, COS)):
                act.wait_ge(trig_in, n + 1)
                act.activation(table, table, ACT.Sin).then_inc(trig_out, 1)
            act.wait_ge(consts_ready, 1)
            root([(0, TT, D)], of_x=True)
            for n in range(12):
                if J[("ada", 0, n)][2] == "s":
                    copy_out(("ada", 0, n), MODL[0][:, n * 512:(n + 1) * 512], bank(("ada", 0, n)))

            for l in range(DEPTH):
                if l:
                    root([(0, TT, D)], of_x=True)
                rows_transposed("hT", l)
                for c in range(3):
                    n = min(512, IN_A - c * 512)
                    for tt in range(TT):
                        copy_out(("in", l, c, tt), PROJ[:, tt, c * 512:c * 512 + n], bank(("in", l, c, tt))[:, 0:n])
                for b in range(2):
                    copy_out(("pool", l, b), POOLT[:, 2 * b:2 * b + 2, :],
                             bank(("pool", l, b)).rearrange("p (g t) -> p g t", g=2))
                root([(0, 20, HD)])
                for tt in range(TT):
                    copy_out(("qT", l, tt), QT[:, :, tt * P:(tt + 1) * P],
                             bank(("qT", l, tt)).rearrange("p (k t) -> p k t", k=4))
                copy_out(("kT", l), KTA, bank(("kT", l)).rearrange("p (k t) -> p k t", k=NKV))
                exps(S_A, True)
                transposed_probs("a", l, PT_A)
                root([(0, 4, 512)])
                rows_transposed("yT", l)
                copy_out(("subT", l), SUBT, bank(("subT", l))[:, 0:256].rearrange("p (k t) -> p k t", k=2))
                root([(0, TT, D)], of_x=True)
                rows_transposed("h2T", l)

                def scores_out(c):
                    for tt in range(TT):
                        copy_out(("s", l, tt, c), SS[tt][:, 4 * c:4 * c + 4, :],
                                 bank(("s", l, tt, c)).rearrange("p (g t) -> p g t", g=4))

                for b in range(2 * NQ):
                    copy_out(("wq", l, b), QTP[:, 2 * b:2 * b + 2, :],
                             bank(("wq", l, b)).rearrange("p (g t) -> p g t", g=2))
                    if b % 2 == 0 and b:
                        scores_out(b // 2 - 1)
                scores_out(NQ - 1)
                if l + 1 < DEPTH:
                    for n in range(12):
                        copy_out(("ada", l + 1, n), MODL[l + 1][:, n * 512:(n + 1) * 512], bank(("ada", l + 1, n)))
                for tt in range(TT):
                    base = (l * TT + tt) * SLOTS
                    act.wait_ge(gexp_in, l * TT + tt + 1)
                    act.activation(GATE[:, tt], GATE[:, tt], ACT.Exp).then_inc(gexp_out, 1)
                    with act.Fori(0, SLOTS // RING) as i:
                        for s in range(RING):
                            act.wait_ge(dot_ready, i * RING + (base + s + 1 + RING))
                            act.activation(ACTV[:, s:s + 1], DOT[:, s:s + 1], ACT.Gelu).then_inc(gelu_ready, 1)

            for l in range(DEPTH):
                root([(0, TT, D)], of_x=True)
                rows_transposed("bhT", l)
                for b in range(4):
                    dst = (FQT, FKT)[b // 2]
                    copy_out(("fqk", l, b), dst[:, 2 * (b % 2):2 * (b % 2) + 2, :],
                             bank(("fqk", l, b)).rearrange("p (g t) -> p g t", g=2))
                for tt in range(TT):
                    copy_out(("fv", l, tt), FV[:, tt], bank(("fv", l, tt)))
                act.wait_ge(logsig_in, l + 1)
                z = RTMP[:, 16:32]
                go(act.activation(z, z, ACT.Exp, scale=-1.0))
                sync()
                act.activation(z, z, ACT.Ln, bias=ONES[:, 0:1]).then_inc(logsig_out, 1)
                root([(0, 2, QL), (2, 4, KVL)])
                for tt in range(TT):
                    copy_out(("cT", l, tt), CT[:, :, tt * P:(tt + 1) * P],
                             bank(("cT", l, tt))[:, 0:384].rearrange("p (k t) -> p k t", k=3))
                for tt in range(TT):
                    q = QM[:, tt].rearrange("p h d -> p (h d)")
                    kv = KV[:, tt].rearrange("p h d -> p (h d)")
                    for c in range(2):
                        n = min(512, 768 - 512 * c)
                        copy_out(("uq", l, tt, c), q[:, 512 * c:512 * c + n], bank(("uq", l, tt, c))[:, 0:n])
                    for c in range(2):
                        copy_out(("ukv", l, tt, c), kv[:, 512 * c:512 * c + 512], bank(("ukv", l, tt, c)))
                exps(S_B, False)
                transposed_probs("f", l, PT_B)
                for name, dst in (("qmT", QMT), ("kmT", KMT)):
                    for tt in range(TT):
                        for b in range(2):
                            copy_out((name, l, tt, b), dst[0:DK, 4 * b:4 * b + 4, tt * P:(tt + 1) * P],
                                     bank((name, l, tt, b))[0:DK].rearrange("p (g t) -> p g t", g=4))
                exps(S_B, False)
                transposed_probs("m", l, PT_B)
                root([(0, 32, HD)])
                rows_transposed("byT", l)
                root([(0, TT, D)], of_x=True)
                rows_transposed("fhT", l)
                for n in range(2):
                    act.wait_ge(router_in, 2 * l + n + 1)
                    z = RTMP[:, 100:116] if n == 0 else RTMP[:, 200:202]
                    act.activation(z, z, ACT.Exp).then_inc(router_out, 1)

                def silu(i, s):
                    b = i * EXP_RING + (l * NBX + s)
                    act.wait_ge(turned, b + 1)
                    gates = PS[:, 6 + s % 2, 0:2 * P].rearrange("p (j t) -> p j t", j=2)[:, :, 0:BT]
                    act.activation(SG[:, s % 2], gates, ACT.Silu).then_inc(silu_done, 1)

                def body(i, s, n):
                    if n:
                        silu(*before(i, s, 1))
                    if s % 2 == 0:
                        for c in range(2):
                            act.wait_ge(picked, i * EXP_RING + (l * NBX + s + c + 1))
                            act.activation(HTB[:, c * 4:(c + 1) * 4].rearrange("p k t -> p (k t)"), PS[:, c, :],
                                           ACT.Copy).then_inc(picked_out, 1)

                blocks(act, l, body, silu, [(picked_out, 1), (silu_done, 1)])
            root([(0, TT, D)], of_x=True)

        @block.tensor
        def _(pe):
            rows = [0]
            probs = [0]

            def begin(name):
                n = J[name][0]
                if n >= NBANK:
                    taken(pe, JORDER[n - NBANK])

            def transpose_rows(kind, l):
                rows[0] += 1
                for tt in range(TT):
                    pe.wait_ge(rows_ready, 4 * (rows[0] - 1) + 2 * (tt + 1))
                    for half in range(2):
                        begin((kind, l, tt, half))
                        for k in range(4):
                            kk = 4 * half + k
                            last = pe.transpose(bank((kind, l, tt, half))[:, k * P:(k + 1) * P],
                                                HR[:, tt, kk * P:(kk + 1) * P], IDENT)
                        last.then_inc(psum_ready, 1)

            def project(job, l, wname, c, n, order=range(TT)):
                loaded(pe, (wname, l, c))
                w = ring[CH[(wname, l, c)][1]][:, 0:KT * n].rearrange("p (k n) -> p k n", k=KT)
                for tt in order:
                    name = job(tt)
                    begin(name)
                    for k in range(KT):
                        last = pe.matmul(bank(name)[:, 0:n], HT[:, k, tt * P:(tt + 1) * P], w[:, k, :],
                                         start=(k == 0), stop=(k == KT - 1))
                    last.then_inc(psum_ready, 1)

            def release():
                pe.sem_inc(chunk_used["p"], 1)

            def weights_first(name, l, wname, c, cols, first, final):
                if first:
                    loaded(pe, (wname, l, c))
                w = ring[CH[(wname, l, c)][1]][:, :].rearrange("p (k n) -> p k n", k=KT)
                begin(name)
                for j in range(2):
                    at = cols + j * P
                    for k in range(KT):
                        last = pe.matmul(bank(name)[:, j * T:(j + 1) * T], w[:, k, at:at + P], HT[:, k, :],
                                         start=(k == 0), stop=(k == KT - 1))
                last.then_inc(psum_ready, 1)

            def attend(kind, l, S, PTX, score, value, sink):
                for tt in range(TT):
                    nk = (tt + 1) * P
                    per = 512 // nk
                    for b in range(NH // per):
                        name = (kind + "sc", l, tt, b)
                        begin(name)
                        for j in range(per):
                            h = first_head(b, per) + 2 * j
                            last = score(bank(name)[:, j * nk:(j + 1) * nk], h, tt, nk)
                        last.then_inc(psum_ready, 1)
                for tt in range(TT):
                    probs[0] += NH + sink
                    pe.wait_ge(probs_ready, probs[0])
                    for b in range(2 * (tt + 1)):
                        name = (kind + "pT", l, tt, b)
                        begin(name)
                        kt, h = divmod(4 * b, NH)
                        for j in range(4):
                            last = pe.transpose(bank(name)[:, j * P:(j + 1) * P],
                                                S[tt][:, h + j, kt * P:(kt + 1) * P], IDENT)
                        last.then_inc(psum_ready, 1)
                    begin((kind + "pv", l, tt))
                    taken(pe, (kind + "pT", l, tt, 2 * (tt + 1) - 1))
                    for h in range(NH):
                        for kt in range(tt + 1):
                            last = pe.matmul(bank((kind + "pv", l, tt))[:, h * HD:(h + 1) * HD], PTX[:, kt, h, :],
                                             value(kt, h), start=(kt == 0), stop=(kt == tt))
                    last.then_inc(psum_ready, 1)

            pe.sem_inc(expert_added, RING)
            pe.wait_ge(consts_ready, 1)
            def modulation(l):
                pe.wait_ge(acc_ready, l + 1)
                for n in range(12):
                    begin(("ada", l, n))
                    pe.matmul(bank(("ada", l, n)), ONES, MODL[l][:, n * 512:(n + 1) * 512],
                              start=True, stop=True).then_inc(psum_ready, 1)

            modulation(0)

            for l in range(DEPTH):
                transpose_rows("hT", l)
                taken(pe, ("hT", l, 1, 1))
                for c in range(3):
                    project(lambda tt: ("in", l, c, tt), l, "in", c, min(512, IN_A - 512 * c))
                    arrived(pe, ("in", l, c, 1))
                    release()
                pe.wait_ge(params_loaded, 16 * 7 * (l + 1))
                taken(pe, ("in", l, 0, 1))
                for b in range(2):
                    begin(("pool", l, b))
                    for j in range(2):
                        g = 2 * b + j
                        to = bank(("pool", l, b))[:, j * T:(j + 1) * T]
                        pe.matmul(to, PROJ[:, 0, g * P:(g + 1) * P], MT[:, g, 0:T], start=True, stop=False)
                        last = pe.matmul(to[:, P:T], PROJ[:, 1, g * P:(g + 1) * P], MT[:, g, T:T + P],
                                         start=False, stop=True)
                    last.then_inc(psum_ready, 1)
                taken(pe, ("pool", l, 1))
                for tt in range(TT):
                    begin(("mix", l, tt))
                    for g in range(4):
                        last = pe.matmul(bank(("mix", l, tt))[:, g * P:(g + 1) * P], POOLT[:, g, tt * P:(tt + 1) * P],
                                         POOLW[:, g, :], start=True, stop=True)
                    last.then_inc(psum_ready, 1)
                pe.wait_ge(qk_ready, 3 * (l + 1))
                for tt in range(TT):
                    begin(("qT", l, tt))
                    for j in range(4):
                        last = pe.transpose(bank(("qT", l, tt))[:, j * P:(j + 1) * P],
                                            PROJ[:, tt, POOL + j * P:POOL + (j + 1) * P], IDENT)
                    last.then_inc(psum_ready, 1)
                begin(("kT", l))
                for kv in range(NKV):
                    for tt in range(TT):
                        at = kv * T + tt * P
                        last = pe.transpose(bank(("kT", l))[:, at:at + P],
                                            KD[:, tt, kv].rearrange("p u d -> p (u d)"), IDENT)
                last.then_inc(psum_ready, 1)
                taken(pe, ("kT", l))

                def score(to, h, tt, nk):
                    at = HD * (h % 2)
                    return pe.matmul(to, QT[at:at + HD, h // 2, tt * P:(tt + 1) * P],
                                     KTA[at:at + HD, h // (NH // NKV), 0:nk], start=True, stop=True)

                attend("a", l, S_A, PT_A, score,
                       lambda kt, h: PROJ[:, kt, 1152 + (h // 4) * HD:1152 + (h // 4 + 1) * HD], 1)
                transpose_rows("yT", l)
                taken(pe, ("yT", l, 1, 1))
                for c in range(2):
                    project(lambda tt: ("out", l, c, tt), l, "out", c, 512)
                    arrived(pe, ("out", l, c, 1))
                    release()
                begin(("subT", l))
                for q in range(2):
                    last = pe.transpose(bank(("subT", l))[:, q * P:(q + 1) * P], SUBK[:, q, :], IDENT)
                last.then_inc(psum_ready, 1)
                transpose_rows("h2T", l)
                taken(pe, ("h2T", l, 1, 1))

                def key_scores(c):
                    taken(pe, ("wq", l, 2 * c + 1))
                    for tt in range(TT):
                        begin(("s", l, tt, c))
                        for j in range(4):
                            hp = 4 * c + j
                            last = pe.matmul(bank(("s", l, tt, c))[:, j * P:(j + 1) * P],
                                             QTP[:, hp, tt * P:(tt + 1) * P], SUBT[:, hp % 2, :],
                                             start=True, stop=True)
                        last.then_inc(psum_ready, 1)

                for c in range(NQ):
                    weights_first(("wq", l, 2 * c), l, "wq", c, 0, True, False)
                    if c:
                        key_scores(c - 1)
                    weights_first(("wq", l, 2 * c + 1), l, "wq", c, 2 * P, False, True)
                    arrived(pe, ("wq", l, 2 * c + 1))
                    release()
                key_scores(NQ - 1)
                if l + 1 < DEPTH:
                    modulation(l + 1)
                for tt in range(TT):
                    base = (l * TT + tt) * SLOTS

                    def add(i, s, first=False):
                        pe.wait_ge(v_loaded[s], i * 16 + (base // RING + 1) * 16)
                        pe.wait_ge(diag_ready, i * RING + (base + s + 1))
                        for half in range(2):
                            last = pe.matmul(PO[:, half, :], DIAG[:, s, :], GV[:, s, half * 512:(half + 1) * 512],
                                             start=first, stop=False, skip_group_check=True)
                        last.then_inc(expert_added, 1)

                    if base:
                        pe.wait_ge(sums_read, 2 * (l * TT + tt))
                    for s in range(RING):
                        add(0, s, s == 0)
                    with pe.Fori(1, SLOTS // RING) as i:
                        for s in range(RING):
                            add(i, s)

            for l in range(DEPTH):
                transpose_rows("bhT", l)
                taken(pe, ("bhT", l, 1, 1))
                for c in range(2):
                    for j in range(2):
                        weights_first(("fqk", l, 2 * c + j), l, "bin", c, 2 * P * j, j == 0, j == 1)
                    arrived(pe, ("fqk", l, 2 * c + 1))
                    release()
                project(lambda tt: ("fv", l, tt), l, "bin", 2, 512)
                arrived(pe, ("fv", l, 1))
                release()
                project(lambda tt: ("rest", l, tt), l, "bin", 3, REST)
                arrived(pe, ("rest", l, 1))
                release()
                pe.wait_ge(cn_ready, 4 * (l + 1))
                for tt in range(TT):
                    begin(("cT", l, tt))
                    for j in range(3):
                        last = pe.transpose(bank(("cT", l, tt))[:, j * P:(j + 1) * P],
                                            R[:, tt, 8 + j * P:8 + (j + 1) * P], IDENT)
                    last.then_inc(psum_ready, 1)
                for tt in range(TT):
                    taken(pe, ("cT", l, tt))
                    for c in range(2):
                        n = min(512, 768 - 512 * c)
                        begin(("uq", l, tt, c))
                        for k in range(2):
                            last = pe.matmul(bank(("uq", l, tt, c))[:, 0:n], CT[:, k, tt * P:(tt + 1) * P],
                                             UQ[:, k, 512 * c:512 * c + n], start=(k == 0), stop=(k == 1))
                        last.then_inc(psum_ready, 1)
                    for c in range(2):
                        begin(("ukv", l, tt, c))
                        pe.matmul(bank(("ukv", l, tt, c)), CT[:, 2, tt * P:(tt + 1) * P],
                                  UKV[:, 512 * c:512 * c + 512], start=True, stop=True).then_inc(psum_ready, 1)
                pe.wait_ge(decay_ready, l + 1)
                if l == 0:
                    pe.wait_ge(consts_ready, 2)

                def fox_score(to, h, tt, nk):
                    at = HD * (h % 2)
                    pe.matmul(to, FQT[at:at + HD, h // 2, tt * P:(tt + 1) * P], FKT[at:at + HD, h // 2, 0:nk],
                              start=True, stop=False)
                    for k in range(tt + 1):
                        last = pe.matmul(to, LFB[:, k, h, :], UTRI[:, k, 0:nk], start=False, stop=(k == tt))
                    return last

                attend("f", l, S_B, PT_B, fox_score, lambda kt, h: FV[:, kt, h * HD:(h + 1) * HD], 0)
                pe.wait_ge(mla_ready, 2 * (l + 1))
                for name, src in (("qmT", QM), ("kmT", KM)):
                    for tt in range(TT):
                        for b in range(2):
                            begin((name, l, tt, b))
                            for j in range(4):
                                last = pe.transpose(bank((name, l, tt, b))[0:DK, j * P:(j + 1) * P],
                                                    src[:, tt, 4 * b + j, :], IDENT)
                            last.then_inc(psum_ready, 1)
                taken(pe, ("kmT", l, 1, 1))

                def mla_score(to, h, tt, nk):
                    return pe.matmul(to, QMT[0:DK, h, tt * P:(tt + 1) * P], KMT[0:DK, h, 0:nk], start=True, stop=True)

                attend("m", l, S_B, PT_B, mla_score, lambda kt, h: KV[:, kt, h, HD:2 * HD], 0)
                transpose_rows("byT", l)
                taken(pe, ("byT", l, 1, 1))
                for c in range(2):
                    project(lambda tt: ("bout", l, c, tt), l, "bout", c, 512)
                    arrived(pe, ("bout", l, c, 1))
                    release()
                transpose_rows("fhT", l)
                taken(pe, ("fhT", l, 1, 1))
                for tt in range(TT):
                    begin(("route", l, tt))
                    for k in range(KT):
                        last = pe.matmul(bank(("route", l, tt))[:, 0:NG + NE], HT[:, k, tt * P:(tt + 1) * P],
                                         GR[:, k, :], start=(k == 0), stop=(k == KT - 1))
                    last.then_inc(psum_ready, 1)
                pe.wait_ge(onehot_ready, l + 1)
                begin(("rank", l))
                rank = bank(("rank", l))[:, 0:3 * NE].rearrange("p (n e) -> p n e", e=NE)
                for n, terms in enumerate((
                    [(UTRI[:, 0, 0:P], 0)], [(UTRI[:, 0, P:T], 0), (UTRI[:, 1, P:T], 1)], [(ONES, 0), (ONES, 1)],
                )):
                    for m, (ones, tt) in enumerate(terms):
                        last = pe.matmul(rank[:, n], ones, PICKS[:, tt], start=(m == 0), stop=(m == len(terms) - 1))
                last.then_inc(psum_ready, 1)
                taken(pe, ("rank", l))

                def down(i, s):
                    b = i * EXP_RING + (l * NBX + s)
                    pe.wait_ge(hidden_ready, b + 1)
                    if l or s > 1 or not isinstance(i, int) or i:
                        pe.wait_ge(y_out, b - 1)
                    for j in range(2):
                        for c in range(2):
                            last = pe.matmul(PS[c * BT:(c + 1) * BT, 4 + s % 2, :], HH[:, s % 2, j, :],
                                             WD[s][:, j, c * 512:(c + 1) * 512], start=(j == 0), stop=(j == 1))
                    last.then_inc(down_done, 1)

                def turn(i, s):
                    b = i * EXP_RING + (l * NBX + s)
                    pe.wait_ge(gate_up_out, b + 1)
                    for j in range(2):
                        last = pe.transpose(PS[:, 6 + s % 2, j * P:(j + 1) * P], GUO[:, s % 2, j * P:(j + 1) * P], IDENT)
                    last.then_inc(turned, 1)

                def body(i, s, n):
                    b = i * EXP_RING + (l * NBX + s)
                    if n > 1:
                        down(*before(i, s, 2))
                    if n:
                        turn(*before(i, s, 1))
                    if s % 2 == 0:
                        pe.wait_ge(sel_ready, b + 2)
                        for k in range(KT):
                            for tt in range(TT):
                                last = pe.matmul(PS[:, k // 4, (k % 4) * P:(k % 4 + 1) * P], HR[:, tt, k * P:(k + 1) * P],
                                                 SEL[:, s // 2, tt, :], start=(tt == 0), stop=(tt == 1))
                            if k % 4 == 3:
                                last.then_inc(picked, 1)
                    if isinstance(i, int):
                        pe.wait_ge(expert_loaded[s], (l * NBX // EXP_RING + i + 1) * 48)
                    else:
                        pe.wait_ge(expert_loaded[s], i * 48 + (l * NBX // EXP_RING + 1) * 48)
                    for k in range(KT):
                        if s % 2 == 0 and k % 4 == 0:
                            pe.wait_ge(picked_out, b + k // 4 + 1)
                        for c, w in enumerate((WG[s], WU[s])):
                            last = pe.matmul(PS[c * BT:(c + 1) * BT, 2 + s % 2, 0:DE], HTB[:, k, (s % 2) * BT:(s % 2 + 1) * BT],
                                             w[:, k, :], start=(k == 0), stop=(k == KT - 1))
                    last.then_inc(gate_up_done, 1)

                def flush(i, s):
                    down(*before(i, s, 1))
                    turn(i, s)
                    down(i, s)

                blocks(pe, l, body, flush, [(picked, 1), (gate_up_done, 1), (turned, 1), (down_done, 1)])

        @block.vector
        def _(dve):
            steps = [0]
            roots = [0]
            atts = [0]
            probs = [0]

            def go(ins):
                steps[0] += 1
                ins.then_inc(vector_step, 1)

            def sync():
                dve.wait_ge(vector_step, steps[0])

            def step(ins):
                go(ins)
                sync()

            def root(n):
                dve.sem_inc(squares_ready, 1)
                if n == TT:
                    dve.tensor_tensor_reduce(HR[:, 1], X[:, 1], X[:, 1], 1.0, 0.0, ALU.mult, ALU.add,
                                             SSQ[:, 1:2]).then_inc(second_squared, 1)
                roots[0] += 1
                dve.wait_ge(root_ready, roots[0])
                step(dve.reciprocal(RS[:, 0:n], RT[:, 0:n]))

            def attention_rows(kind, l, S, scale, bias, sink):
                for tt in range(TT):
                    nk = (tt + 1) * P
                    per = 512 // nk
                    for b in range(NH // per):
                        name = (kind + "sc", l, tt, b)
                        arrived(dve, name)
                        heads = slice(first_head(b, per), first_head(b, per) + 2 * per - 1, 2)
                        dve.scalar_tensor_tensor(S[tt][:, heads, :],
                                                 bank(name).rearrange("p (h s) -> p h s", h=per), scale,
                                                 bias(tt, heads, per, nk), ALU.mult, ALU.add).then_inc(evac["v"], 1)
                    taken(dve, name)
                    step(dve.tensor_reduce(MX[:, tt], S[tt], AX, ALU.max))
                    if sink:
                        step(dve.tensor_tensor(MX[:, tt], MX[:, tt], SINK, ALU.max))
                        step(dve.tensor_tensor(SE[:, tt], SINK, MX[:, tt], ALU.subtract))
                    dve.tensor_scalar(NM[:, tt], MX[:, tt], -1.0, None, ALU.mult).then_inc(negmax_ready, 1)
                    atts[0] += 1
                    dve.wait_ge(negmax_ready, atts[0])

            def attention_values(kind, l, at, sink):
                for tt in range(TT):
                    probs[0] += NH + sink
                    dve.wait_ge(probs_ready, probs[0])
                    if sink:
                        step(dve.tensor_tensor(DEN[:, tt], DEN[:, tt], EXS[:, tt], ALU.add))
                    step(dve.reciprocal(RD[:, tt], DEN[:, tt]))
                    arrived(dve, (kind + "pv", l, tt))
                    dve.tensor_tensor(HR[:, tt, at:at + 512].rearrange("p (h d) -> p h d", h=NH),
                                      bank((kind + "pv", l, tt)).rearrange("p (h d) -> p h d", h=NH),
                                      RD[:, tt, :].unsqueeze(2).broadcast_to([P, NH, HD]), ALU.mult).then_inc(evac["v"], 1)

            dve.sem_inc(dot_ready, RING)

            FREQ, ANG, TURN = TMP[:, 0:16], TMP[:, 32:64], TMP[:, 64:96]
            POS = RW[:, 2:4]
            dve.memset(MODL[0][:, 3072:6144], 0.0).then_inc(acc_zeroed, 1)
            for k in range(16):
                go(dve.memset(FREQ[:, k:k + 1], 10000.0 ** (-k / 16.0)))
            dve.wait_ge(pos_loaded, 16)
            step(dve.tensor_copy(POS, RW[:, 0:TT].bitcast(I32)))
            for tt in range(TT):
                step(dve.tensor_scalar(ANG[:, tt * 16:(tt + 1) * 16], FREQ, POS[:, tt:tt + 1], None, ALU.mult))
            C1 = 6.28125
            C2 = 0.0019350051879882812
            C3 = 2 * pi - C1 - C2
            for n, (table, turn, quarter) in enumerate(((SIN, 0.0, 0.0), (COS, 0.25, pi / 2))):
                tab = table.rearrange("p t f -> p (t f)")
                step(dve.tensor_scalar(TURN, ANG, 1.0 / (2 * pi), turn, ALU.mult, ALU.add))
                step(dve.tensor_scalar(TURN, TURN, 12582912.0, None, ALU.add))
                step(dve.tensor_scalar(TURN, TURN, 12582912.0, None, ALU.subtract))
                step(dve.scalar_tensor_tensor(tab, TURN, -C1, ANG, ALU.mult, ALU.add))
                step(dve.scalar_tensor_tensor(tab, TURN, -C2, tab, ALU.mult, ALU.add))
                step(dve.scalar_tensor_tensor(tab, TURN, -C3, tab, ALU.mult, ALU.add))
                step(dve.tensor_scalar(tab, tab, quarter, 3.1415925, ALU.add, ALU.min))
                step(dve.tensor_scalar(tab, tab, -3.1415925, None, ALU.max))
                dve.sem_inc(trig_in, 1)

            dve.wait_ge(cond_ready, 1)

            def accumulate(l, first, count):
                if first == 0:
                    dve.wait_ge(bada_loaded, 16 * (l + 1))
                for n in range(first, first + count):
                    c3, kp = divmod(n, 4)
                    name = ("ada", l, c3, kp)
                    loaded(dve, name)
                    w = ring[CH[name][1]].rearrange("p (k n) -> p k n", k=2)
                    acc = MODL[l][:, c3 * 2048:(c3 + 1) * 2048]
                    for k in range(2):
                        step(dve.scalar_tensor_tensor(acc, w[:, k, :], COND[:, 2 * kp + k:2 * kp + k + 1], acc,
                                                      ALU.mult, ALU.add))
                    dve.sem_inc(chunk_used["v"], 1)
                if n == 11:
                    dve.sem_inc(acc_ready, 1)

            def accumulate_next(l, first, count):
                if l + 1 < DEPTH:
                    accumulate(l + 1, first, count)

            def gain_rows(which):
                for n in which:
                    arrived(dve, ("ada", 0, n))
                    gain = NGAIN[:, n // 2 == 4, (n % 2) * 512:(n % 2 + 1) * 512]
                    dve.scalar_tensor_tensor(MODL[0][:, n * 512:(n + 1) * 512], bank(("ada", 0, n)), 1.0, gain,
                                             ALU.add, ALU.mult).then_inc(evac["v"], 1)

            def modulated(l, i):
                for tt in range(TT):
                    step(dve.scalar_tensor_tensor(HR[:, tt], X[:, tt], RS[:, tt:tt + 1], mrow(l, i + 1), ALU.mult, ALU.mult))
                    dve.tensor_tensor(HR[:, tt], HR[:, tt], mrow(l, i), ALU.add).then_inc(rows_ready, 2)

            accumulate(0, 0, 12)
            dve.wait_ge(gains_loaded, 32)
            dve.wait_ge(x_loaded, 16)
            for l in range(DEPTH):
                root(TT)
                if l == 0:
                    gain_rows((2, 3))
                    taken(dve, ("ada", 0, 1))
                    taken(dve, ("ada", 0, 3))
                else:
                    taken(dve, ("ada", l, 11))
                    dve.wait_ge(gains_loaded, 16 * 2 * (l + 1))
                    for n, i in enumerate((1, 4)):
                        step(dve.scalar_tensor_tensor(mrow(l, i), mrow(l, i), 1.0, HTF[:, n * D:(n + 1) * D], ALU.add, ALU.mult))
                modulated(l, 0)
                if l == 0:
                    gain_rows((8, 9))
                    taken(dve, ("ada", 0, 9))
                    taken(dve, ("ada", 0, 11))
                accumulate_next(l, 0, 4)
                dve.wait_ge(params_loaded, 16 * 7 * (l + 1))
                taken(dve, ("in", l, 2, 1))
                qk = PROJ[:, :, POOL:POOL + 640]
                sq = QSQ.rearrange("p (t n) -> p t n", t=TT)
                step(dve.tensor_tensor(sq, qk, qk, ALU.mult))
                step(dve.tensor_reduce(SSQ[:, 0:20], QSQ.rearrange("p (h d) -> p h d", d=HD), AX, ALU.add))
                root(20)
                heads = qk.rearrange("p t (h d) -> p t h d", d=HD)
                rs = RS[:, 0:20].rearrange("p (t h) -> p t h", t=TT)
                step(dve.tensor_tensor(heads, heads, rs.unsqueeze(3).broadcast_to([P, TT, 10, HD]), ALU.mult))
                for tt in range(TT):
                    q = heads[:, tt, 0:NH]
                    ins = dve.tensor_tensor(q, q, QKG[:, 0:HD].unsqueeze(1).broadcast_to([P, NH, HD]), ALU.mult)
                    if tt == 0:
                        step(ins)
                    else:
                        ins.then_inc(qk_ready, 1)
                for u in range(2):
                    for tt in range(TT):
                        ins = dve.tensor_tensor(KD[:, tt, :, u, :], heads[:, tt, NH:NH + NKV],
                                                QKG[:, HD:2 * HD].unsqueeze(1).broadcast_to([P, NKV, HD]), ALU.mult)
                        if tt == 0:
                            step(ins)
                        else:
                            ins.then_inc(qk_ready, 1)
                for tt in range(TT):
                    arrived(dve, ("mix", l, tt))
                    dve.tensor_tensor(HR[:, tt, 0:512], bank(("mix", l, tt)), PSC, ALU.mult).then_inc(evac["v"], 1)
                attention_rows("a", l, S_A, HD ** -0.5,
                               lambda tt, heads, per, nk: BIAS[:, heads, 2 * P - nk:2 * P], True)
                attention_values("a", l, 512, 1)
                taken(dve, ("apv", l, 1))
                for tt in range(TT):
                    for half in range(2):
                        y = HR[:, tt, half * 512:(half + 1) * 512]
                        n = 2 * tt + half
                        step(dve.tensor_tensor_reduce(JUNK[:, 0:512], y, y, 1.0, 0.0, ALU.mult, ALU.add, SSQ[:, n:n + 1]))
                root(4)
                for tt in range(TT):
                    for half in range(2):
                        y = HR[:, tt, half * 512:(half + 1) * 512]
                        n = 2 * tt + half
                        dve.scalar_tensor_tensor(y, y, RS[:, n:n + 1], MIXG[:, half * 512:(half + 1) * 512],
                                                 ALU.mult, ALU.mult).then_inc(rows_ready, 1)
                accumulate_next(l, 4, 2)
                for c in range(2):
                    for tt in range(TT):
                        name = ("out", l, c, tt)
                        arrived(dve, name)
                        part = slice(c * 512, (c + 1) * 512)
                        dve.tensor_tensor(TMP, bank(name), mrow(l, 2)[:, part], ALU.mult).then_inc(evac["v"], 1)
                        taken(dve, name)
                        step(dve.tensor_tensor(X[:, tt, part], X[:, tt, part], TMP, ALU.add))
                        if 2 * c + tt < 3:
                            accumulate_next(l, 6 + 2 * c + tt, 1)
                root(TT)
                modulated(l, 3)
                accumulate_next(l, 9, 3)

                def best16(n, values, vals, idxs):
                    for a in range(n):
                        go(dve.max(vals[:, a, 0:8], values[:, a, :]))
                    sync()
                    for a in range(n):
                        go(dve.max_index(idxs[:, a, 0:8], vals[:, a, 0:8], values[:, a, :]))
                    sync()
                    for a in range(n):
                        go(dve.match_replace(values[:, a, :], vals[:, a, 0:8], values[:, a, :], LOWEST))
                    sync()
                    for a in range(n):
                        go(dve.max(vals[:, a, 8:16], values[:, a, :]))
                    sync()
                    for a in range(n):
                        go(dve.max_index(idxs[:, a, 8:16], vals[:, a, 8:16], values[:, a, :]))
                    sync()

                v2 = V16.rearrange("p (h q) k -> p h q k", q=2)
                f2 = F16.rearrange("p (h q) k -> p h q k", q=2)
                wide = [P, HQ, TOPK, TOPK]

                def best_of_halves(tt, c):
                    taken(dve, ("s", l, tt, c))
                    best16(2 * HQ, SS[tt][:, 2 * HQ * c:2 * HQ * (c + 1)], V16, I16)
                    step(dve.tensor_copy(F16, I16))

                def best_of_sums(tt, c):
                    step(dve.tensor_tensor(CAND.rearrange("p h (i j) -> p h i j", i=TOPK),
                                           v2[:, :, 0, :].unsqueeze(3).broadcast_to(wide),
                                           v2[:, :, 1, :].unsqueeze(2).broadcast_to(wide), ALU.add))
                    best16(HQ, CAND, BV, BI)

                def expert_numbers(tt, c):
                    for half, (op, by, dst) in enumerate(((ALU.logical_shift_right, 4, E1), (ALU.bitwise_and, 15, E2))):
                        step(dve.tensor_scalar(BU, BI, by, None, op))
                        step(dve.tensor_copy(BF, BU))
                        flat = OH.rearrange("p h k c -> p (h k) c")
                        places = BF.rearrange("p h k -> p (h k)")
                        step(dve.tensor_tensor(flat, places.unsqueeze(2).broadcast_to([P, HQ * TOPK, TOPK]),
                                               IOTA.unsqueeze(1).broadcast_to([P, HQ * TOPK, TOPK]), ALU.is_equal))
                        step(dve.tensor_tensor(OH, OH, f2[:, :, half, :].unsqueeze(2).broadcast_to(wide), ALU.mult))
                        step(dve.tensor_reduce(dst, OH, AX, ALU.add))
                    step(dve.scalar_tensor_tensor(E1, E1, float(NKEY), E2, ALU.mult, ALU.add))
                    part = slice(c * HQ * TOPK, (c + 1) * HQ * TOPK)
                    dve.tensor_scalar(IDX[:, tt, part].rearrange("p (h k) -> p h k", h=HQ), E1, float(l * NEXP), None,
                                      ALU.add).then_inc(idx_ready, 1)
                    step(dve.tensor_tensor(GATE[:, tt, part].rearrange("p (h k) -> p h k", h=HQ), BV,
                                           BV[:, :, 0:1].broadcast_to([P, HQ, TOPK]), ALU.subtract))
                    dve.wait_ge(idx_ready, NQ * (l * TT + tt) + c + 1)

                routing = (best_of_halves, best_of_sums, expert_numbers)
                for c in range(NQ):
                    for part in routing:
                        part(0, c)
                for tt in range(TT):
                    base = (l * TT + tt) * SLOTS

                    def dot(i, s):
                        dve.wait_ge(u_loaded[s], i * 16 + (base // RING + 1) * 16)
                        dve.wait_ge(dot_ready, i * RING + (base + s + RING))
                        dve.tensor_tensor_reduce(JUNK, GU[:, s, :], HR[:, tt], 1.0, 0.0, ALU.mult, ALU.add,
                                                 DOT[:, s:s + 1]).then_inc(dot_ready, 1)

                    def diag(i, s):
                        dve.wait_ge(gelu_ready, i * RING + (base + s + 1))
                        dve.wait_ge(expert_added, i * RING + (base + s + 1))
                        dve.tensor_scalar(DIAG[:, s, :], IDENT, ACTV[:, s:s + 1], GATE[:, tt, bass.ds(i * RING + s, 1)],
                                          ALU.mult, ALU.mult).then_inc(diag_ready, 1)

                    dve.sem_inc(gexp_in, 1)
                    dve.wait_ge(gexp_out, l * TT + tt + 1)
                    gate = GATE[:, tt].rearrange("p (h k) -> p h k", h=PH)
                    step(dve.tensor_reduce(RS[:, 0:PH], gate, AX, ALU.add))
                    step(dve.reciprocal(RT[:, 0:PH], RS[:, 0:PH]))
                    step(dve.tensor_tensor(gate, gate, RT[:, 0:PH].unsqueeze(2).broadcast_to([P, PH, TOPK]), ALU.mult))

                    rounds = NQ * len(routing) if tt == 0 else 1
                    for i in range(rounds):
                        if tt == 0:
                            routing[i % len(routing)](1, i // len(routing))
                        dot(i, 0)
                        for s in range(1, RING):
                            dot(i, s)
                            diag(i, s - 1)
                        if i < rounds - 1:
                            diag(i, RING - 1)
                    with dve.Fori(rounds, SLOTS // RING) as i:
                        dot(i, 0)
                        diag(i - 1, RING - 1)
                        for s in range(1, RING):
                            dot(i, s)
                            diag(i, s - 1)
                    diag(SLOTS // RING - 1, RING - 1)
                    dve.wait_ge(expert_added, base + SLOTS + RING)
                    for half in range(2):
                        part = slice(half * 512, (half + 1) * 512)
                        dve.tensor_tensor(TMP, PO[:, half, :], mrow(l, 5)[:, part], ALU.mult).then_inc(sums_read, 1)
                        dve.wait_ge(sums_read, 2 * (l * TT + tt) + half + 1)
                        step(dve.tensor_tensor(X[:, tt, part], X[:, tt, part], TMP, ALU.add))
                dve.sem_inc(layer_done, 1)

            def gained(gain, inc):
                for tt in range(TT):
                    dve.scalar_tensor_tensor(HR[:, tt], X[:, tt], RS[:, tt:tt + 1], gain, ALU.mult,
                                             ALU.mult).then_inc(inc, 2 if inc is rows_ready else 1)

            pb = 16 * 7 * DEPTH + 16
            for l in range(DEPTH):
                root(TT)
                dve.wait_ge(params_loaded, pb + 16 * 11 * (l + 1))
                gained(AN, rows_ready)
                for tt in range(TT):
                    arrived(dve, ("rest", l, tt))
                    dve.tensor_copy(R[:, tt, :], bank(("rest", l, tt))[:, 0:REST]).then_inc(evac["v"], 1)
                taken(dve, ("rest", l, 1))
                z, az = RTMP[:, 0:16].rearrange("p (t h) -> p t h", t=TT), RTMP[:, 16:32].rearrange("p (t h) -> p t h", t=TT)
                step(dve.tensor_tensor(z, R[:, :, 0:NH], BFB.unsqueeze(1).broadcast_to([P, TT, NH]), ALU.add))
                step(dve.tensor_scalar(az, z, -1.0, None, ALU.mult))
                step(dve.tensor_tensor(az, az, z, ALU.max))
                dve.sem_inc(logsig_in, 1)
                for tt in range(TT):
                    for n, (a, b) in enumerate(((8, 8 + QL), (8 + QL, 8 + QL + KVL))):
                        y = R[:, tt, a:b]
                        step(dve.tensor_tensor_reduce(JUNK[:, 0:b - a], y, y, 1.0, 0.0, ALU.mult, ALU.add,
                                                      SSQ[:, 2 * n + tt:2 * n + tt + 1]))
                dve.wait_ge(logsig_out, l + 1)
                step(dve.tensor_scalar(z, z, 0.0, None, ALU.min))
                step(dve.tensor_tensor(z, z, az, ALU.subtract))
                step(dve.tensor_scalar(z, z, -(HD ** 0.5), None, ALU.mult))
                dve.tensor_copy(LFB, z.unsqueeze(3).broadcast_to([P, TT, NH, P])).then_inc(decay_ready, 1)
                root(4)
                for tt in range(TT):
                    for n, (a, b, gain) in enumerate(((8, 8 + QL, QG), (8 + QL, 8 + QL + KVL, KG))):
                        y = R[:, tt, a:b]
                        dve.scalar_tensor_tensor(y, y, RS[:, 2 * n + tt:2 * n + tt + 1], gain, ALU.mult,
                                                 ALU.mult).then_inc(cn_ready, 1)
                if l == 0:
                    dve.wait_ge(trig_out, 2)
                    dve.wait_ge(consts_ready, 2)
                kr = R[:, :, 8 + QL + KVL:REST]
                kt = [RTMP[:, 300 + 32 * i:332 + 32 * i].rearrange("p (t f) -> p t f", t=TT) for i in range(4)]
                go(dve.tensor_tensor(kt[0], kr[:, :, 0:16], COS, ALU.mult))
                go(dve.tensor_tensor(kt[1], kr[:, :, 16:32], SIN, ALU.mult))
                go(dve.tensor_tensor(kt[2], kr[:, :, 16:32], COS, ALU.mult))
                step(dve.tensor_tensor(kt[3], kr[:, :, 0:16], SIN, ALU.mult))
                go(dve.tensor_tensor(kt[0], kt[0], kt[1], ALU.subtract))
                step(dve.tensor_tensor(kt[2], kt[2], kt[3], ALU.add))
                for tt in range(TT):
                    for n, src in ((0, kt[0]), (1, kt[2])):
                        go(dve.tensor_copy(KM[:, tt, :, HD + 16 * n:HD + 16 * n + 16],
                                           src[:, tt].unsqueeze(1).broadcast_to([P, NH, 16])))
                taken(dve, ("ukv", l, 1, 1))
                for tt in range(TT):
                    step(dve.tensor_copy(KM[:, tt, :, 0:HD], KV[:, tt, :, 0:HD]))
                dve.sem_inc(mla_ready, 1)
                for tt in range(TT):
                    x1, x2 = QM[:, tt, :, HD:HD + 16], QM[:, tt, :, HD + 16:DK]
                    cs, sn = (t[:, tt].unsqueeze(1).broadcast_to([P, NH, 16]) for t in (COS, SIN))
                    qt = [RTMP[:, 430 + 128 * i:558 + 128 * i].rearrange("p (h f) -> p h f", h=NH) for i in range(4)]
                    go(dve.tensor_tensor(qt[0], x1, cs, ALU.mult))
                    go(dve.tensor_tensor(qt[1], x2, sn, ALU.mult))
                    go(dve.tensor_tensor(qt[2], x2, cs, ALU.mult))
                    step(dve.tensor_tensor(qt[3], x1, sn, ALU.mult))
                    go(dve.tensor_tensor(x1, qt[0], qt[1], ALU.subtract))
                    step(dve.tensor_tensor(x2, qt[2], qt[3], ALU.add))
                dve.sem_inc(mla_ready, 1)

                def causal(tt, heads, per, nk):
                    return CMASK[:, 2 * P - nk:2 * P].unsqueeze(1).broadcast_to([P, per, nk])

                attention_rows("f", l, S_B, HD ** -0.5, causal, False)
                attention_values("f", l, 0, 0)
                attention_rows("m", l, S_B, DK ** -0.5, causal, False)
                attention_values("m", l, 512, 0)
                taken(dve, ("mpv", l, 1))
                sq = SQB.rearrange("p (t n) -> p t n", t=TT)
                step(dve.tensor_tensor(sq, HR, HR, ALU.mult))
                step(dve.tensor_reduce(SSQ[:, 0:32], SQB.rearrange("p (h d) -> p h d", d=HD), AX, ALU.add))
                root(32)
                for tt in range(TT):
                    y = HR[:, tt].rearrange("p (h d) -> p h d", d=HD)
                    step(dve.tensor_tensor(y, y, RS[:, 16 * tt:16 * tt + 16].unsqueeze(2).broadcast_to([P, 16, HD]), ALU.mult))
                    dve.tensor_tensor(HR[:, tt], HR[:, tt], ON, ALU.mult).then_inc(rows_ready, 2)
                for c in range(2):
                    for tt in range(TT):
                        name = ("bout", l, c, tt)
                        arrived(dve, name)
                        part = slice(c * 512, (c + 1) * 512)
                        dve.tensor_tensor(X[:, tt, part], X[:, tt, part], bank(name), ALU.add).then_inc(evac["v"], 1)
                taken(dve, ("bout", l, 1, 1))
                root(TT)
                for tt in range(TT):
                    dve.scalar_tensor_tensor(HR[:, tt].rearrange("p (k a) -> p k a", k=KT),
                                             X[:, tt].rearrange("p (a k) -> p k a", k=KT), RS[:, tt:tt + 1],
                                             FN.rearrange("p (a k) -> p k a", k=KT), ALU.mult,
                                             ALU.mult).then_inc(rows_ready, 2)

                GL = RTMP[:, 0:80].rearrange("p (t n) -> p t n", t=TT)
                for tt in range(TT):
                    arrived(dve, ("route", l, tt))
                    dve.tensor_copy(GL[:, tt], bank(("route", l, tt))[:, 0:NG + NE]).then_inc(evac["v"], 1)
                taken(dve, ("route", l, 1))
                gexp = RTMP[:, 100:116].rearrange("p (t g) -> p t g", t=TT)
                gtop = RTMP[:, 120:136].rearrange("p (t g) -> p t g", t=TT)
                gidx = RTMP[:, 140:156].rearrange("p (t g) -> p t g", t=TT).bitcast(U32)
                gone = RTMP[:, 160:176].rearrange("p (t g) -> p t g", t=TT)
                gfl = RTMP[:, 180:196].rearrange("p (t g) -> p t g", t=TT)
                d2 = RTMP[:, 200:202].rearrange("p (t g) -> p t g", t=TT)
                ig = RTMP[:, 210:226].rearrange("p (t g) -> p t g", t=TT)
                itop = RTMP[:, 230:246].rearrange("p (t g) -> p t g", t=TT)
                iidx = RTMP[:, 250:266].rearrange("p (t g) -> p t g", t=TT).bitcast(U32)
                ifl = RTMP[:, 270:286].rearrange("p (t g) -> p t g", t=TT)
                prod = RTMP[:, 300:364].rearrange("p (t g e) -> p t g e", t=TT, g=NG)
                sm = RTMP[:, 400:440].rearrange("p (n t g) -> p n t g", n=20, t=TT)
                w4 = RTMP[:, 450:466].rearrange("p (n t e) -> p n t e", n=2, t=TT)
                iota8 = RW[:, 48:56]
                for tt in range(TT):
                    go(dve.max(gtop[:, tt], GL[:, tt, 0:NG]))
                sync()
                for tt in range(TT):
                    go(dve.max_index(gidx[:, tt], gtop[:, tt], GL[:, tt, 0:NG]))
                step(dve.tensor_tensor(gexp, GL[:, :, 0:NG], gtop[:, :, 0:1].broadcast_to([P, TT, NG]), ALU.subtract))
                dve.sem_inc(router_in, 1)
                step(dve.tensor_copy(gfl, gidx))
                step(dve.tensor_tensor(gone, gfl[:, :, 0:1].broadcast_to([P, TT, NG]),
                                       iota8.unsqueeze(1).broadcast_to([P, TT, NG]), ALU.is_equal))
                logits = GL[:, :, NG:NG + NE].rearrange("p t (g e) -> p t g e", g=NG)
                step(dve.tensor_tensor(prod, logits, gone.unsqueeze(3).broadcast_to([P, TT, NG, EPG]), ALU.mult))
                step(dve.memset(ig, LOWEST))
                for tt in range(TT):
                    step(dve.tensor_reduce(ig[:, tt, 0:EPG], prod[:, tt].rearrange("p g e -> p e g"), AX, ALU.add))
                for tt in range(TT):
                    go(dve.max(itop[:, tt], ig[:, tt]))
                sync()
                for tt in range(TT):
                    go(dve.max_index(iidx[:, tt], itop[:, tt], ig[:, tt]))
                step(dve.tensor_tensor(d2, itop[:, :, 1:2], itop[:, :, 0:1], ALU.subtract))
                dve.sem_inc(router_in, 1)
                step(dve.tensor_copy(ifl, iidx))
                dve.wait_ge(router_out, 2 * l + 2)
                step(dve.tensor_reduce(sm[:, 0], gexp, AX, ALU.add))
                step(dve.reciprocal(sm[:, 1], sm[:, 0]))
                step(dve.tensor_scalar(sm[:, 2], d2, 1.0, None, ALU.add))
                step(dve.reciprocal(sm[:, 3], sm[:, 2]))
                step(dve.tensor_tensor(GK[:, :, 0:1], sm[:, 3], sm[:, 1], ALU.mult))
                step(dve.tensor_tensor(GK[:, :, 1:2], GK[:, :, 0:1], d2, ALU.mult))
                for k in range(2):
                    step(dve.tensor_tensor(w4[:, k], ifl[:, :, k:k + 1].broadcast_to([P, TT, EPG]),
                                           iota8[:, 0:EPG].unsqueeze(1).broadcast_to([P, TT, EPG]), ALU.is_equal))
                    for tt in range(TT):
                        step(dve.tensor_tensor(ONEHOT[:, k, tt].rearrange("p (g e) -> p g e", g=NG),
                                               gone[:, tt].unsqueeze(2).broadcast_to([P, NG, EPG]),
                                               w4[:, k, tt].unsqueeze(1).broadcast_to([P, NG, EPG]), ALU.mult))
                dve.tensor_tensor(PICKS, ONEHOT[:, 0], ONEHOT[:, 1], ALU.add).then_inc(onehot_ready, 1)

                rk = RTMP[:, 700:796].rearrange("p (n e) -> p n e", e=NE)
                arrived(dve, ("rank", l))
                dve.tensor_copy(rk, bank(("rank", l))[:, 0:3 * NE].rearrange("p (n e) -> p n e", e=NE)).then_inc(evac["v"], 1)
                taken(dve, ("rank", l))
                nx, xend, xb = (RTMP[:, 800 + 32 * n:832 + 32 * n] for n in range(3))
                rank, count = rk[:, 0:TT], rk[:, TT]
                q = RTMP[:, 300:364].rearrange("p (t e) -> p t e", t=TT)
                blk = RTMP[:, 900:964].rearrange("p (t e) -> p t e", t=TT)
                more = RTMP[:, 100:164].rearrange("p (t e) -> p t e", t=TT)
                step(dve.tensor_scalar(rank, rank, -1.0, None, ALU.add))
                step(dve.tensor_scalar(nx, count, BT + 0.5, None, ALU.is_gt))
                step(dve.tensor_scalar(q, rank, BT - 0.5, None, ALU.is_gt))
                for n in range(2, T // BT):
                    step(dve.scalar_tensor_tensor(nx, count, n * BT + 0.5, nx, ALU.is_gt, ALU.add))
                    step(dve.scalar_tensor_tensor(q, rank, n * BT - 0.5, q, ALU.is_gt, ALU.add))
                step(dve.tensor_tensor_scan(xend, nx, CMASK[:, 0:NE], 0.0, ALU.add, ALU.add))
                dve.tensor_copy(PLAN[:, NX:NX + 1], xend[:, NE - 1:NE]).then_inc(plan_step, 1)
                cmpx = mod[:, 9752:9752 + NX * NE].rearrange("p (x e) -> p x e", e=NE)
                step(dve.tensor_tensor(cmpx, xend.unsqueeze(1).broadcast_to([P, NX, NE]),
                                       iota8.unsqueeze(2).broadcast_to([P, NX, NE]), ALU.is_le))
                step(dve.tensor_reduce(RT[:, 0:NX], cmpx, AX, ALU.add))
                dve.wait_ge(plan_step, l + 1)
                dve.tensor_scalar(PLAN[:, 0:NX], RT[:, 0:NX], float(NE - 1), None, ALU.min).then_inc(plan_ready, 1)
                step(dve.tensor_tensor(xb, xend, nx, ALU.subtract))
                step(dve.tensor_tensor(xb, xb, ENUM, ALU.subtract))
                step(dve.tensor_scalar(xb, xb, float(NB - 1), None, ALU.add))
                step(dve.tensor_scalar(more, q, 1.0, None, ALU.min))
                step(dve.tensor_tensor(blk, q, xb.unsqueeze(1).broadcast_to([P, TT, NE]), ALU.add))
                step(dve.tensor_tensor(blk, blk, more, ALU.mult))
                step(dve.tensor_tensor(blk, blk, ENUM.unsqueeze(1).broadcast_to([P, TT, NE]), ALU.add))
                step(dve.tensor_tensor(blk, blk, q, ALU.subtract))
                step(dve.scalar_tensor_tensor(blk, blk, float(BT), rank, ALU.mult, ALU.add))
                for k in range(2):
                    step(dve.tensor_tensor(q, ONEHOT[:, k], blk, ALU.mult))
                    step(dve.tensor_reduce(DREL[:, :, k], q, AX, ALU.add))
                step(dve.tensor_copy(DESTI, DREL.rearrange("p t k -> p (t k)")))
                dve.sem_inc(plan_ready, 1)

                def y_rows(i, s):
                    b = i * EXP_RING + (l * NBX + s)
                    dve.wait_ge(down_done, b + 1)
                    if not isinstance(i, int):
                        dve.wait_ge(y_stored[s % 2], i * 64 + 32 * (l * NB // 2 + s // 2))
                    elif EXP_RING * i + s - 2 < NB:
                        if l or i or s > 1:
                            dve.wait_ge(y_stored[s % 2], 32 * (l * NB // 2 + i * 2 + s // 2))
                    else:
                        dve.wait_ge(extra_stored[l][s % 2], 32 * ((EXP_RING * i + s - NB) // 2))
                    dve.tensor_copy(YO[:, s % 2], PS[:, 4 + s % 2, :]).then_inc(y_out, 1)

                def hidden(i, s):
                    b = i * EXP_RING + (l * NBX + s)
                    dve.wait_ge(silu_done, b + 1)
                    ups = PS[:, 6 + s % 2, 0:2 * P].rearrange("p (j t) -> p j t", j=2)[:, :, BT:P]
                    dve.tensor_tensor(HH[:, s % 2], SG[:, s % 2], ups, ALU.mult).then_inc(hidden_ready, 1)

                def body(i, s, n):
                    b = i * EXP_RING + (l * NBX + s)
                    if s % 2 == 0:
                        if l or s or not isinstance(i, int) or i:
                            dve.wait_ge(sel_step, b)
                        dve.tensor_tensor(EQ, SLOT.unsqueeze(1).unsqueeze(1).broadcast_to([P, TT, 2, 2 * BT]),
                                          DREL.unsqueeze(3).broadcast_to([P, TT, 2, 2 * BT]), ALU.is_equal).then_inc(sel_step, 1)
                        dve.wait_ge(sel_step, b + 1)
                        dve.tensor_tensor(SEL[:, s // 2], EQ[:, :, 0], EQ[:, :, 1], ALU.add).then_inc(sel_ready, 2)
                        dve.tensor_scalar(DREL, DREL, float(-2 * BT), None, ALU.add).then_inc(sel_step, 1)
                    if n > 1:
                        y_rows(*before(i, s, 2))
                    if n:
                        hidden(*before(i, s, 1))
                    dve.wait_ge(gate_up_done, b + 1)
                    dve.tensor_copy(GUO[:, s % 2], PS[:, 2 + s % 2, 0:DE]).then_inc(gate_up_out, 1)

                def flush(i, s):
                    y_rows(*before(i, s, 1))
                    hidden(i, s)
                    y_rows(i, s)

                blocks(dve, l, body, flush, [(sel_step, 1), (sel_ready, 1), (gate_up_out, 1), (hidden_ready, 1), (y_out, 1)])
                dve.wait_ge(y_gathered, 16 * 2 * TT * (l + 1))
                for tt in range(TT):
                    for k in range(2):
                        step(dve.scalar_tensor_tensor(X[:, tt], YG[:, 2 * tt + k], GK[:, tt, k:k + 1], X[:, tt], ALU.mult, ALU.add))
                dve.sem_inc(layer_done, 1)
            root(TT)
            gained(FINAL, out_ready)


_INS = ["x", "c", "w_ada", "b_ada", "norm1_g", "norm2_g", "w_in", "pool_w", "pool_scale", "q_norm_g", "k_norm_g",
        "attn_sinks", "mix_norm_g", "w_out", "peer_wq", "peer_subkeys", "peer_u", "peer_v", "positions_2",
        "attn_norm_2", "w_in_2", "b_f_2", "q_norm_2", "w_uq_2", "kv_norm_2", "w_ukv_2", "fox_out_norm_2",
        "mla_out_norm_2", "w_o_2", "ffn_norm_2", "w_group_2", "w_router_2", "w_gate_2", "w_up_2", "w_down_2",
        "final_norm_2"]
_OUTS = [((1, 256, 1024), "float32")]


def kernel(**inputs):
    import numpy as _np
    import concourse.bacc as _bacc
    from concourse import mybir as _mybir
    from concourse.bass_utils import run_bass_kernel_spmd as _run

    nc = _bacc.Bacc("TRN2", target_bir_lowering=False, num_devices=1)
    arrays, args = {}, []
    for name in _INS:
        a = _np.ascontiguousarray(inputs[name])
        arrays[f"in_{name}_dram"] = a
        args.append(nc.dram_tensor(f"in_{name}_dram", a.shape, _mybir.dt.from_np(a.dtype), kind="ExternalInput").ap())
    for i, (shape, dtype) in enumerate(_OUTS):
        dt = _mybir.dt.from_np(_np.dtype(dtype))
        args.append(nc.dram_tensor(f"out_{i}_dram", shape, dt, kind="ExternalOutput").ap())
    build(nc, *args)
    r = _run(nc, [arrays], core_ids=[0])
    got = tuple(r.results[0][f"out_{i}_dram"] for i in range(len(_OUTS)))
    return got[0]
```
